# Optimizing a Trainium2 kernel written in Bass

```python
import math
import jax
import jax.numpy as jnp
from jax import lax
import numpy as np
import jax, jax.numpy as jnp

D_MODEL = 1024
BATCH = 1
SEQ = 256
DEPTH = 1

CHUNK = 64
HEAD_DIM = 64
N_BRANCH = 4
BRANCH_WIDTH = D_MODEL // N_BRANCH
CONV_WIDTH = 3
SC_WIDTH = BRANCH_WIDTH
SB_HEADS = BRANCH_WIDTH // HEAD_DIM
SB_WIDTH = SB_HEADS * HEAD_DIM
SB_BLOCK = 128
RW_HEADS = BRANCH_WIDTH // HEAD_DIM
RW_WIDTH = RW_HEADS * HEAD_DIM
RW_DECAY_LORA = 64
RW_A_LORA = 64
RW_GATE_LORA = 128
RW_GN_EPS = 64e-5
RW_DECAY_SCALE = math.exp(-0.5)
SG_GROUPS = 4
SG_WIDTH = BRANCH_WIDTH
SG_GROUP_WIDTH = SG_WIDTH // SG_GROUPS
SG_CHUNK = 128
D_FF = ((8 * D_MODEL // 3 + 127) // 128) * 128
RMS_EPS = 1e-6
LN_EPS = 1e-5

SC_OFF = 0
SB_OFF = SC_OFF + 3 * SC_WIDTH
RW_OFF = SB_OFF + 3 * SB_WIDTH
RW_COLS = 3 * RW_WIDTH + RW_DECAY_LORA + RW_A_LORA + RW_GATE_LORA
SG_OFF = RW_OFF + RW_COLS
GATE_OFF = SG_OFF + 2 * SG_WIDTH
IN_COLS = GATE_OFF + N_BRANCH * D_MODEL


def rms_norm(x, g):
    xf = x.astype(jnp.float32)
    y = xf * lax.rsqrt(jnp.mean(xf * xf, axis=-1, keepdims=True) + RMS_EPS)
    return (y * g.astype(jnp.float32)).astype(x.dtype)

def layer_norm(x, g, b):
    xf = x.astype(jnp.float32)
    mu = jnp.mean(xf, axis=-1, keepdims=True)
    var = jnp.mean(jnp.square(xf - mu), axis=-1, keepdims=True)
    y = (xf - mu) * lax.rsqrt(var + LN_EPS) * g.astype(jnp.float32) + b.astype(jnp.float32)
    return y.astype(x.dtype)

def causal_dwconv(x, w):
    k = w.shape[0]
    t = x.shape[1]
    xp = jnp.pad(x, ((0, 0), (k - 1, 0), (0, 0)))
    out = xp[:, 0:t] * w[0]
    for i in range(1, k):
        out = out + xp[:, i:i + t] * w[i]
    return out

def token_shift(x):
    return jnp.pad(x, ((0, 0), (1, 0), (0, 0)))[:, :-1]

def short_conv_mixer(z, conv_w):
    b_gate, c_gate, xin = jnp.split(z, 3, axis=-1)
    return b_gate * causal_dwconv(c_gate * xin, conv_w)

def stick_breaking_attention(q, k, v):
    bsz, t, h, dh = q.shape
    nb = t // SB_BLOCK
    scale = 1.0 / math.sqrt(dh)
    qb = q.reshape(bsz, nb, SB_BLOCK, h, dh).transpose(1, 0, 3, 2, 4)
    kh = k.transpose(0, 2, 1, 3)
    vh = v.transpose(0, 2, 1, 3)
    kpos = jnp.arange(t)

    def block(args):
        qi, bi = args
        z = jnp.einsum('bhqd,bhkd->bhqk', qi, kh).astype(jnp.float32) * scale
        qpos = bi * SB_BLOCK + jnp.arange(SB_BLOCK)
        mask = kpos[None, :] < qpos[:, None]
        log_beta = jax.nn.log_sigmoid(z)
        log_keep = jnp.where(mask, log_beta - z, 0.0)
        suffix = lax.cumsum(log_keep, axis=3, reverse=True) - log_keep
        attn = jnp.where(mask, jnp.exp(log_beta + suffix), 0.0)
        return jnp.einsum('bhqk,bhkd->bhqd', attn.astype(vh.dtype), vh)

    out = lax.map(block, (qb, jnp.arange(nb)))
    return out.transpose(1, 0, 3, 2, 4).reshape(bsz, t, h * dh)

def rwkv7_scan(r, w, k, v, a_vec, b_vec):
    bsz, t, h, n = r.shape

    def step(s, inp):
        r_t, w_t, k_t, v_t, a_t, b_t = inp
        sa = jnp.einsum('bhvk,bhk->bhv', s, a_t)
        s = s * w_t[:, :, None, :] + sa[..., None] * b_t[:, :, None, :] + v_t[..., None] * k_t[:, :, None, :]
        return s, jnp.einsum('bhvk,bhk->bhv', s, r_t)

    xs = tuple(u.astype(jnp.float32).transpose(1, 0, 2, 3) for u in (r, w, k, v, a_vec, b_vec))
    s0 = jnp.zeros((bsz, h, n, n), jnp.float32)
    _, y = lax.scan(step, s0, xs)
    return y.transpose(1, 0, 2, 3)

def rwkv7_mixer(z, mu, w0, w2, a0, a2, g2, k_k, k_a, r_k, gn_g, gn_b):
    bsz, t, _ = z.shape
    z = z + (token_shift(z) - z) * mu
    c0, c1, c2 = RW_WIDTH, 2 * RW_WIDTH, 3 * RW_WIDTH
    c3, c4 = c2 + RW_DECAY_LORA, c2 + RW_DECAY_LORA + RW_A_LORA
    r, k, v = z[..., :c0], z[..., c0:c1], z[..., c1:c2]
    xw, xa, xg = z[..., c2:c3], z[..., c3:c4], z[..., c4:]
    decay = jnp.exp(-RW_DECAY_SCALE * jax.nn.sigmoid((w0 + jnp.tanh(xw) @ w2).astype(jnp.float32)))
    a = jax.nn.sigmoid(a0 + xa @ a2)
    g = jax.nn.sigmoid(xg) @ g2
    hs = (bsz, t, RW_HEADS, HEAD_DIM)
    kk = (k * k_k).reshape(hs).astype(jnp.float32)
    kk = kk / jnp.maximum(jnp.sqrt(jnp.sum(kk * kk, axis=-1, keepdims=True)), 1e-12)
    k = k * (1.0 + (a - 1.0) * k_a)
    rh, kh, vh, ah = r.reshape(hs), k.reshape(hs), v.reshape(hs), a.reshape(hs)
    y = rwkv7_scan(rh, decay.reshape(hs), kh, vh, -kk, kk * ah.astype(jnp.float32))
    mean = jnp.mean(y, axis=-1, keepdims=True)
    var = jnp.mean(jnp.square(y - mean), axis=-1, keepdims=True)
    y = ((y - mean) * lax.rsqrt(var + RW_GN_EPS)).reshape(bsz, t, RW_WIDTH)
    y = y * gn_g.astype(jnp.float32) + gn_b.astype(jnp.float32)
    bonus = jnp.sum((rh * kh * r_k).astype(jnp.float32), axis=-1, keepdims=True) * vh.astype(jnp.float32)
    y = (y + bonus.reshape(bsz, t, RW_WIDTH)).astype(z.dtype)
    return y * g

def spatial_gating(z, ln_g, ln_b, w_s, b_s):
    bsz, t, _ = z.shape
    u, v = jnp.split(jax.nn.gelu(z), 2, axis=-1)
    v = layer_norm(v, ln_g, ln_b)
    vb = v.reshape(bsz, t // SG_CHUNK, SG_CHUNK, SG_GROUPS, SG_GROUP_WIDTH)
    w_causal = jnp.tril(w_s)
    mixed = jnp.einsum('gts,bnsgc->bntgc', w_causal, vb) + b_s.T[:, :, None]
    return u * mixed.reshape(bsz, t, SG_WIDTH)

def hybrid_mixer(h, w_in, gate_b, sc_conv_w, sc_out, sb_out, rw_mu, rw_w0, rw_w2, rw_a0, rw_a2,
                 rw_g2, rw_k_k, rw_k_a, rw_r_k, rw_gn_g, rw_gn_b, rw_out, sg_ln_g, sg_ln_b,
                 sg_w, sg_b, sg_out, w_o):
    bsz, t, _ = h.shape
    proj = h @ w_in
    y_a = short_conv_mixer(proj[..., SC_OFF:SB_OFF], sc_conv_w)
    q, k, v = jnp.split(proj[..., SB_OFF:RW_OFF], 3, axis=-1)
    hs = (bsz, t, SB_HEADS, HEAD_DIM)
    y_b = stick_breaking_attention(q.reshape(hs), k.reshape(hs), v.reshape(hs))
    y_c = rwkv7_mixer(proj[..., RW_OFF:SG_OFF], rw_mu, rw_w0, rw_w2, rw_a0, rw_a2, rw_g2,
                      rw_k_k, rw_k_a, rw_r_k, rw_gn_g, rw_gn_b)
    y_d = spatial_gating(proj[..., SG_OFF:GATE_OFF], sg_ln_g, sg_ln_b, sg_w, sg_b)
    gates = jax.nn.sigmoid((proj[..., GATE_OFF:] + gate_b).astype(jnp.float32)).astype(h.dtype)
    gates = gates.reshape(bsz, t, N_BRANCH, D_MODEL)
    merged = (gates[:, :, 0] * (y_a @ sc_out) + gates[:, :, 1] * (y_b @ sb_out)
              + gates[:, :, 2] * (y_c @ rw_out) + gates[:, :, 3] * (y_d @ sg_out))
    return merged @ w_o

def conv_glu_ffn(h, w_up, conv_w, w_down):
    up = causal_dwconv(h @ w_up, conv_w)
    gate, val = jnp.split(up, 2, axis=-1)
    return (jax.nn.silu(gate) * val) @ w_down

def first_inputs(seed: int = 0) -> dict:
    key = jax.random.key(seed)
    keys = iter(jax.random.split(key, 40))
    f32 = jnp.float32
    L = DEPTH

    def nrm(shape, scale):
        return jax.random.normal(next(keys), shape, f32) * scale

    return {
        "x": nrm((BATCH, SEQ, D_MODEL), 1.0),
        "mix_norm_g": 1.0 + nrm((L, D_MODEL), 0.05),
        "w_in": nrm((L, D_MODEL, IN_COLS), D_MODEL ** -0.5),
        "gate_b": nrm((L, N_BRANCH * D_MODEL), 0.1),
        "sc_conv_w": nrm((L, CONV_WIDTH, SC_WIDTH), CONV_WIDTH ** -0.5),
        "sc_out": nrm((L, SC_WIDTH, D_MODEL), SC_WIDTH ** -0.5),
        "sb_out": nrm((L, SB_WIDTH, D_MODEL), SB_WIDTH ** -0.5),
        "rw_mu": jax.random.uniform(next(keys), (L, RW_COLS), f32),
        "rw_w0": nrm((L, RW_WIDTH), 0.5),
        "rw_w2": nrm((L, RW_DECAY_LORA, RW_WIDTH), 0.1),
        "rw_a0": nrm((L, RW_WIDTH), 0.1),
        "rw_a2": nrm((L, RW_A_LORA, RW_WIDTH), 0.1),
        "rw_g2": nrm((L, RW_GATE_LORA, RW_WIDTH), RW_GATE_LORA ** -0.5),
        "rw_k_k": 0.85 + nrm((L, RW_WIDTH), 0.05),
        "rw_k_a": 1.0 + nrm((L, RW_WIDTH), 0.05),
        "rw_r_k": nrm((L, RW_HEADS, HEAD_DIM), 0.1),
        "rw_gn_g": 1.0 + nrm((L, RW_WIDTH), 0.05),
        "rw_gn_b": nrm((L, RW_WIDTH), 0.01),
        "rw_out": nrm((L, RW_WIDTH, D_MODEL), RW_WIDTH ** -0.5),
        "sg_ln_g": 1.0 + nrm((L, SG_WIDTH), 0.05),
        "sg_ln_b": nrm((L, SG_WIDTH), 0.01),
        "sg_w": nrm((L, SG_GROUPS, SG_CHUNK, SG_CHUNK), 0.05),
        "sg_b": 1.0 + nrm((L, SG_GROUPS, SG_CHUNK), 0.05),
        "sg_out": nrm((L, SG_WIDTH, D_MODEL), SG_WIDTH ** -0.5),
        "w_o": nrm((L, D_MODEL, D_MODEL), 0.5 * D_MODEL ** -0.5),
        "ffn_norm_g": 1.0 + nrm((L, D_MODEL), 0.05),
        "w_up": nrm((L, D_MODEL, 2 * D_FF), D_MODEL ** -0.5),
        "ffn_conv_w": nrm((L, CONV_WIDTH, 2 * D_FF), CONV_WIDTH ** -0.5),
        "w_down": nrm((L, D_FF, D_MODEL), 0.5 * D_FF ** -0.5),
        "final_norm_g": 1.0 + nrm((D_MODEL,), 0.05),
    }

def first_block(x, mix_norm_g, w_in, gate_b, sc_conv_w, sc_out, sb_out, rw_mu, rw_w0, rw_w2,
              rw_a0, rw_a2, rw_g2, rw_k_k, rw_k_a, rw_r_k, rw_gn_g, rw_gn_b, rw_out, sg_ln_g,
              sg_ln_b, sg_w, sg_b, sg_out, w_o, ffn_norm_g, w_up, ffn_conv_w, w_down,
              final_norm_g):
    for l in range(DEPTH):
        h = rms_norm(x, mix_norm_g[l])
        x = x + hybrid_mixer(h, w_in[l], gate_b[l], sc_conv_w[l], sc_out[l], sb_out[l], rw_mu[l],
                             rw_w0[l], rw_w2[l], rw_a0[l], rw_a2[l], rw_g2[l], rw_k_k[l],
                             rw_k_a[l], rw_r_k[l], rw_gn_g[l], rw_gn_b[l], rw_out[l], sg_ln_g[l],
                             sg_ln_b[l], sg_w[l], sg_b[l], sg_out[l], w_o[l])
        h = rms_norm(x, ffn_norm_g[l])
        x = x + conv_glu_ffn(h, w_up[l], ffn_conv_w[l], w_down[l])
    return rms_norm(x, final_norm_g)


N_META = 16
NORM_EPS = 1e-6
SSM_WIDTH = D_MODEL // 2
SSM_GROUP = 16
SSM_GROUPS = SSM_WIDTH // SSM_GROUP
SSM_STATE = 64
ML_WIDTH = D_MODEL
ML_HEADS = 4
ML_HEAD_DIM = ML_WIDTH // ML_HEADS
ML_CHUNK = 64
ML_CONV = 4
ML_QKV_BLOCK = 4
PEER_HEADS = 8
PEER_NKEYS = 128
PEER_EXPERTS = PEER_NKEYS * PEER_NKEYS
PEER_TOPK = 16
PEER_QDIM = 256
PEER_HALF = PEER_QDIM // 2
PEER_TOKEN_BLOCK = 256
IN_COLS_2 = SSM_WIDTH + 2 * ML_WIDTH + 2 * D_MODEL


def rmsnorm(x, g):
    x32 = x.astype(jnp.float32)
    y = x32 * lax.rsqrt(jnp.mean(x32 * x32, axis=-1, keepdims=True) + NORM_EPS)
    return (y * g.astype(jnp.float32)).astype(x.dtype)

def s5_branch(u, a_re, a_im, log_dt, b_re, b_im, c_re, c_im, d, w_glu, b_glu):
    f32 = jnp.float32
    bn, L, _ = u.shape
    u32 = u.astype(f32).reshape(bn, L, SSM_GROUPS, SSM_GROUP)
    lam = lax.complex(a_re.astype(f32), a_im.astype(f32))
    dt = jnp.exp(log_dt.astype(f32))[:, None]
    a_bar = jnp.exp(lam * dt)
    b_bar = ((a_bar - 1.0) / lam)[..., None] * lax.complex(b_re.astype(f32), b_im.astype(f32))
    bu = jnp.einsum('blgc,gpc->blgp', u32.astype(jnp.complex64), b_bar)
    a_seq = jnp.broadcast_to(a_bar, (1, L) + a_bar.shape)

    def combine(e1, e2):
        a1, b1 = e1
        a2, b2 = e2
        return a1 * a2, a2 * b1 + b2

    _, states = lax.associative_scan(combine, (a_seq, bu), axis=1)
    c = lax.complex(c_re.astype(f32), c_im.astype(f32))
    y = jnp.real(jnp.einsum('blgp,gcp->blgc', states, c)) + d.astype(f32).reshape(SSM_GROUPS, SSM_GROUP) * u32
    y = jax.nn.gelu(y.reshape(bn, L, SSM_WIDTH))
    y = y * jax.nn.sigmoid(y @ w_glu.astype(f32) + b_glu.astype(f32))
    return y.astype(u.dtype)

def causal_depthwise_conv(x, w, b):
    K = w.shape[0]
    L = x.shape[1]
    xp = jnp.pad(x, ((0, 0), (K - 1, 0), (0, 0)))
    return sum(xp[:, j:j + L] * w[j] for j in range(K)) + b

def blockdiag(x, w):
    sh = x.shape
    xb = x.reshape(sh[:-1] + (w.shape[0], w.shape[1]))
    return jnp.einsum('blnc,ncd->blnd', xb, w).reshape(sh)

def mlstm_chunk_step(carry, xs):
    c_mat, n_vec, m_st = carry
    q, k, v, log_i, log_f = xs
    b = jnp.cumsum(log_f, axis=-1)
    g = b[..., -1]
    causal = jnp.tril(jnp.ones((ML_CHUNK, ML_CHUNK), dtype=bool))
    d_log = jnp.where(causal, b[..., :, None] - b[..., None, :] + log_i[..., None, :], -jnp.inf)
    inter_log = b + m_st[..., None]
    m_t = jnp.maximum(inter_log, jnp.max(d_log, axis=-1))
    w_intra = jnp.exp(d_log - m_t[..., None])
    s = jnp.einsum('bhtd,bhsd->bhts', q, k) * w_intra
    w_inter = jnp.exp(inter_log - m_t)
    num = jnp.einsum('bhts,bhsd->bhtd', s, v) + w_inter[..., None] * jnp.einsum('bhed,bhtd->bhte', c_mat, q)
    den = jnp.sum(s, axis=-1) + w_inter * jnp.einsum('bhd,bhtd->bht', n_vec, q)
    h = num / jnp.maximum(jnp.abs(den), jnp.exp(-m_t))[..., None]
    a = g[..., None] - b + log_i
    m_new = jnp.maximum(g + m_st, jnp.max(a, axis=-1))
    w_state = jnp.exp(a - m_new[..., None])
    decay = jnp.exp(g + m_st - m_new)
    c_new = decay[..., None, None] * c_mat + jnp.einsum('bhs,bhse,bhsd->bhed', w_state, v, k)
    n_new = decay[..., None] * n_vec + jnp.einsum('bhs,bhsd->bhd', w_state, k)
    return (c_new, n_new, m_new), h

def mlstm_branch(xm, z, conv_w, conv_b, wq, wk, wv, w_if, b_if, norm_g, skip):
    f32 = jnp.float32
    bn, L, _ = xm.shape
    H, dh = ML_HEADS, ML_HEAD_DIM
    xc = jax.nn.silu(causal_depthwise_conv(xm, conv_w, conv_b))
    q = blockdiag(xc, wq)
    k = blockdiag(xc, wk)
    v = blockdiag(xm, wv)
    gates = (jnp.concatenate([q, k, v], axis=-1) @ w_if + b_if).astype(f32)
    log_i = gates[..., :H]
    log_f = jax.nn.log_sigmoid(gates[..., H:])
    k = k * (dh ** -0.5)
    pad_f = (-N_META) % ML_CHUNK
    pad_b = (-(L + pad_f)) % ML_CHUNK
    n_chunks = (L + pad_f + pad_b) // ML_CHUNK

    def heads_to_chunks(t):
        t = jnp.pad(t.astype(f32).reshape(bn, L, H, dh), ((0, 0), (pad_f, pad_b), (0, 0), (0, 0)))
        return t.reshape(bn, n_chunks, ML_CHUNK, H, dh).transpose(1, 0, 3, 2, 4)

    def gate_to_chunks(t):
        t = jnp.pad(t, ((0, 0), (pad_f, pad_b), (0, 0)))
        return t.reshape(bn, n_chunks, ML_CHUNK, H).transpose(1, 0, 3, 2)

    init = (jnp.zeros((bn, H, dh, dh), f32), jnp.zeros((bn, H, dh), f32), jnp.zeros((bn, H), f32))
    _, hc = lax.scan(mlstm_chunk_step, init,
                     (heads_to_chunks(q), heads_to_chunks(k), heads_to_chunks(v),
                      gate_to_chunks(log_i), gate_to_chunks(log_f)))
    h = hc.transpose(1, 0, 3, 2, 4).reshape(bn, n_chunks * ML_CHUNK, H, dh)[:, pad_f:pad_f + L]
    h = jax.nn.sigmoid(z.astype(f32)).reshape(bn, L, H, dh) * h
    h = h * lax.rsqrt(jnp.mean(h * h, axis=-1, keepdims=True) + NORM_EPS)
    h = h.reshape(bn, L, ML_WIDTH) * norm_g.astype(f32) + skip.astype(f32) * xc.astype(f32)
    return h.astype(xm.dtype)

def peer_ffn(xn, w_q, sub_keys, u_tab, v_tab):
    f32 = jnp.float32
    bn, L, D = xn.shape
    T = bn * L
    n_blk = -(-T // PEER_TOKEN_BLOCK)
    xt = jnp.pad(xn.reshape(T, D), ((0, n_blk * PEER_TOKEN_BLOCK - T), (0, 0)))
    xt = xt.reshape(n_blk, PEER_TOKEN_BLOCK, D)
    keys32 = sub_keys.astype(f32)

    def block(xb):
        q = (xb @ w_q).astype(f32).reshape(PEER_TOKEN_BLOCK, PEER_HEADS, 2, PEER_HALF)
        s = jnp.einsum('thid,hikd->thik', q, keys32)
        sv, si = lax.top_k(s, PEER_TOPK)
        cand = sv[..., 0, :, None] + sv[..., 1, None, :]
        cidx = si[..., 0, :, None] * PEER_NKEYS + si[..., 1, None, :]
        cand = cand.reshape(PEER_TOKEN_BLOCK, PEER_HEADS, PEER_TOPK * PEER_TOPK)
        cidx = cidx.reshape(PEER_TOKEN_BLOCK, PEER_HEADS, PEER_TOPK * PEER_TOPK)
        cs, ci = lax.top_k(cand, PEER_TOPK)
        eidx = jnp.take_along_axis(cidx, ci, axis=-1)
        gate = jax.nn.softmax(cs, axis=-1)
        ug = u_tab[eidx]
        act = jax.nn.gelu(jnp.einsum('td,thkd->thk', xb, ug).astype(f32))
        vg = v_tab[eidx]
        return jnp.einsum('thk,thkd->td', (gate * act).astype(vg.dtype), vg)

    out = lax.map(block, xt).reshape(n_blk * PEER_TOKEN_BLOCK, D)[:T]
    return out.reshape(bn, L, D).astype(xn.dtype)

def second_inputs(seed: int = 0) -> dict:
    key = jax.random.key(seed)
    ks = list(jax.random.split(key, 40))
    f32 = jnp.float32
    it = iter(ks)

    def nrm(shape, scale):
        return jax.random.normal(next(it), shape, f32) * scale

    def gain(shape):
        return 1.0 + nrm(shape, 0.02)

    Dp = DEPTH
    x = nrm((BATCH, SEQ, D_MODEL), 1.0)
    meta_tokens = nrm((N_META, D_MODEL), 1.0)
    norm1_g = gain((Dp, D_MODEL))
    w_in = nrm((Dp, D_MODEL, IN_COLS_2), D_MODEL ** -0.5)
    ssm_a_re = -0.5 * jnp.exp(nrm((Dp, SSM_GROUPS, SSM_STATE), 0.05))
    ssm_a_im = jnp.pi * jnp.arange(SSM_STATE, dtype=f32) + nrm((Dp, SSM_GROUPS, SSM_STATE), 0.01)
    ssm_log_dt = jax.random.uniform(next(it), (Dp, SSM_GROUPS), f32, math.log(1e-3), math.log(1e-1))
    ssm_b_re = nrm((Dp, SSM_GROUPS, SSM_STATE, SSM_GROUP), (2 * SSM_GROUP) ** -0.5)
    ssm_b_im = nrm((Dp, SSM_GROUPS, SSM_STATE, SSM_GROUP), (2 * SSM_GROUP) ** -0.5)
    ssm_c_re = nrm((Dp, SSM_GROUPS, SSM_GROUP, SSM_STATE), (2 * SSM_STATE) ** -0.5)
    ssm_c_im = nrm((Dp, SSM_GROUPS, SSM_GROUP, SSM_STATE), (2 * SSM_STATE) ** -0.5)
    ssm_d = nrm((Dp, SSM_WIDTH), 0.5)
    ssm_w_glu = nrm((Dp, SSM_WIDTH, SSM_WIDTH), SSM_WIDTH ** -0.5)
    ssm_b_glu = nrm((Dp, SSM_WIDTH), 0.02)
    w_ssm_out = nrm((Dp, SSM_WIDTH, D_MODEL), SSM_WIDTH ** -0.5)
    ml_conv_w = nrm((Dp, ML_CONV, ML_WIDTH), 0.5)
    ml_conv_b = nrm((Dp, ML_WIDTH), 0.02)
    nb = ML_WIDTH // ML_QKV_BLOCK
    ml_wq = nrm((Dp, nb, ML_QKV_BLOCK, ML_QKV_BLOCK), ML_QKV_BLOCK ** -0.5)
    ml_wk = nrm((Dp, nb, ML_QKV_BLOCK, ML_QKV_BLOCK), ML_QKV_BLOCK ** -0.5)
    ml_wv = nrm((Dp, nb, ML_QKV_BLOCK, ML_QKV_BLOCK), ML_QKV_BLOCK ** -0.5)
    ml_w_if = nrm((Dp, 3 * ML_WIDTH, 2 * ML_HEADS), (3 * ML_WIDTH) ** -0.5)
    ml_b_if = jnp.concatenate([nrm((Dp, ML_HEADS), 0.1),
                               3.0 + 3.0 * jax.random.uniform(next(it), (Dp, ML_HEADS), f32)], axis=-1)
    ml_norm_g = gain((Dp, ML_WIDTH))
    ml_skip = 1.0 + nrm((Dp, ML_WIDTH), 0.1)
    w_ml_out = nrm((Dp, ML_WIDTH, D_MODEL), ML_WIDTH ** -0.5)
    w_out = nrm((Dp, D_MODEL, D_MODEL), D_MODEL ** -0.5)
    norm2_g = gain((Dp, D_MODEL))
    peer_w_q = nrm((Dp, D_MODEL, PEER_HEADS * PEER_QDIM), D_MODEL ** -0.5)
    peer_sub_keys = nrm((Dp, PEER_HEADS, 2, PEER_NKEYS, PEER_HALF), PEER_HALF ** -0.5)
    peer_u = nrm((Dp, PEER_EXPERTS, D_MODEL), D_MODEL ** -0.5)
    peer_v = nrm((Dp, PEER_EXPERTS, D_MODEL), 0.5 * PEER_HEADS ** -0.5)
    final_norm_g = gain((D_MODEL,))
    return {"x": x, "meta_tokens": meta_tokens, "norm1_g": norm1_g, "w_in": w_in,
            "ssm_a_re": ssm_a_re, "ssm_a_im": ssm_a_im, "ssm_log_dt": ssm_log_dt,
            "ssm_b_re": ssm_b_re, "ssm_b_im": ssm_b_im, "ssm_c_re": ssm_c_re, "ssm_c_im": ssm_c_im,
            "ssm_d": ssm_d, "ssm_w_glu": ssm_w_glu, "ssm_b_glu": ssm_b_glu, "w_ssm_out": w_ssm_out,
            "ml_conv_w": ml_conv_w, "ml_conv_b": ml_conv_b, "ml_wq": ml_wq, "ml_wk": ml_wk, "ml_wv": ml_wv,
            "ml_w_if": ml_w_if, "ml_b_if": ml_b_if, "ml_norm_g": ml_norm_g, "ml_skip": ml_skip,
            "w_ml_out": w_ml_out, "w_out": w_out, "norm2_g": norm2_g, "peer_w_q": peer_w_q,
            "peer_sub_keys": peer_sub_keys, "peer_u": peer_u, "peer_v": peer_v,
            "final_norm_g": final_norm_g}

def second_block(x, meta_tokens, norm1_g, w_in, ssm_a_re, ssm_a_im, ssm_log_dt, ssm_b_re, ssm_b_im,
              ssm_c_re, ssm_c_im, ssm_d, ssm_w_glu, ssm_b_glu, w_ssm_out, ml_conv_w, ml_conv_b,
              ml_wq, ml_wk, ml_wv, ml_w_if, ml_b_if, ml_norm_g, ml_skip, w_ml_out, w_out, norm2_g,
              peer_w_q, peer_sub_keys, peer_u, peer_v, final_norm_g):
    bn = x.shape[0]
    meta = jnp.broadcast_to(meta_tokens.astype(x.dtype)[None], (bn, N_META, D_MODEL))
    h = jnp.concatenate([meta, x], axis=1)
    splits = [SSM_WIDTH, SSM_WIDTH + ML_WIDTH, SSM_WIDTH + 2 * ML_WIDTH,
              SSM_WIDTH + 2 * ML_WIDTH + D_MODEL]
    for l in range(DEPTH):
        xn = rmsnorm(h, norm1_g[l])
        proj = xn @ w_in[l]
        u_s, x_m, z_m, g_s, g_m = jnp.split(proj, splits, axis=-1)
        y_s = s5_branch(u_s, ssm_a_re[l], ssm_a_im[l], ssm_log_dt[l], ssm_b_re[l], ssm_b_im[l],
                        ssm_c_re[l], ssm_c_im[l], ssm_d[l], ssm_w_glu[l], ssm_b_glu[l]) @ w_ssm_out[l]
        y_m = mlstm_branch(x_m, z_m, ml_conv_w[l], ml_conv_b[l], ml_wq[l], ml_wk[l], ml_wv[l],
                           ml_w_if[l], ml_b_if[l], ml_norm_g[l], ml_skip[l]) @ w_ml_out[l]
        mixed = jax.nn.sigmoid(g_s) * y_s + jax.nn.sigmoid(g_m) * y_m
        h = h + mixed @ w_out[l]
        h = h + peer_ffn(rmsnorm(h, norm2_g[l]), peer_w_q[l], peer_sub_keys[l], peer_u[l], peer_v[l])
    return rmsnorm(h, final_norm_g)[:, N_META:]


def setup_inputs(seed=0):
    out = dict(first_inputs(seed))
    for name, value in second_inputs(seed + 1).items():
        if name != "x":
            out[name + "_2"] = value
    return out


def reference(
    x, mix_norm_g, w_in, gate_b, sc_conv_w, sc_out, sb_out, rw_mu, rw_w0, rw_w2, rw_a0, rw_a2,
    rw_g2, rw_k_k, rw_k_a, rw_r_k, rw_gn_g, rw_gn_b, rw_out, sg_ln_g, sg_ln_b, sg_w, sg_b,
    sg_out, w_o, ffn_norm_g, w_up, ffn_conv_w, w_down, final_norm_g, meta_tokens_2, norm1_g_2,
    w_in_2, ssm_a_re_2, ssm_a_im_2, ssm_log_dt_2, ssm_b_re_2, ssm_b_im_2, ssm_c_re_2,
    ssm_c_im_2, ssm_d_2, ssm_w_glu_2, ssm_b_glu_2, w_ssm_out_2, ml_conv_w_2, ml_conv_b_2,
    ml_wq_2, ml_wk_2, ml_wv_2, ml_w_if_2, ml_b_if_2, ml_norm_g_2, ml_skip_2, w_ml_out_2,
    w_out_2, norm2_g_2, peer_w_q_2, peer_sub_keys_2, peer_u_2, peer_v_2, final_norm_g_2,
):
    x = first_block(
        x, mix_norm_g, w_in, gate_b, sc_conv_w, sc_out, sb_out, rw_mu, rw_w0, rw_w2, rw_a0,
        rw_a2, rw_g2, rw_k_k, rw_k_a, rw_r_k, rw_gn_g, rw_gn_b, rw_out, sg_ln_g, sg_ln_b, sg_w,
        sg_b, sg_out, w_o, ffn_norm_g, w_up, ffn_conv_w, w_down, final_norm_g,
    )
    return second_block(
        x, meta_tokens_2, norm1_g_2, w_in_2, ssm_a_re_2, ssm_a_im_2, ssm_log_dt_2, ssm_b_re_2,
        ssm_b_im_2, ssm_c_re_2, ssm_c_im_2, ssm_d_2, ssm_w_glu_2, ssm_b_glu_2, w_ssm_out_2,
        ml_conv_w_2, ml_conv_b_2, ml_wq_2, ml_wk_2, ml_wv_2, ml_w_if_2, ml_b_if_2, ml_norm_g_2,
        ml_skip_2, w_ml_out_2, w_out_2, norm2_g_2, peer_w_q_2, peer_sub_keys_2, peer_u_2,
        peer_v_2, final_norm_g_2,
    )


_drawn_inputs = setup_inputs


def setup_inputs(seed=0):
    import zlib

    import numpy as np

    out = dict(_drawn_inputs(seed))
    spreads = {}
    factors = {'rw_w2': 2.784,
     'rw_a0': 4.538,
     'rw_k_k': 29.028,
     'rw_k_a': 4.3,
     'rw_gn_g': 4.486,
     'rw_gn_b': 8.0,
     'sg_ln_g': 8.0,
     'sg_ln_b': 46.047,
     'sg_b': 4.116,
     'ssm_a_re_2': 64.0,
     'ssm_a_im_2': 41.152,
     'ssm_log_dt_2': 42.104,
     'ssm_b_re_2': 50.36,
     'ssm_b_im_2': 51.648,
     'ssm_c_re_2': 50.368,
     'ssm_c_im_2': 51.184,
     'ssm_w_glu_2': 9.986,
     'ssm_b_glu_2': 64.0,
     'ml_conv_b_2': 3.068,
     'ml_norm_g_2': 4.722,
     'norm2_g_2': 13.486,
     'final_norm_g_2': 7.885,
     'ml_skip_2': 3.424}
    for name, (base, spread) in spreads.items():
        noise = np.random.default_rng([zlib.crc32(name.encode()), seed]).standard_normal(out[name].shape)
        drawn = base * np.exp(spread * noise) if base else spread * noise
        out[name] = jnp.asarray(drawn.astype(out[name].dtype))
    for name, factor in factors.items():
        out[name] = (out[name] * factor).astype(out[name].dtype)
    return out
```

```python
from contextlib import ExitStack

import concourse.bass as bass
from concourse import mybir

P = 128
T = 256
M = 16
TT = T + M
D = 1024
KT = D // P
FT = 2816 // P
EARLY = 8
SLOTS = 8
RMS_EPS = 1e-6
LN_EPS = 1e-5
GN_EPS = 64e-5
DECAY_SCALE = 0.6065306597126334
TWO_PI = 6.283185307179586

ALU = mybir.AluOpType
ACT = mybir.ActivationFunctionType
F32 = mybir.dt.float32
F32R = mybir.dt.float32r
U32 = mybir.dt.uint32
AX = mybir.AxisListType.X

COLS = {"mix_norm_g": 8, "gate_b": 32, "rw_mu": 8, "rw_w0": 2, "rw_a0": 2, "rw_k_k": 2, "rw_k_a": 2,
        "rw_gn_g": 2, "rw_gn_b": 2, "ffn_norm_g": 8, "norm1_g_2": 8, "ssm_d_2": 4, "ssm_b_glu_2": 4,
        "ml_conv_b_2": 8, "ml_norm_g_2": 8, "ml_skip_2": 8, "norm2_g_2": 8, "final_norm_g": 8, "rw_r_k": 2,
        "sc_conv_w": 6, "ffn_conv_w": 3 * 44, "ml_conv_w_2": 32, "ssm_a_re_2": 16, "ssm_a_im_2": 16,
        "ssm_log_dt_2": 16, "ml_b_if_2": 2}
FIRST = {"lora": 512, "ln_rows": 512, "sgw": 512, "sgb": 512, "same": P, "upper": P, "upper_eq": P,
         "level0": P, "levels_t": 6 * P, "after": P, "causal": P, "sb_mask0": T, "sb_mask1": P, "carry": T,
         "eye2": 64}
SECOND = {"b_re": 512, "b_im": 512, "c_re": 512, "c_im": 512, "w_if": 192, "neg0": T, "neg1": T, "sel": 512}


def offsets(sizes):
    out, at = {}, 0
    for name, n in sizes.items():
        out[name] = at
        at += n
    return out, at


class Area:

    def __init__(self, tensor, at=0):
        self.tensor, self.at = tensor, at

    def take(self, *dims):
        n = 1
        for d in dims:
            n *= d
        v = self.tensor[:, self.at:self.at + n]
        self.at += n
        assert self.at <= self.tensor.shape[1], self.at
        if len(dims) == 2:
            v = v.rearrange("p (a b) -> p a b", a=dims[0])
        if len(dims) == 3:
            v = v.rearrange("p (a b c) -> p a b c", a=dims[0], b=dims[1])
        return v


class Ring:

    def __init__(self):
        self.rounds = [0] * SLOTS
        self.block = 0


class Own:

    def __init__(self, eng, steps):
        self.eng, self.steps, self.n = eng, steps, 0

    def link(self, ins):
        self.n += 1
        ins.then_inc(self.steps, 1)
        self.eng.wait_ge(self.steps, self.n)

    def tell(self, ins, sem, value=1):
        ins.then_inc(sem, 1)
        self.eng.wait_ge(sem, value)


def build(nc, out, stream, x_t, meta_t, cols, first, second, last, keep):
    with ExitStack() as ctx:
        sems = {}

        def S(name):
            if name not in sems:
                sems[name] = ctx.enter_context(nc.semaphore(name))
            return sems[name]

        def sb(name, shape, dt=F32):
            return ctx.enter_context(nc.sbuf_tensor(name, shape, dt))

        def split_place(name, shape):
            with nc.sbuf_tensor(name, shape, F32) as whole:
                pass
            return whole, ctx.enter_context(nc.sbuf_tensor(name + "_parts", shape, F32R))

        ring, ring_parts = split_place("ring", [P, SLOTS, D])
        par = sb("par", [P, sum(COLS.values())])
        cst = sb("cst", [P, 3 * P])
        x, x_parts = split_place("x", [P, KT, T])
        h, h_parts = split_place("h", [P, KT, TT])
        scale = sb("scale", [P, TT])
        arena, arena_parts = split_place("arena", [P, 38912])
        bank = [ctx.enter_context(nc.psum_tensor(f"bank{i}", [P, 512], F32)) for i in range(8)]
        ident, ones, iota = cst[:, 0:P], cst[:, P:2 * P], cst[:, 2 * P:3 * P]
        at, _ = offsets(COLS)

        def col(name, i):
            return par[:, at[name] + i:at[name] + i + 1]

        full = [S(f"slot_full{s}") for s in range(SLOTS)]
        used = [S(f"slot_used{s}") for s in range(SLOTS)]
        drained = [S(f"bank_free{b}") for b in range(8)]
        fill = Ring()
        vec, sca, poo = Own(nc.vector, S("vector_step")), Own(nc.scalar, S("scalar_step")), Own(nc.gpsimd, S("pool_step"))

        def load(sp, slots, rounds=1):
            n, base = len(slots), fill.block

            def one(i):
                for q, s in enumerate(slots):
                    sp.wait_ge(used[s], fill.rounds[s] + i) if fill.rounds[s] else None
                    src = stream[bass.ds(base + i * n + q, 1)].rearrange("a p n -> (a p) n")
                    sp.dma_start(ring[:, s, :], src).then_inc(full[s], 16)

            if rounds == 1:
                one(0)
            else:
                assert all(fill.rounds[s] for s in slots)
                with sp.Fori(0, rounds) as i:
                    one(i)
            for s in slots:
                fill.rounds[s] += rounds
            fill.block += n * rounds

        class Tiles:

            def __init__(self):
                self.rounds = [0] * SLOTS
                self.banks = [0] * 8

            def advance(self, slots, rounds, banks):
                for q, s in enumerate(slots):
                    self.rounds[s] += rounds
                    if banks:
                        self.banks[banks[q % len(banks)]] += rounds

        pe_at, ev_at = Tiles(), Tiles()

        def use_of(banks, q, n):
            b = banks[q % len(banks)]
            mine = [r for r in range(n) if banks[r % len(banks)] == b]
            return b, len(mine), mine.index(q)

        def project(pe, slots, banks, rounds, mats):
            def one(i):
                for q, s in enumerate(slots):
                    b, per, before = use_of(banks, q, len(slots))
                    pe.wait_ge(full[s], (i + pe_at.rounds[s] + 1) * 16)
                    pe.wait_ge(drained[b], i * per + pe_at.banks[b] + before + 1)
                    mats(q, ring[:, s, :].rearrange("p (k n) -> p k n", n=P), bank[b], i).then_inc(used[s], 1)

            if rounds == 1:
                one(0)
            else:
                with pe.Fori(0, rounds) as i:
                    one(i)
            pe_at.advance(slots, rounds, banks)

        def evacuate(eng, slots, banks, rounds, take):
            def one(i):
                for q, s in enumerate(slots):
                    b, _, _ = use_of(banks, q, len(slots))
                    eng.wait_ge(used[s], i + ev_at.rounds[s] + 1)
                    take(q, bank[b], i).then_inc(drained[b], 1)

            if rounds == 1:
                one(0)
            else:
                with eng.Fori(0, rounds) as i:
                    one(i)
            ev_at.advance(slots, rounds, banks)

        def channels(width, lo=0):
            def mats(q, w, b, i):
                for k in range(KT):
                    mm = nc.tensor.matmul(b[:, 0:width], w[:, k, :], h[:, k, lo:lo + width],
                                          start=k == 0, stop=k == KT - 1)
                return mm
            return mats

        def tokens(q, w, b, i):
            for tt in range(2):
                for k in range(KT):
                    mm = nc.tensor.matmul(b[:, tt * P:(tt + 1) * P], h[:, k, tt * P:(tt + 1) * P], w[:, k, :],
                                          start=k == 0, stop=k == KT - 1)
            return mm

        normed = {"n": 0}

        def rms_norm(src, dst, gain, eps, squares, width=T, tail=None):
            n = normed["n"]
            normed["n"] += 1
            sq, total, mean, root = S("norm_squares"), S("norm_total"), S("norm_mean"), S("norm_root")
            with nc.Block() as block:
                if tail:
                    @block.sync
                    def _(sp):
                        tail(sp)

                @block.scalar
                def _(act):
                    for k in range(KT):
                        nc.scalar.activation(squares[:, k, 0:width], src(k), ACT.Square).then_inc(sq, 1)
                    act.wait_ge(mean, n + 1)
                    nc.scalar.activation(scale[:, 0:width], scale[:, 0:width], ACT.Sqrt).then_inc(root, 1)

                @block.tensor
                def _(pe):
                    for k in range(KT):
                        pe.wait_ge(sq, n * KT + k + 1)
                        mm = nc.tensor.matmul(bank[7][:, 0:width], ones, squares[:, k, 0:width],
                                              start=k == 0, stop=k == KT - 1)
                    mm.then_inc(total, 1)

                @block.vector
                def _(dve):
                    dve.wait_ge(total, n + 1)
                    vec.link(nc.vector.tensor_scalar(scale[:, 0:width], bank[7][:, 0:width], 1.0 / D, eps,
                                                     ALU.mult, ALU.add))
                    vec.tell(nc.vector.reciprocal(scale[:, 0:width], scale[:, 0:width]), mean, n + 1)
                    dve.wait_ge(root, n + 1)
                    for k in range(KT):
                        last_one = nc.vector.scalar_tensor_tensor(dst(k), src(k), col(gain, k), scale[:, 0:width],
                                                                  ALU.mult, ALU.mult)
                    vec.link(last_one)

        a1 = Area(arena)
        z = a1.take(20, T)
        v_sb, v_sg = a1.take(2, T), a1.take(2, T)
        gates = a1.take(32, T)
        f_at, f_size = offsets(FIRST)
        fst = a1.take(f_size)
        y = a1.take(8, T)
        scratch_at = a1.at
        squares = Area(arena, scratch_at).take(KT, TT)

        def f(name, n=None):
            return fst[:, f_at[name]:f_at[name] + (n or FIRST[name])]

        with nc.Block() as block:
            @block.sync
            def _(sp):
                sp.dma_start(x[:], x_t).then_inc(S("x_in"), 16)
                load(sp, range(SLOTS))

            @block.scalar
            def _(act):
                act.dma_start(cst[:], keep).then_inc(S("constants_in"), 16)
                act.dma_start(par[:], cols).then_inc(S("constants_in"), 16)
                act.dma_start(fst, first).then_inc(S("first_in"), 16)
                act.wait_ge(S("constants_in"), 32)
                act.wait_ge(S("x_in"), 16)
                act.wait_ge(S("first_in"), 16)

            @block.vector
            def _(dve):
                for b in range(8):
                    dve.sem_inc(drained[b], 1)

        rms_norm(lambda k: x[:, k, :], lambda k: h[:, k, 0:T], "mix_norm_g", RMS_EPS, squares)

        with nc.Block() as block:
            @block.sync
            def _(sp):
                load(sp, range(SLOTS), 2)
                load(sp, range(4))

            @block.tensor
            def _(pe):
                project(pe, range(8), range(4), 2, channels(T))
                project(pe, range(4), range(4), 1, channels(T))
                project(pe, range(4, 8), range(4), 1, tokens)

            @block.scalar
            def _(act):
                evacuate(act, range(8), range(4), 2, lambda q, b, i: nc.scalar.activation(
                    z[:, bass.ds(i * 8 + q, 1), :].rearrange("p a t -> p (a t)"), b[:, 0:T], ACT.Copy))
                evacuate(act, range(4), range(4), 1, lambda q, b, i: nc.scalar.activation(
                    z[:, 16 + q, :], b[:, 0:T], ACT.Copy))
                evacuate(act, range(4, 8), range(4), 1, lambda q, b, i: nc.scalar.activation(
                    (v_sb if q < 2 else v_sg)[:, :, q % 2 * P:(q % 2 + 1) * P],
                    b[:, 0:T].rearrange("p (a n) -> p a n", a=2), ACT.Copy))

        a2 = Area(arena, scratch_at)
        shift = a2.take(8, T)
        a_t, b_t, k_t, r_t = (shift[:, 2 * i:2 * i + 2, :] for i in range(4))
        lora_h = a2.take(T)
        w_sig, cum, d_inv, d_prev, kk, kk2, kmod, a_sig, decay, g_rw, bonus = (a2.take(2, T) for _ in range(11))
        tm = a2.take(4, 2, T)
        pairs_at = a2.at
        X, XT, Z, NT, MT, MTak, MTrb, MTrk = (a2.take(8, P) for _ in range(8))
        a3 = Area(arena, pairs_at)
        sb_l, sb_b, sb_k = a3.take(1536), a3.take(1536), a3.take(1536)
        sg_d, sg_q, sg_st = a3.take(2, T), a3.take(2, T), a3.take(8)
        sg_wt = a3.take(4, P)
        a4 = Area(arena, scratch_at + 2048 + T)
        AM, GH = a4.take(8, P), a4.take(8, P)
        n0, phi = a4.take(8, 64), a4.take(8, 64)
        assert a4.at <= scratch_at + 2048 + T + 7 * 512
        rp, y0, yd2, state, sc_c, sc_t = X[:, 0:4, :], X[:, 4:8, :], Z[:, 0:4, :], NT[:, 0, :], y[:, 6:8, :], Z
        rp, y0, yd2 = (v.rearrange("p a b -> p (a b)").rearrange("p (c t) -> p c t", c=2) for v in (rp, y0, yd2))
        st2 = NT.rearrange("p a b -> p (a b)")[:, 0:256].rearrange("p (n c v) -> p n c v", n=2, c=2)
        stp = NT.rearrange("p a b -> p (a b)")[:, 256:384].rearrange("p (c v) -> p c v", c=2)
        B3 = {"p": P, "h": 4}
        r_z, k_z, v_z, g_z = z[:, 0:2, :], z[:, 2:4, :], z[:, 4:6, :], z[:, 7, :]
        q_z, kk_z, u_z = z[:, 14:16, :], z[:, 16:18, :], z[:, 18:20, :]
        LEVELS = 5
        turns = {"n": 0}
        gate_n = {"pe": 0, "act": 0}

        def turn(pe, ins):
            turns["n"] += 1
            ins.then_inc(S("tensor_turn"), 1)
            pe.wait_ge(S("tensor_turn"), turns["n"])

        def four(m):
            return m.unsqueeze(1).broadcast_to([P, 4, m.shape[1]])

        def eight(m):
            return m.unsqueeze(1).broadcast_to([P, 8, m.shape[1]])

        def b3(b, w=T):
            return bank[b][:, :].rearrange("p (c t) -> p c t", t=w)

        def gate_products(pe, n):
            for _ in range(n):
                s = gate_n["pe"] % 4
                project(pe, [s], [s % 2], 1, channels(T))
                gate_n["pe"] += 1

        def gate_reads(act, n):
            for _ in range(n):
                g = gate_n["act"]
                evacuate(act, [g % 4], [g % 2], 1, lambda q, b, i: nc.scalar.activation(
                    gates[:, g, :], b[:, 0:T], ACT.Identity, bias=col("gate_b", g)))
                gate_n["act"] += 1

        with nc.Block() as block:
            @block.sync
            def _(sp):
                load(sp, range(4), 7)
                load(sp, range(4, 8))

            @block.gpsimd
            def _(pool):
                g = nc.gpsimd
                for c in range(2):
                    cx, acc, tap = sc_c[:, c, :], y[:, c, :], y[:, 2 + c, :]
                    poo.link(g.tensor_tensor(cx, z[:, 10 + c, :], z[:, 12 + c, :], ALU.mult))
                    poo.link(g.tensor_scalar(acc, cx, col("sc_conv_w", 4 + c), None, ALU.mult))
                    for back in (1, 2):
                        poo.link(g.tensor_scalar(tap, cx, col("sc_conv_w", 2 * (2 - back) + c), None, ALU.mult))
                        poo.link(g.tensor_tensor(acc[:, back:T], acc[:, back:T], tap[:, 0:T - back], ALU.add))
                    poo.link(g.tensor_tensor(acc, acc, z[:, 8 + c, :], ALU.mult))
                poo.eng.sem_inc(S("short_conv"), 1)

            def grow(dve, v, lev):
                dve.wait_ge(S("level_x"), lev)
                for half in range(2):
                    q4 = slice(4 * half, 4 * half + 4)
                    if lev < LEVELS:
                        vec.link(v.tensor_tensor(X[:, q4, :], X[:, q4, :], b3(4 + half, P), ALU.add))
                    ins = v.tensor_tensor(XT[:, q4, :], XT[:, q4, :], b3(6 + half, P), ALU.add)
                    vec.link(ins) if half == 0 else vec.tell(ins, S("level_grown"), lev)

            @block.vector
            def _(dve):
                v = nc.vector
                vec.link(v.tensor_tensor(shift[:, :, 1:T], z[:, 0:8, 0:T - 1], z[:, 0:8, 1:T], ALU.subtract))
                vec.link(v.tensor_scalar(shift[:, :, 0:1], z[:, 0:8, 0:1], -1.0, None, ALU.mult))
                for c in range(8):
                    ins = v.scalar_tensor_tensor(z[:, c, :], shift[:, c, :], col("rw_mu", c), z[:, c, :],
                                                 ALU.mult, ALU.add)
                vec.tell(ins, S("rw_mixed"))
                for c in range(2):
                    vec.link(v.tensor_scalar(kk[:, c, :], k_z[:, c, :], col("rw_k_k", c), None, ALU.mult))
                vec.tell(v.tensor_tensor(kk2, kk, kk, ALU.mult), S("kk_squares"))

                dve.wait_ge(S("sg_v"), 1)
                mean, rstd = sg_st[:, 0:2], sg_st[:, 2:4]
                vec.link(v.tensor_tensor(sg_wt, f("sgw").rearrange("p (g t) -> p g t", g=4), four(f("causal")), ALU.mult))
                vec.link(v.tensor_reduce(mean, v_sg, AX, ALU.add))
                vec.link(v.tensor_scalar(mean, mean, 1.0 / T, None, ALU.mult))
                for tt in range(2):
                    vec.link(v.tensor_scalar(sg_d[:, tt, :], v_sg[:, tt, :], mean[:, tt:tt + 1], None, ALU.subtract))
                vec.link(v.tensor_tensor(sg_q, sg_d, sg_d, ALU.mult))
                vec.link(v.tensor_reduce(rstd, sg_q, AX, ALU.add))
                vec.link(v.tensor_scalar(rstd, rstd, 1.0 / T, LN_EPS, ALU.mult, ALU.add))
                vec.tell(v.reciprocal(rstd, rstd), S("sg_var"))

                dve.wait_ge(S("sb_logs"), 1)
                parts = [(3, 0), (4, 512), (5, 1024)]
                for b, o in parts:
                    vec.link(v.tensor_scalar(sb_b[:, o:o + 512], bank[b][:, :], 0.125, 0.0, ALU.mult, ALU.min))
                vec.link(v.tensor_tensor(sb_b, sb_b, sb_l, ALU.subtract))
                for b, o in parts:
                    vec.link(v.scalar_tensor_tensor(sb_k[:, o:o + 512], bank[b][:, :], -0.125, sb_b[:, o:o + 512],
                                                    ALU.mult, ALU.add))
                halves = [(sb_k[:, 0:1024].rearrange("p (h t) -> p h t", h=4), four(f("sb_mask0"))),
                          (sb_k[:, 1024:1536].rearrange("p (h t) -> p h t", h=4), four(f("sb_mask1")))]
                vec.link(v.tensor_tensor(halves[0][0], halves[0][0], halves[0][1], ALU.mult))
                vec.tell(v.tensor_tensor(halves[1][0], halves[1][0], halves[1][1], ALU.mult), S("sb_keep"))

                dve.wait_ge(S("rw_sigmoids"), 1)
                for c in range(2):
                    vec.link(v.tensor_tensor_scan(cum[:, c, :], f("carry"), w_sig[:, c, :], 0.0, ALU.mult, ALU.add))
                vec.tell(v.tensor_tensor(d_prev, cum, w_sig, ALU.subtract), S("rw_cum"))
                for c in range(2):
                    vec.link(v.tensor_scalar(kmod[:, c, :], a_sig[:, c, :], -1.0, col("rw_k_a", c), ALU.add, ALU.mult))
                vec.link(v.scalar_tensor_tensor(kmod, kmod, 1.0, k_z, ALU.add, ALU.mult))
                dve.wait_ge(S("kk_root"), 1)
                vec.link(v.tensor_scalar(kk2, kk2, 1e-12, None, ALU.max))
                vec.link(v.reciprocal(kk2, kk2))
                vec.link(v.tensor_tensor(kk, kk, kk2, ALU.mult))
                for c in range(2):
                    ins = v.scalar_tensor_tensor(kk2[:, c, :], r_z[:, c, :], col("rw_r_k", c), kmod[:, c, :],
                                                 ALU.mult, ALU.mult)
                vec.tell(ins, S("rw_rk"))
                dve.wait_ge(S("rw_decays"), 1)
                vec.link(v.scalar_tensor_tensor(a_t, kk, -1.0, d_prev, ALU.mult, ALU.mult))
                vec.link(v.tensor_tensor(kk, kk, a_sig, ALU.mult))
                vec.link(v.tensor_tensor(b_t, kk, d_inv, ALU.mult))
                vec.link(v.tensor_tensor(k_t, kmod, d_inv, ALU.mult))
                vec.tell(v.tensor_tensor(r_t, r_z, decay, ALU.mult), S("rw_scaled"))

                dve.wait_ge(S("sg_root"), 1)
                for tt in range(2):
                    vec.link(v.scalar_tensor_tensor(sg_q[:, tt, :], sg_d[:, tt, :], rstd[:, tt:tt + 1],
                                                    f("ln_rows")[:, 0:T], ALU.mult, ALU.mult))
                vec.tell(v.tensor_tensor(sg_q, sg_q, f("ln_rows")[:, T:2 * T].unsqueeze(1).broadcast_to([P, 2, T]),
                                         ALU.add), S("sg_normed"))

                dve.wait_ge(S("sb_suffix"), 1)
                for b, o in ((5, 0), (6, 512), (7, 1024)):
                    ins = v.tensor_tensor(sb_b[:, o:o + 512], sb_b[:, o:o + 512], bank[b][:, :], ALU.add)
                vec.tell(ins, S("sb_arg"))
                dve.wait_ge(S("rw_bonus"), 1)
                vec.tell(v.tensor_tensor(bonus, b3(4), v_z, ALU.mult), S("rw_bonus_read"))
                dve.wait_ge(S("sb_exp"), 1)
                vec.link(v.tensor_tensor(halves[0][0], halves[0][0], halves[0][1], ALU.mult))
                vec.tell(v.tensor_tensor(halves[1][0], halves[1][0], halves[1][1], ALU.mult), S("sb_weights"))
                dve.wait_ge(S("sg_mixed"), 1)
                dve.wait_ge(S("short_conv"), 1)
                vec.link(v.tensor_tensor(y[:, 6:8, :], b3(2), f("sgb").rearrange("p (c t) -> p c t", c=2), ALU.add))
                vec.link(v.tensor_tensor(y[:, 6:8, :], y[:, 6:8, :], u_z, ALU.mult))
                dve.wait_ge(S("sb_out"), 1)
                vec.tell(v.tensor_copy(y[:, 2:4, :], b3(3)), S("early_read"))

                n = 0
                lv = f("levels_t").rearrange("p (l t) -> p l t", l=6)
                for odd in range(2):
                    q4 = slice(4 * odd, 4 * odd + 4)
                    for kind in range(5):
                        b = 2 + n % 6
                        dve.wait_ge(S("pair_done"), n + 1)
                        src = b3(b, P)
                        if kind == 0:
                            vec.tell(v.tensor_tensor(X[:, q4, :], src, four(f("level0")), ALU.mult), S("pair_read"), n + 1)
                            vec.link(v.tensor_tensor(X[:, q4, :], X[:, q4, :], four(ident), ALU.add))
                        elif kind == 1:
                            vec.tell(v.tensor_copy(MT[:, q4, :], src), S("pair_read"), n + 1)
                            vec.link(v.tensor_tensor(XT[:, q4, :], MT[:, q4, :], four(lv[:, 0, :]), ALU.mult))
                            vec.link(v.tensor_tensor(XT[:, q4, :], XT[:, q4, :], four(ident), ALU.add))
                        else:
                            dst, m = ((MTak, "upper"), (MTrb, "upper_eq"), (MTrk, "upper_eq"))[kind - 2]
                            vec.tell(v.tensor_tensor(dst[:, q4, :], src, four(f(m)), ALU.mult), S("pair_read"), n + 1)
                        n += 1

                for lev in range(1, LEVELS + 1):
                    if lev > 1:
                        dve.wait_ge(S("level_z"), lev - 1)
                    vec.tell(v.tensor_tensor(NT, MT, eight(lv[:, lev, :]), ALU.mult), S("level_nt"), lev)
                    if lev > 1:
                        grow(dve, v, lev - 1)
                grow(dve, v, LEVELS)
                dve.wait_ge(S("mv_done"), 1)
                vec.tell(v.tensor_copy(AM[:, :, 64:P], b3(2, 64)), S("mv_read"))
                dve.wait_ge(S("chunk_ops"), 1)
                vec.link(v.tensor_tensor(rp, b3(5), r_t, ALU.add))
                vec.link(v.tensor_tensor(phi, b3(7, 64), eight(f("eye2")), ALU.add))
                vec.link(v.tensor_copy(n0, b3(2, 64)))
                vec.link(v.tensor_copy(y0, b3(6)))
                for c in range(4):
                    last_decay = decay[:, :, 64 * c + 63:64 * c + 64].broadcast_to([P, 2, 64])
                    if c == 0:
                        vec.tell(v.tensor_tensor(st2[:, 1], n0[:, 0:2, :], last_decay, ALU.mult), S("rw_state"), 1)
                    elif c < 3:
                        dve.wait_ge(S("state_step"), c)
                        vec.link(v.tensor_tensor(stp, bank[4][:, 0:P].rearrange("p (c v) -> p c v", c=2),
                                                 n0[:, 2 * c:2 * c + 2, :], ALU.add))
                        vec.tell(v.tensor_tensor(st2[:, (c + 1) % 2], stp, last_decay, ALU.mult), S("rw_state"), c + 1)
                dve.wait_ge(S("state_step"), 3)
                vec.tell(v.tensor_tensor(y0[:, :, 64:T], y0[:, :, 64:T], b3(3)[:, :, 64:T], ALU.add), S("rw_y"))

                dve.wait_ge(S("gn_mean"), 1)
                vec.link(v.scalar_tensor_tensor(y0, b3(5), -1.0 / 64, y0, ALU.mult, ALU.add))
                vec.tell(v.tensor_tensor(yd2, y0, y0, ALU.mult), S("gn_squares"))
                dve.wait_ge(S("gn_var"), 1)
                vec.link(v.tensor_scalar(yd2, b3(6), 1.0 / 64, GN_EPS, ALU.mult, ALU.add))
                vec.tell(v.reciprocal(yd2, yd2), S("gn_inverse"))
                dve.wait_ge(S("gn_root"), 1)
                vec.link(v.tensor_tensor(y0, y0, yd2, ALU.mult))
                for c in range(2):
                    vec.link(v.tensor_scalar(y0[:, c, :], y0[:, c, :], col("rw_gn_g", c), col("rw_gn_b", c),
                                             ALU.mult, ALU.add))
                vec.link(v.tensor_tensor(y0, y0, bonus, ALU.add))
                vec.link(v.tensor_tensor(y[:, 4:6, :], y0, g_rw, ALU.mult))

            @block.scalar
            def _(act):
                a = nc.scalar
                sca.tell(a.activation(v_sg, v_sg, ACT.Gelu_apprx_tanh), S("sg_v"))
                a.activation(u_z, u_z, ACT.Gelu_apprx_tanh)
                act.wait_ge(S("sb_scores"), 1)
                for b, o in ((3, 0), (4, 512), (5, 1024)):
                    ins = a.activation(sb_l[:, o:o + 512], bank[b][:, :], ACT.Abs, scale=0.125)
                sca.link(ins)
                sca.link(a.activation(sb_l, sb_l, ACT.Exp, scale=-1.0))
                sca.tell(a.activation(sb_l, sb_l, ACT.Ln, bias=ones[:, 0:1]), S("sb_logs"))
                act.wait_ge(S("rw_mixed"), 1)
                a.activation(z[0:64, 6, :], z[0:64, 6, :], ACT.Tanh)
                sca.tell(a.activation(lora_h, g_z, ACT.Sigmoid), S("lora_in"))
                gate_reads(act, 2)
                act.wait_ge(S("rw_lora"), 1)
                for c in range(2):
                    a.activation(w_sig[:, c, :], b3(6)[:, c, :], ACT.Sigmoid, bias=col("rw_w0", c))
                    a.activation(a_sig[:, c, :], b3(7)[:, c, :], ACT.Sigmoid, bias=col("rw_a0", c))
                sca.tell(a.activation(g_rw, b3(2), ACT.Copy), S("rw_sigmoids"))
                act.wait_ge(S("kk_sum"), 1)
                sca.tell(a.activation(kk2, b3(3), ACT.Sqrt), S("kk_root"))
                act.wait_ge(S("sg_var"), 1)
                sca.tell(a.activation(sg_st[:, 2:4], sg_st[:, 2:4], ACT.Sqrt), S("sg_root"))
                act.wait_ge(S("rw_cum"), 1)
                a.activation(decay, cum, ACT.Exp, scale=-DECAY_SCALE)
                a.activation(d_inv, cum, ACT.Exp, scale=DECAY_SCALE)
                sca.tell(a.activation(d_prev, d_prev, ACT.Exp, scale=-DECAY_SCALE), S("rw_decays"))
                gate_reads(act, 3)
                act.wait_ge(S("sb_arg"), 1)
                sca.tell(a.activation(sb_k, sb_b, ACT.Exp), S("sb_exp"))
                gate_reads(act, 3)
                act.wait_ge(S("tm_done"), 1)
                for n in range(4):
                    ins = a.activation(tm[:, n], b3(4 + n), ACT.Copy)
                sca.tell(ins, S("tm_read"))
                gate_reads(act, 3)
                for lev in range(1, LEVELS + 1):
                    act.wait_ge(S("level_z"), lev)
                    a.activation(Z[:, 0:4, :], b3(2, P), ACT.Copy)
                    sca.tell(a.activation(Z[:, 4:8, :], b3(3, P), ACT.Copy), S("level_zc"), lev)
                    gate_reads(act, 2)
                for odd in range(2):
                    ins = a.activation(AM[:, 4 * odd:4 * odd + 4, 0:64].rearrange("p (a c) k -> p a c k", a=2),
                                       tm[:, 0].rearrange("p a (c r k) -> p r a c k", c=2, r=2)[:, odd], ACT.Copy)
                ins.then_inc(S("am_a"), 1)
                act.wait_ge(S("gh_done"), 1)
                a.activation(GH[:, 0:4, :], b3(3, P), ACT.Copy)
                sca.tell(a.activation(GH[:, 4:8, :], b3(4, P), ACT.Copy), S("gh_read"))
                gate_reads(act, 5)
                act.wait_ge(S("gn_inverse"), 1)
                sca.tell(a.activation(yd2, yd2, ACT.Sqrt), S("gn_root"))
                gate_reads(act, 6)
                for b in range(2):
                    act.wait_ge(drained[b], ev_at.banks[b] + 1)
                sca.link(a.activation(gates.rearrange("p g t -> p (g t)"), gates.rearrange("p g t -> p (g t)"),
                                      ACT.Sigmoid))

            @block.tensor
            def _(pe):
                mm = nc.tensor.matmul

                def pair(m):
                    odd, tt, c = m // 4, m % 4 // 2, m % 2
                    return 2 * c + odd, c, 64 * odd, tt

                def head(hh):
                    return hh // 2, 64 * (hh % 2)

                for hh in (0, 2, 1, 3):
                    c, p = head(hh)
                    if hh == 1:
                        turn(pe, ins)
                    mm(bank[3 + hh // 2][:, hh % 2 * T:(hh % 2 + 1) * T], kk_z[p:p + 64, c, 0:P], q_z[p:p + 64, c, :],
                       start=True, stop=True)
                    ins = mm(bank[5][:, hh * P:(hh + 1) * P], kk_z[p:p + 64, c, P:T], q_z[p:p + 64, c, P:T],
                             start=True, stop=True)
                ins.then_inc(S("sb_scores"), 1)
                gate_products(pe, 2)
                pe.wait_ge(S("lora_in"), 1)
                lw = f("lora")
                for c in range(2):
                    o = slice(c * T, (c + 1) * T)
                    mm(bank[6][:, o], lw[0:64, c * P:(c + 1) * P], z[0:64, 6, :], start=True, stop=True)
                    mm(bank[7][:, o], lw[64:P, c * P:(c + 1) * P], z[64:P, 6, :], start=True, stop=True)
                    ins = mm(bank[2][:, o], lw[:, T + c * P:T + (c + 1) * P], lora_h, start=True, stop=True)
                ins.then_inc(S("rw_lora"), 1)
                pe.wait_ge(S("kk_squares"), 1)
                pe.wait_ge(S("sb_keep"), 1)
                mm(bank[3][:, :], f("same"), kk2.rearrange("p c t -> p (c t)"), start=True, stop=True)\
                    .then_inc(S("kk_sum"), 1)
                pe.wait_ge(S("rw_sigmoids"), 1)
                k0, k1 = sb_k[:, 0:1024], sb_k[:, 1024:1536]
                mm(bank[7][:, :], f("after"), k1, start=True, stop=True)
                for half in range(2):
                    b = bank[5 + half]
                    mm(b[:, :], f("after"), k0[:, half * 512:(half + 1) * 512], start=True, stop=False)
                    for q in range(2):
                        hh = 2 * half + q
                        ins = mm(b[:, q * T + P:(q + 1) * T], ones, k1[:, hh * P:(hh + 1) * P],
                                 start=False, stop=q == 1)
                ins.then_inc(S("sb_suffix"), 1)
                gate_products(pe, 3)
                pe.wait_ge(S("rw_rk"), 1)
                mm(bank[4][:, :], f("same"), kk2.rearrange("p c t -> p (c t)"), start=True, stop=True)\
                    .then_inc(S("rw_bonus"), 1)
                pe.wait_ge(S("sg_normed"), 1)
                for g in range(4):
                    c, p = head(g)
                    for tt in range(2):
                        ins = mm(bank[2][p:p + 64, c * T + tt * P:c * T + (tt + 1) * P],
                                 sg_q[:, tt, g * 64:(g + 1) * 64], sg_wt[:, g, :], start=True, stop=True)
                ins.then_inc(S("sg_mixed"), 1)
                pe.wait_ge(S("sb_weights"), 1)
                for hh in range(4):
                    c, p = head(hh)
                    mm(bank[3][p:p + 64, c * T:(c + 1) * T], v_sb[:, 0, hh * 64:(hh + 1) * 64],
                       k0[:, hh * T:(hh + 1) * T], start=True, stop=False)
                    ins = mm(bank[3][p:p + 64, c * T + P:(c + 1) * T], v_sb[:, 1, hh * 64:(hh + 1) * 64],
                             k1[:, hh * P:(hh + 1) * P], start=False, stop=True)
                ins.then_inc(S("sb_out"), 1)
                gate_products(pe, 3)
                pe.wait_ge(S("rw_scaled"), 1)
                pe.wait_ge(S("sb_arg"), 1)
                pe.wait_ge(S("rw_bonus_read"), 1)
                for n, m in enumerate((a_t, b_t, k_t, v_z)):
                    for tt in range(2):
                        for c in range(2):
                            o = tt * T + c * P
                            ins = nc.tensor.transpose(bank[4 + n][:, o:o + P], m[:, c, tt * P:(tt + 1) * P], ident)
                ins.then_inc(S("tm_done"), 1)
                gate_products(pe, 3)
                pe.wait_ge(S("early_read"), 1)
                pe.wait_ge(S("tm_read"), 1)
                n = 0
                for odd in range(2):
                    for lhs, rhs in ((a_t, b_t), (b_t, a_t), (k_t, a_t), (b_t, r_t), (k_t, r_t)):
                        if n >= 6:
                            pe.wait_ge(S("pair_read"), n - 5)
                        for m in range(4):
                            _, c, p, tt = pair(4 * odd + m)
                            o = slice(tt * P, (tt + 1) * P)
                            ins = mm(bank[2 + n % 6][:, m * P:(m + 1) * P], lhs[p:p + 64, c, o], rhs[p:p + 64, c, o],
                                     start=True, stop=True)
                        ins.then_inc(S("pair_done"), 1)
                        n += 1
                for lev in range(1, LEVELS + 1):
                    pe.wait_ge(S("level_nt"), lev)
                    if lev == 1:
                        pe.wait_ge(S("pair_read"), 10)
                    else:
                        pe.wait_ge(S("level_grown"), lev - 1)
                    for m in range(8):
                        ins = mm(bank[2 + m // 4][:, m % 4 * P:(m % 4 + 1) * P], NT[:, m, :], X[:, m, :],
                                 start=True, stop=True)
                    ins.then_inc(S("level_z"), 1)
                    gate_products(pe, 1)
                    pe.wait_ge(S("level_zc"), lev)
                    for m in range(8):
                        o = slice(m % 4 * P, (m % 4 + 1) * P)
                        if lev < LEVELS:
                            mm(bank[4 + m // 4][:, o], XT[:, m, :], Z[:, m, :], start=True, stop=True)
                        ins = mm(bank[6 + m // 4][:, o], Z[:, m, :], XT[:, m, :], start=True, stop=True)
                    ins.then_inc(S("level_x"), 1)
                    gate_products(pe, 1)
                for m in range(8):
                    hh, _, _, tt = pair(m)
                    ins = mm(bank[2][:, m * 64:(m + 1) * 64], MTak[:, m, :],
                             tm[:, 3, tt, hh * 64:(hh + 1) * 64], start=True, stop=True)
                ins.then_inc(S("mv_done"), 1)
                pe.wait_ge(S("level_grown"), LEVELS)
                pe.wait_ge(S("mv_read"), 1)
                pe.wait_ge(S("am_a"), 1)
                for m in range(8):
                    ins = mm(bank[3 + m // 4][:, m % 4 * P:(m % 4 + 1) * P], XT[:, m, :], AM[:, m, :],
                             start=True, stop=True)
                ins.then_inc(S("gh_done"), 1)
                gate_products(pe, 2)
                pe.wait_ge(S("gh_read"), 1)
                for m in range(8):
                    hh, c, p, tt = pair(m)
                    o = slice(c * T + tt * P, c * T + (tt + 1) * P)
                    mm(bank[5][p:p + 64, o], GH[:, m, 0:64], MTrb[:, m, :], start=True, stop=True)
                    mm(bank[6][p:p + 64, o], GH[:, m, 64:P], MTrb[:, m, :], start=True, stop=False)
                    mm(bank[6][p:p + 64, o], tm[:, 3, tt, hh * 64:(hh + 1) * 64], MTrk[:, m, :], start=False, stop=True)
                for ch in (0, 2, 1, 3):
                    if ch == 1:
                        turn(pe, ins)
                    tt, r = ch // 2, slice(64 * (ch % 2), 64 * (ch % 2) + 64)
                    for hh in range(4):
                        c, p = head(hh)
                        m, o, hs = 4 * (hh % 2) + 2 * tt + c, slice((2 * ch + c) * 64, (2 * ch + c + 1) * 64), slice(hh * 64, (hh + 1) * 64)
                        mm(bank[7][p:p + 64, o], GH[r, m, 0:64], tm[r, 1, tt, hs], start=True, stop=True)
                        mm(bank[2][p:p + 64, o], tm[r, 1, tt, hs], GH[r, m, 64:P], start=True, stop=False)
                        ins = mm(bank[2][p:p + 64, o], tm[r, 2, tt, hs], tm[r, 3, tt, hs], start=False, stop=True)
                ins.then_inc(S("chunk_ops"), 1)
                gate_products(pe, 3)
                for ch in range(1, 4):
                    pe.wait_ge(S("rw_state"), ch)
                    for hh in range(4):
                        c, p = head(hh)
                        ins = mm(bank[3][p:p + 64, c * T + 64 * ch:c * T + 64 * (ch + 1)], st2[p:p + 64, ch % 2, c, :],
                                 rp[p:p + 64, c, 64 * ch:64 * (ch + 1)], start=True, stop=True)
                    if ch < 3:
                        for hh in range(4):
                            c, p = head(hh)
                            ins = mm(bank[4][p:p + 64, c * 64:(c + 1) * 64], phi[p:p + 64, 2 * ch + c, :],
                                     st2[p:p + 64, ch % 2, c, :], start=True, stop=True)
                    ins.then_inc(S("state_step"), 1)
                pe.wait_ge(S("rw_y"), 1)
                mm(bank[5][:, :], f("same"), y0.rearrange("p c t -> p (c t)"), start=True, stop=True)\
                    .then_inc(S("gn_mean"), 1)
                pe.wait_ge(S("gn_squares"), 1)
                mm(bank[6][:, :], f("same"), yd2.rearrange("p c t -> p (c t)"), start=True, stop=True)\
                    .then_inc(S("gn_var"), 1)
                gate_products(pe, 6)

        a5 = Area(arena, scratch_at)
        merged, prod = a5.take(8, T), a5.take(4, T)
        by_branch = gates.rearrange("p (b n) t -> p b n t", b=4)
        with nc.Block() as block:
            @block.sync
            def _(sp):
                load(sp, range(4))
                load(sp, range(4, 8))
                load(sp, range(4))
                load(sp, (4, 5, 6, 7, 0, 1))

            @block.tensor
            def _(pe):
                def branches(q, w, b, i):
                    for br in range(4):
                        dst = (b if br < 2 else bank[4 + q])[:, br % 2 * T:(br % 2 + 1) * T]
                        for k in range(2):
                            mm = nc.tensor.matmul(dst, w[:, 2 * br + k, :], y[:, 2 * br + k, :],
                                                  start=k == 0, stop=k == 1)
                    return mm

                def onto(q, w, b, i):
                    for k in range(KT):
                        mm = nc.tensor.matmul(b[:, 0:T], w[:, k, :], merged[:, k, :], start=k == 0, stop=k == KT - 1)
                    return mm

                project(pe, range(4, 8), range(4), 1, branches)
                project(pe, range(4), range(4), 1, branches)
                pe.wait_ge(S("merged"), KT)
                project(pe, range(4, 8), range(4), 1, onto)
                project(pe, range(4), range(4), 1, onto)

            @block.vector
            def _(dve):
                v = nc.vector

                def merge_one(n, q, b):
                    vec.link(v.tensor_tensor(prod[:, 0:2, :], b[:, :].rearrange("p (c t) -> p c t", c=2),
                                             by_branch[:, 0:2, n, :], ALU.mult))
                    return v.tensor_tensor(prod[:, 2:4, :], b3(4 + q), by_branch[:, 2:4, n, :], ALU.mult)

                for half, slots in enumerate((range(4, 8), range(4))):
                    for q, s in enumerate(slots):
                        evacuate(dve, [s], [q], 1, lambda _, b, i: merge_one(4 * half + q, q, b))
                        dve.wait_ge(drained[q], ev_at.banks[q] + 1)
                        vec.link(v.tensor_tensor(prod[:, 0:2, :], prod[:, 0:2, :], prod[:, 2:4, :], ALU.add))
                        vec.tell(v.tensor_tensor(merged[:, 4 * half + q, :], prod[:, 0, :], prod[:, 1, :], ALU.add),
                                 S("merged"), 4 * half + q + 1)
                for half, slots in enumerate((range(4, 8), range(4))):
                    evacuate(dve, slots, range(4), 1, lambda q, b, i: v.tensor_tensor(
                        x[:, 4 * half + q, :], x[:, 4 * half + q, :], b[:, 0:T], ALU.add))
                dve.wait_ge(drained[3], ev_at.banks[3] + 1)

        rms_norm(lambda k: x[:, k, :], lambda k: h[:, k, 0:T], "ffn_norm_g", RMS_EPS, squares)
        a6 = Area(arena)
        conv = a6.take(2, 2, T)
        hidden = a6.take(2, T)
        xin = a6.take(KT, TT)
        sq2 = a6.take(KT, TT)
        FS = (4, 5, 6, 7, 0, 1)
        with nc.Block() as block:
            r0 = [pe_at.rounds[s] for s in FS]

            @block.sync
            def _(sp):
                sp.dma_start(xin[:, :, 0:M], meta_t).then_inc(S("meta_in"), 16)
                load(sp, FS, FT // 2 - 1)
                load(sp, range(4))
                sp.wait_ge(S("meta_in"), 16)

            @block.tensor
            def _(pe):
                mm = nc.tensor.matmul
                for b in range(4):
                    pe.wait_ge(drained[b], pe_at.banks[b] + 1)
                    mm(bank[b][:, :], ident, x[:, 2 * b:2 * b + 2, :].rearrange("p c t -> p (c t)"), start=True, stop=False)

                def up(i, j):
                    for q in (3 * j, 3 * j + 1):
                        pe.wait_ge(full[FS[q]], (i + r0[q] + 1) * 16)
                        if q == 3 * j and not (isinstance(i, int) and i == 0):
                            pe.wait_ge(S("up_read"), i * 2 + (j - 1))
                        b = bank[4 + 2 * j + q - 3 * j]
                        w = ring[:, FS[q], :].rearrange("p (k n) -> p k n", n=P)
                        for k in range(KT):
                            ins = mm(b[:, 0:T], w[:, k, :], h[:, k, 0:T], start=k == 0, stop=k == KT - 1)
                        ins.then_inc(used[FS[q]], 1)

                def down(i, j, last_one=False):
                    q = 3 * j + 2
                    pe.wait_ge(full[FS[q]], (i + r0[q] + 1) * 16)
                    pe.wait_ge(S("ff_hidden"), i * 2 + j + 1)
                    for n in range(KT):
                        ins = mm(bank[n // 2][:, n % 2 * T:(n % 2 + 1) * T], ring[:, FS[q], n * P:(n + 1) * P],
                                 hidden[:, j, :], start=False, stop=last_one and n % 2 == 1)
                    ins.then_inc(used[FS[q]], 1)

                up(0, 0)
                up(0, 1)
                down(0, 0)
                with pe.Fori(1, FT // 2) as i:
                    up(i, 0)
                    down(i - 1, 1)
                    up(i, 1)
                    down(i, 0)
                down(FT // 2 - 1, 1, True)

            @block.vector
            def _(dve):
                v = nc.vector

                def tap(k, c):
                    return par[:, bass.ds(c + (at["ffn_conv_w"] + 2 * FT * k), 1)]

                with dve.Fori(0, FT // 2) as i:
                    n = 0

                    def link(ins):
                        nonlocal n
                        n += 1
                        ins.then_inc(S("ff_step"), 1)
                        dve.wait_ge(S("ff_step"), i * 14 + n)

                    for j in range(2):
                        for part in range(2):
                            q = 3 * j + part
                            dve.wait_ge(used[FS[q]], i + r0[q] + 1)
                            src, dst, c = bank[4 + 2 * j + part], conv[:, j, part, :], i * 2 + (j + FT * part)
                            link(v.tensor_scalar(dst, src[:, 0:T], tap(2, c), None, ALU.mult))
                            for back in (1, 2):
                                ins = v.scalar_tensor_tensor(dst[:, back:T], src[:, 0:T - back], tap(2 - back, c),
                                                             dst[:, back:T], ALU.mult, ALU.add)
                                link(ins)
                        dve.sem_inc(S("up_read"), 1)
                        dve.wait_ge(S("ff_silu"), i * 2 + j + 1)
                        if j == 0:
                            dve.wait_ge(used[FS[2]], i + r0[2])
                        else:
                            dve.wait_ge(used[FS[5]], i + r0[5])
                        link(v.tensor_tensor(hidden[:, j, :], conv[:, j, 0, :], conv[:, j, 1, :], ALU.mult))
                        dve.sem_inc(S("ff_hidden"), 1)
                dve.wait_ge(used[FS[5]], r0[5] + FT // 2)
                for b in range(4):
                    ins = v.tensor_copy(x[:, 2 * b:2 * b + 2, :], b3(b))
                    ins.then_inc(drained[b], 1)
                for b in range(4):
                    dve.wait_ge(drained[b], pe_at.banks[b] + 2)

            @block.scalar
            def _(act):
                with act.Fori(0, FT // 2) as i:
                    for j in range(2):
                        act.wait_ge(S("up_read"), i * 2 + j + 1)
                        nc.scalar.activation(conv[:, j, 0, :], conv[:, j, 0, :], ACT.Silu).then_inc(S("ff_silu"), 1)
            for tiles in (pe_at, ev_at):
                tiles.advance(FS, FT // 2, None)
                for b in range(4):
                    tiles.banks[b] += 1
        rms_norm(lambda k: x[:, k, :], lambda k: xin[:, k, M:TT], "final_norm_g", RMS_EPS, squares_b := sq2)

        rms_norm(lambda k: xin[:, k, :], lambda k: h[:, k, :], "norm1_g_2", RMS_EPS, squares_b, TT)
        a7 = Area(arena, a6.at)
        us, xm = a7.take(4, TT), a7.take(8, TT)
        zg = a7.take(24, T)
        s_at, s_size = offsets(SECOND)
        snd = a7.take(s_size)

        def g2(name, lo=0, n=None):
            return snd[:, s_at[name] + lo:s_at[name] + lo + (n or SECOND[name])]

        with nc.Block() as block:
            @block.sync
            def _(sp):
                sp.dma_start(snd, second).then_inc(S("second_in"), 16)
                load(sp, range(4), 2)
                load(sp, (4, 5, 6))
                load(sp, range(4))
                sp.wait_ge(S("second_in"), 16)

            @block.gpsimd
            def _(pool):
                nc.gpsimd.tensor_copy(x[:], xin[:, :, M:TT]).then_inc(S("residual"), 1)
                pool.wait_ge(S("residual"), 1)

            @block.tensor
            def _(pe):
                project(pe, range(4), range(4), 3, channels(TT))

            @block.scalar
            def _(act):
                both = arena[:, a6.at:a6.at + 12 * TT].rearrange("p (c t) -> p c t", t=TT)
                evacuate(act, range(4), range(4), 3, lambda q, b, i: nc.scalar.activation(
                    both[:, bass.ds(i * 4 + q, 1), :].rearrange("p a t -> p (a t)"), b[:, 0:TT], ACT.Copy))

        r1 = Area(arena)
        e_t = r1.take(2, 1024)
        rows = r1.take(6, TT)
        small = r1.take(20, 16)
        colb = r1.take(3, 4)
        rs4 = r1.take(4, T)
        dmat = [r1.take(640)]
        assert r1.at <= a6.at
        a8 = Area(arena, a7.at)
        er, ei = a8.take(16, TT), a8.take(16, TT)
        xc = a8.take(8, TT)
        dmat.append(a8.take(640))
        s5_at = a8.at
        kc, vc, vt = a8.take(8, TT), a8.take(8, TT), a8.take(3, D)
        qc, h_ml = xm, xm[:, :, M:TT]
        a9 = Area(arena, s5_at)
        bu = a9.take(2, 4, TT)
        zt = a9.take(2, 4, TT)
        rot, rt = a9.take(2, 2 * TT), a9.take(2, 2 * TT)
        s_out = e_t[:, 0, :].rearrange("p (c s t) -> p c s t", c=2, s=2)
        s_tmp = e_t[:, 1, :].rearrange("p (c s t) -> p c s t", c=2, s=2)
        proj_n = {"pe": 0, "act": 0}
        zsig, gs_g, gm_g = zg[:, 0:8, :], zg[:, 8:16, :], zg[:, 16:24, :]
        PAIRS = 8

        def z_products(pe, n):
            for _ in range(n):
                s = proj_n["pe"] % 4
                project(pe, [s], [s % 2], 1, channels(T, M))
                proj_n["pe"] += 1

        def z_reads(act, n):
            for _ in range(n):
                g = proj_n["act"]
                evacuate(act, [g % 4], [g % 2], 1, lambda q, b, i: nc.scalar.activation(zg[:, g, :], b[:, 0:T], ACT.Copy))
                proj_n["act"] += 1

        def sm(n):
            return small[:, n, :]

        (S_DT, S_X, S_TH, S_K, S_R, S_SIN, S_HALF, S_COS, S_TANH, S_EM, S_NR, S_NI, S_DEN, S_CR, S_CI, S_T, S_ER, S_EI,
         S_E2R, S_E2I) = range(20)

        with nc.Block() as block:
            bd = [pe_at.rounds[s] for s in (4, 5, 6)]

            @block.sync
            def _(sp):
                load(sp, range(4), 5)
                load(sp, (7,))
                for s in (4, 5, 6):
                    load(sp, (s,))

            @block.vector
            def _(dve):
                v = nc.vector
                are, aim = par[:, at["ssm_a_re_2"]:at["ssm_a_re_2"] + 16], par[:, at["ssm_a_im_2"]:at["ssm_a_im_2"] + 16]
                dve.wait_ge(S("s5_dt"), 1)
                vec.link(v.tensor_tensor(sm(S_X), are, sm(S_DT), ALU.mult))
                vec.link(v.tensor_tensor(sm(S_TH), aim, sm(S_DT), ALU.mult))
                vec.link(v.tensor_scalar(sm(S_K), sm(S_TH), 1.0 / TWO_PI, None, ALU.mult))
                vec.link(v.tensor_scalar(sm(S_K), sm(S_K), 12582912.0, None, ALU.add))
                vec.link(v.tensor_scalar(sm(S_K), sm(S_K), 12582912.0, None, ALU.subtract))
                vec.link(v.scalar_tensor_tensor(sm(S_TH), sm(S_K), -6.28125, sm(S_TH), ALU.mult, ALU.add))
                vec.link(v.scalar_tensor_tensor(sm(S_TH), sm(S_K), -0.0019353071795864769, sm(S_TH), ALU.mult, ALU.add))
                vec.tell(v.tensor_scalar(sm(S_TH), sm(S_TH), 3.1415925, -3.1415925, ALU.min, ALU.max), S("s5_angle"))
                w0 = at["ml_conv_w_2"]
                for c in range(8):
                    vec.link(v.tensor_scalar(xc[:, c, :], xm[:, c, :], par[:, w0 + 24 + c:w0 + 25 + c],
                                             col("ml_conv_b_2", c), ALU.mult, ALU.add))
                    for back in (1, 2, 3):
                        j = w0 + 8 * (3 - back) + c
                        ins = v.scalar_tensor_tensor(xc[:, c, back:TT], xm[:, c, 0:TT - back], par[:, j:j + 1],
                                                     xc[:, c, back:TT], ALU.mult, ALU.add)
                        vec.link(ins) if back < 3 else vec.tell(ins, S("ml_conv"), c + 1)
                dve.wait_ge(S("s5_sines"), 1)
                vec.link(v.tensor_tensor(sm(S_T), sm(S_HALF), sm(S_HALF), ALU.mult))
                vec.link(v.tensor_scalar(sm(S_COS), sm(S_T), -2.0, 1.0, ALU.mult, ALU.add))
                vec.link(v.tensor_copy(sm(S_ER), sm(S_COS)))
                vec.tell(v.tensor_copy(sm(S_EI), sm(S_SIN)), S("s5_unit"))
                vec.link(v.tensor_scalar(sm(S_DEN), sm(S_TANH), -1.0, 1.0, ALU.mult, ALU.add))
                vec.link(v.reciprocal(sm(S_DEN), sm(S_DEN)))
                vec.link(v.scalar_tensor_tensor(sm(S_EM), sm(S_TANH), 2.0, sm(S_DEN), ALU.mult, ALU.mult))
                vec.link(v.tensor_tensor(sm(S_NR), sm(S_EM), sm(S_COS), ALU.mult))
                vec.link(v.scalar_tensor_tensor(sm(S_NR), sm(S_T), -2.0, sm(S_NR), ALU.mult, ALU.add))
                vec.link(v.tensor_tensor(sm(S_NI), sm(S_R), sm(S_SIN), ALU.mult))
                vec.link(v.tensor_tensor(sm(S_DEN), are, are, ALU.mult))
                vec.link(v.tensor_tensor(sm(S_T), aim, aim, ALU.mult))
                vec.link(v.tensor_tensor(sm(S_DEN), sm(S_DEN), sm(S_T), ALU.add))
                vec.link(v.reciprocal(sm(S_DEN), sm(S_DEN)))
                vec.link(v.tensor_tensor(sm(S_CR), sm(S_NR), are, ALU.mult))
                vec.link(v.tensor_tensor(sm(S_T), sm(S_NI), aim, ALU.mult))
                vec.link(v.tensor_tensor(sm(S_CR), sm(S_CR), sm(S_T), ALU.add))
                vec.link(v.tensor_tensor(sm(S_CR), sm(S_CR), sm(S_DEN), ALU.mult))
                vec.link(v.tensor_tensor(sm(S_CI), sm(S_NI), are, ALU.mult))
                vec.link(v.tensor_tensor(sm(S_T), sm(S_NR), aim, ALU.mult))
                vec.link(v.tensor_tensor(sm(S_CI), sm(S_CI), sm(S_T), ALU.subtract))
                vec.link(v.tensor_tensor(sm(S_CI), sm(S_CI), sm(S_DEN), ALU.mult))
                c_re, c_im = (g2(n).rearrange("p (s c) -> p s c", s=16) for n in ("c_re", "c_im"))
                t0, t1, t2 = (rs4.rearrange("p a b -> p (a b)")[:, 0:512].rearrange("p (s c) -> p s c", s=16),
                              dmat[0][:, 0:512].rearrange("p (s c) -> p s c", s=16),
                              dmat[1][:, 0:512].rearrange("p (s c) -> p s c", s=16))
                cr, ci = (sm(n).unsqueeze(2).broadcast_to([P, 16, 32]) for n in (S_CR, S_CI))
                vec.link(v.tensor_tensor(t0, c_re, cr, ALU.mult))
                vec.link(v.tensor_tensor(t1, c_im, ci, ALU.mult))
                vec.link(v.tensor_tensor(t0, t0, t1, ALU.subtract))
                vec.link(v.tensor_tensor(t1, c_re, ci, ALU.mult))
                vec.link(v.tensor_tensor(t2, c_im, cr, ALU.mult))
                vec.link(v.tensor_copy(c_re, t0))
                vec.link(v.scalar_tensor_tensor(c_im, t1, -1.0, t2, ALU.mult, ALU.subtract))

                dve.wait_ge(S("if_sum"), 1)
                vec.tell(v.tensor_copy(rows[0:8, 5, :], bank[6][0:8, 0:TT]), S("if_rows"))
                dve.wait_ge(S("if_split"), 1)
                ig, lf, cf, mx, ab, tr = (rows[0:4, n, :] for n in range(6))
                vec.link(v.tensor_scalar(ig, bank[7][0:4, 0:TT], col("ml_b_if_2", 0)[0:4], None, ALU.add))
                vec.link(v.tensor_scalar(lf, bank[6][0:4, 0:TT], col("ml_b_if_2", 1)[0:4], None, ALU.add))
                vec.tell(v.scalar_tensor_tensor(ab, lf, -1.0, lf, ALU.mult, ALU.max), S("ml_abs"))
                dve.wait_ge(S("ml_log"), 1)
                vec.link(v.tensor_scalar(lf, lf, 0.0, None, ALU.min))
                vec.link(v.tensor_tensor(lf, lf, ab, ALU.subtract))
                one_row = ones[0:4, 0:1].broadcast_to([4, TT])
                vec.link(v.tensor_tensor_scan(cf, one_row, lf, 0.0, ALU.mult, ALU.add))
                vec.link(v.tensor_tensor_scan(mx, lf, ig, 0.0, ALU.add, ALU.max))
                vec.link(v.tensor_tensor(ig, ig, cf, ALU.subtract))
                vec.tell(v.tensor_tensor(cf, cf, mx, ALU.subtract), S("ml_rows"))
                dve.wait_ge(S("ml_cols"), 1)
                vec.tell(v.tensor_copy(colb, bank[5][:, 0:12].rearrange("p (s h) -> p s h", s=3)), S("ml_cols_read"))
                for hh in range(4):
                    d = dmat[hh % 2]
                    d1, d2, dm = d[:, 0:T], d[:, T:T + P], d[0:M, 384:640]
                    dve.wait_ge(S("head_scores"), hh + 1)
                    vec.link(v.scalar_tensor_tensor(d1, bank[2][:, 0:T], colb[:, 1, hh:hh + 1], g2("neg0"),
                                                    ALU.add, ALU.add))
                    vec.link(v.scalar_tensor_tensor(d2, bank[2][:, P:T], colb[:, 2, hh:hh + 1], g2("neg1", P, P),
                                                    ALU.add, ALU.add))
                    vec.tell(v.tensor_scalar(dm, bank[2][0:M, 0:T], colb[0:M, 0, hh:hh + 1], None, ALU.add),
                             S("head_logs"), hh + 1)
                    dve.wait_ge(S("head_exp"), hh + 1)
                    vec.link(v.scalar_tensor_tensor(d[:, 0:384], bank[3][:, 0:384], 0.0625, d[:, 0:384], ALU.mult, ALU.mult))
                    vec.tell(v.scalar_tensor_tensor(dm, bank[4][0:M, 0:T], 0.0625, dm, ALU.mult, ALU.mult),
                             S("head_weights"), hh + 1)
                    dve.wait_ge(S("head_sums"), hh + 1)
                    rd = rs4[:, 0, :]
                    vec.link(v.tensor_scalar(rd, bank[6][:, 0:T], -1.0, None, ALU.mult))
                    vec.link(v.tensor_tensor(rd, rd, bank[6][:, 0:T], ALU.max))
                    vec.link(v.tensor_tensor(rd, rd, bank[2][:, T:2 * T], ALU.max))
                    vec.link(v.reciprocal(rd, rd))
                    vec.tell(v.tensor_tensor(h_ml[:, 2 * hh:2 * hh + 2, :], b3(5), rd.unsqueeze(1).broadcast_to([P, 2, T]),
                                             ALU.mult), S("head_read"), hh + 1)
                dve.wait_ge(S("z_sigmoid"), 1)
                vec.link(v.tensor_tensor(h_ml, h_ml, zsig, ALU.mult))
                hsq = vc[:, :, 0:T]
                vec.tell(v.tensor_tensor(hsq, h_ml, h_ml, ALU.mult), S("ml_squares"))
                dve.wait_ge(S("ml_sums"), 1)
                for half in range(2):
                    vec.link(v.tensor_scalar(rs4[:, 2 * half:2 * half + 2, :], b3(2 + half), 1.0 / T, RMS_EPS,
                                             ALU.mult, ALU.add))
                vec.tell(v.reciprocal(rs4, rs4), S("ml_inverse"))
                dve.wait_ge(S("ml_root"), 1)
                for c in range(8):
                    vec.link(v.scalar_tensor_tensor(h_ml[:, c, :], h_ml[:, c, :], col("ml_norm_g_2", c), rs4[:, c // 2, :],
                                                    ALU.mult, ALU.mult))
                    vec.link(v.scalar_tensor_tensor(h_ml[:, c, :], xc[:, c, M:TT], col("ml_skip_2", c), h_ml[:, c, :],
                                                    ALU.mult, ALU.add))
                dve.sem_inc(S("ml_out"), 1)

                dve.wait_ge(S("tables"), 1)
                for p in range(PAIRS):
                    dve.wait_ge(S("bu_ready"), 4 * p + 4)
                    cs, sn = er[:, 2 * p:2 * p + 2, :], ei[:, 2 * p:2 * p + 2, :]
                    src = bu[:, p % 2].rearrange("p (s c) t -> p c s t", s=2)
                    re, im = src[:, 0], src[:, 1]
                    xr, xi = (rot[:, n, :].rearrange("p (s t) -> p s t", s=2) for n in range(2))
                    q0, q1 = (rt[:, n, :].rearrange("p (s t) -> p s t", s=2) for n in range(2))
                    vec.link(v.tensor_tensor(q0, im, sn, ALU.mult))
                    vec.link(v.tensor_tensor(xr, re, cs, ALU.mult))
                    vec.link(v.tensor_tensor(xr, xr, q0, ALU.add))
                    vec.link(v.tensor_tensor(q1, re, sn, ALU.mult))
                    vec.link(v.tensor_tensor(xi, im, cs, ALU.mult))
                    vec.tell(v.tensor_tensor(xi, xi, q1, ALU.subtract), S("bu_turned"), p + 1)
                    if p >= 2:
                        dve.wait_ge(S("s_ready"), p - 1)
                    for s in range(2):
                        r = sm(S_R)[:, 2 * p + s:2 * p + s + 1].broadcast_to([P, TT])
                        for c, xx in ((0, xr), (1, xi)):
                            ins = v.tensor_tensor_scan(zt[:, p % 2, 2 * c + s, :], r, xx[:, s, :], 0.0, ALU.mult, ALU.add)
                    vec.tell(ins, S("z_ready"), p + 1)
                dve.wait_ge(S("c_done"), PAIRS)
                for c in range(4):
                    ins = v.scalar_tensor_tensor(us[:, c, M:TT], us[:, c, M:TT], col("ssm_d_2", c),
                                                 bank[6 + c // 2][:, c % 2 * T:(c % 2 + 1) * T], ALU.mult, ALU.add)
                vec.tell(ins, S("s5_y"))

            @block.gpsimd
            def _(pool):
                g = nc.gpsimd
                pool.wait_ge(S("s5_unit"), 1)
                poo.link(g.memset(er[:, :, 0:1], 1.0))
                poo.link(g.memset(ei[:, :, 0:1], 0.0))
                n = 1
                while n < TT:
                    w = min(n, TT - n)
                    for half in range(2):
                        o = slice(8 * half, 8 * half + 8)
                        br = sm(S_ER)[:, o].unsqueeze(2).broadcast_to([P, 8, w])
                        bi = sm(S_EI)[:, o].unsqueeze(2).broadcast_to([P, 8, w])
                        ta, tb = (e_t[:, k, 0:8 * min(w, P)].rearrange("p (s t) -> p s t", s=8) for k in range(2))
                        lo_r, lo_i, hi_r, hi_i = er[:, o, 0:w], ei[:, o, 0:w], er[:, o, n:n + w], ei[:, o, n:n + w]
                        poo.link(g.tensor_tensor(hi_r, lo_r, br, ALU.mult))
                        poo.link(g.tensor_tensor(ta, lo_i, bi, ALU.mult))
                        poo.link(g.tensor_tensor(hi_r, hi_r, ta, ALU.subtract))
                        poo.link(g.tensor_tensor(hi_i, lo_i, br, ALU.mult))
                        poo.link(g.tensor_tensor(tb, lo_r, bi, ALU.mult))
                        poo.link(g.tensor_tensor(hi_i, hi_i, tb, ALU.add))
                    poo.link(g.tensor_tensor(sm(S_E2R), sm(S_ER), sm(S_ER), ALU.mult))
                    poo.link(g.tensor_tensor(sm(S_E2I), sm(S_EI), sm(S_EI), ALU.mult))
                    poo.link(g.tensor_tensor(sm(S_EI), sm(S_ER), sm(S_EI), ALU.mult))
                    poo.link(g.tensor_tensor(sm(S_EI), sm(S_EI), sm(S_EI), ALU.add))
                    poo.link(g.tensor_tensor(sm(S_ER), sm(S_E2R), sm(S_E2I), ALU.subtract))
                    n *= 2
                pool.sem_inc(S("tables"), 1)
                for p in range(PAIRS):
                    cs, sn = er[:, 2 * p:2 * p + 2, M:TT], ei[:, 2 * p:2 * p + 2, M:TT]
                    zr, zi = zt[:, p % 2, 0:2, M:TT], zt[:, p % 2, 2:4, M:TT]
                    pool.wait_ge(S("z_ready"), p + 1)
                    if p >= 1:
                        pool.wait_ge(S("c_done"), p)
                    poo.link(g.tensor_tensor(s_out[:, 0], zr, cs, ALU.mult))
                    poo.link(g.tensor_tensor(s_tmp[:, 0], zi, sn, ALU.mult))
                    poo.link(g.tensor_tensor(s_out[:, 0], s_out[:, 0], s_tmp[:, 0], ALU.subtract))
                    poo.link(g.tensor_tensor(s_out[:, 1], zr, sn, ALU.mult))
                    poo.link(g.tensor_tensor(s_tmp[:, 1], zi, cs, ALU.mult))
                    poo.tell(g.tensor_tensor(s_out[:, 1], s_out[:, 1], s_tmp[:, 1], ALU.add), S("s_ready"), p + 1)

            @block.scalar
            def _(act):
                a = nc.scalar
                qn = {"n": 0}

                def read_unit(dst, src):
                    act.wait_ge(S("qkv_done"), qn["n"] + 1)
                    a.activation(dst, src, ACT.Copy).then_inc(S("qkv_read"), 1)
                    qn["n"] += 1

                ldt = par[:, at["ssm_log_dt_2"]:at["ssm_log_dt_2"] + 16]
                sca.tell(a.activation(sm(S_DT), ldt, ACT.Exp), S("s5_dt"))
                z_reads(act, 2)
                act.wait_ge(S("s5_angle"), 1)
                a.activation(sm(S_R), sm(S_X), ACT.Exp)
                a.activation(sm(S_TANH), sm(S_X), ACT.Tanh, scale=0.5)
                a.activation(sm(S_SIN), sm(S_TH), ACT.Sin)
                sca.tell(a.activation(sm(S_HALF), sm(S_TH), ACT.Sin, scale=0.5), S("s5_sines"))
                for k in range(8):
                    read_unit(vc[:, k, :], bank[2 + qn["n"] % 4][:, 0:TT])
                for st in range(3):
                    for half in range(2):
                        n = M if st == 0 else P
                        read_unit(vt[0:n, st, half * 512:(half + 1) * 512], bank[2 + qn["n"] % 4][0:n, :])
                z_reads(act, 2)
                for c in range(8):
                    act.wait_ge(S("ml_conv"), c + 1)
                    a.activation(xc[:, c, :], xc[:, c, :], ACT.Silu).then_inc(S("xc_ready"), 1)
                for dst in (qc, kc):
                    for k in range(8):
                        read_unit(dst[:, k, :], bank[2 + qn["n"] % 4][:, 0:TT])
                z_reads(act, 4)
                for b in range(2):
                    act.wait_ge(drained[b], ev_at.banks[b] + 1)
                sca.tell(a.activation(zsig.rearrange("p c t -> p (c t)"), zsig.rearrange("p c t -> p (c t)"), ACT.Sigmoid),
                         S("z_sigmoid"))
                act.wait_ge(S("ml_abs"), 1)
                ab, mx = rows[0:4, 4, :], rows[0:4, 3, :]
                sca.link(a.activation(ab, ab, ACT.Exp, scale=-1.0))
                sca.tell(a.activation(ab, ab, ACT.Ln, bias=ones[0:4, 0:1]), S("ml_log"))
                act.wait_ge(S("ml_rows"), 1)
                sca.tell(a.activation(mx, mx, ACT.Exp, scale=-1.0), S("ml_expm"))
                z_reads(act, 2)
                for hh in range(4):
                    d = dmat[hh % 2]
                    act.wait_ge(S("head_logs"), hh + 1)
                    a.activation(d[:, 0:384], d[:, 0:384], ACT.Exp)
                    sca.tell(a.activation(d[0:M, 384:640], d[0:M, 384:640], ACT.Exp), S("head_exp"), hh + 1)
                    z_reads(act, 1)
                z_reads(act, 2)
                act.wait_ge(S("ml_inverse"), 1)
                sca.tell(a.activation(rs4, rs4, ACT.Sqrt), S("ml_root"))
                act.wait_ge(S("ml_out"), 1)
                for p in range(PAIRS):
                    act.wait_ge(S("bu_done"), p + 1)
                    if p >= 2:
                        act.wait_ge(S("bu_turned"), p - 1)
                    for n in range(4):
                        a.activation(bu[:, p % 2, n, :], bank[2 + n][:, 0:TT], ACT.Copy).then_inc(S("bu_ready"), 1)
                    z_reads(act, 1)
                for b in range(2):
                    act.wait_ge(drained[b], ev_at.banks[b] + 1)
                sca.link(a.activation(zg[:, 8:24, :].rearrange("p c t -> p (c t)"),
                                      zg[:, 8:24, :].rearrange("p c t -> p (c t)"), ACT.Sigmoid))
                act.wait_ge(S("s5_y"), 1)
                sca.link(a.activation(us[:, :, M:TT], us[:, :, M:TT], ACT.Gelu_apprx_tanh))

            @block.tensor
            def _(pe):
                mm = nc.tensor.matmul
                blockdiag = [ring[:, s, :].rearrange("p (k n) -> p k n", n=P) for s in (4, 5, 6)]
                un = {"n": 0}

                def unit_bank():
                    n = un["n"]
                    if n >= 4:
                        pe.wait_ge(S("qkv_read"), n - 3)
                    un["n"] += 1
                    return bank[2 + n % 4]

                spans = ((0, M), (M, P), (M + P, P))
                z_products(pe, 2)
                pe.wait_ge(full[6], 16 * (bd[2] + 1))
                for k in range(8):
                    ins = mm(unit_bank()[:, 0:TT], blockdiag[2][:, k, :], xm[:, k, :], start=True, stop=True)
                    ins.then_inc(S("qkv_done"), 1)
                for st, (lo, n) in enumerate(spans):
                    for half in range(2):
                        b = unit_bank()
                        for k in range(4):
                            ins = mm(b[0:n, k * P:(k + 1) * P], xm[:, 4 * half + k, lo:lo + n],
                                     blockdiag[2][:, 4 * half + k, :], start=True, stop=True)
                        ins.then_inc(S("qkv_done"), 1)
                z_products(pe, 2)
                pe.wait_ge(S("xc_ready"), 8)
                for w in range(2):
                    pe.wait_ge(full[4 + w], 16 * (bd[w] + 1))
                    for k in range(8):
                        ins = mm(unit_bank()[:, 0:TT], blockdiag[w][:, k, :], xc[:, k, :], start=True, stop=True)
                        ins.then_inc(S("qkv_done"), 1)
                z_products(pe, 4)
                pe.wait_ge(S("qkv_read"), 30)
                w_if = g2("w_if").rearrange("p (k n) -> p k n", n=8)
                for n in range(24):
                    src = (qc, kc, vc)[n // 8][:, n % 8, :]
                    ins = mm(bank[6][0:8, 0:TT], w_if[:, n, :], src, start=n == 0, stop=n == 23)
                ins.then_inc(S("if_sum"), 1)
                for w in range(3):
                    pe.sem_inc(used[4 + w], 1)
                pe.wait_ge(S("if_rows"), 1)
                mm(bank[7][0:4, 0:TT], ident[0:8, 0:4], rows[0:8, 5, :], start=True, stop=True)
                mm(bank[6][0:4, 0:TT], ident[0:8, 4:8], rows[0:8, 5, :], start=True, stop=True).then_inc(S("if_split"), 1)
                z_products(pe, 2)
                pe.wait_ge(S("ml_rows"), 1)
                for st, (lo, n) in enumerate(spans):
                    ins = mm(bank[5][0:n, 4 * st:4 * st + 4], rows[0:4, 0, lo:lo + n], ident[0:4, 0:4], start=True, stop=True)
                ins.then_inc(S("ml_cols"), 1)
                pe.wait_ge(S("ml_expm"), 1)
                pe.wait_ge(S("ml_cols_read"), 1)
                sel = g2("sel").rearrange("p (h n) -> p h n", h=4)
                for hh in range(4):
                    if hh:
                        pe.wait_ge(S("head_read"), hh)
                    mm(bank[2][:, 0:T], sel[0:4, hh, :], rows[0:4, 2, M:TT], start=True, stop=True)
                    mm(bank[2][:, T:2 * T], sel[0:4, hh, :], rows[0:4, 3, M:TT], start=True, stop=True)
                    for st, (b, off, tlo) in enumerate(((4, 0, 0), (3, 0, 0), (3, T, P))):
                        lo, n = spans[st]
                        for c in (2 * hh, 2 * hh + 1):
                            ins = mm(bank[b][0:n, off:off + T - tlo], kc[:, c, lo:lo + n], qc[:, c, M + tlo:TT],
                                     start=c % 2 == 0, stop=c % 2 == 1)
                    ins.then_inc(S("head_scores"), 1)
                    z_products(pe, 1)
                    pe.wait_ge(S("head_weights"), hh + 1)
                    d = dmat[hh % 2]
                    wts = ((d[:, 0:T], 1, P, 0), (d[:, T:T + P], 2, P, P), (d[0:M, 384:640], 0, M, 0))
                    for e in range(3):
                        for j, (w, st, n, tlo) in enumerate(wts):
                            lhs = ones[0:n, :] if e == 2 else vt[0:n, st, hh * T + e * P:hh * T + (e + 1) * P]
                            dst = bank[6][:, tlo:T] if e == 2 else bank[5][:, e * T + tlo:(e + 1) * T]
                            ins = mm(dst, lhs, w, start=j == 0, stop=j == 2)
                    ins.then_inc(S("head_sums"), 1)
                z_products(pe, 2)
                pe.wait_ge(S("ml_squares"), 1)
                for c in range(8):
                    hh = c // 2
                    ins = mm(bank[2 + hh // 2][:, hh % 2 * T:(hh % 2 + 1) * T], ones, vc[:, c, 0:T],
                             start=c % 2 == 0, stop=c % 2 == 1)
                ins.then_inc(S("ml_sums"), 1)
                pe.wait_ge(S("ml_inverse"), 1)
                b_re, b_im = (g2(n).rearrange("p (c n) -> p c n", c=4) for n in ("b_re", "b_im"))
                c_re, c_im = (g2(n).rearrange("p (s c) -> p s c", s=16) for n in ("c_re", "c_im"))

                def states(p):
                    pe.wait_ge(S("s_ready"), p + 1)
                    for s in range(2):
                        j = 2 * p + s
                        c, r = j // 4, 32 * (j % 4)
                        dst = bank[6 + c // 2][r:r + 32, c % 2 * T:(c % 2 + 1) * T]
                        mm(dst, c_re[:, j, :], s_out[:, 0, s, :], start=True, stop=False)
                        ins = mm(dst, c_im[:, j, :], s_out[:, 1, s, :], start=False, stop=True)
                    ins.then_inc(S("c_done"), 1)

                for p in range(PAIRS):
                    if p:
                        pe.wait_ge(S("bu_ready"), 4 * p)
                    for s in range(2):
                        j = 2 * p + s
                        c, r = j // 4, 32 * (j % 4)
                        for k, w in enumerate((b_re, b_im)):
                            ins = mm(bank[2 + 2 * s + k][:, 0:TT], w[r:r + 32, c, :], us[r:r + 32, c, :], start=True, stop=True)
                        if s == 0:
                            turn(pe, ins)
                    ins.then_inc(S("bu_done"), 1)
                    z_products(pe, 1)
                    if p:
                        states(p - 1)
                states(PAIRS - 1)
            pe_at.advance((4, 5, 6), 1, None)
            ev_at.advance((4, 5, 6), 1, None)

        a10 = Area(arena)
        glu, mixed, part = a10.take(4, T), a10.take(8, T), a10.take(4, T)
        assert a10.at <= a6.at
        y5 = us[:, :, M:TT]
        combos = ((5, 6, 7), (0, 1, 2), (3, 4, 5), (6, 7, 0))
        cycle = (1, 2, 3, 4, 5, 6, 7, 0)
        with nc.Block() as block:
            @block.sync
            def _(sp):
                load(sp, (7,))
                for slots in combos[1:]:
                    load(sp, slots)
                load(sp, cycle)
                load(sp, cycle)

            @block.tensor
            def _(pe):
                def gate(q, w, b, i):
                    for n in range(2):
                        for k in range(4):
                            mm = nc.tensor.matmul(b[:, n * T:(n + 1) * T], w[:, 4 * n + k, :], y5[:, k, :],
                                                  start=k == 0, stop=k == 3)
                    return mm

                def branches(q, w, b, i):
                    if q == 0:
                        return gate(q, w, b, i)
                    for k in range(KT):
                        mm = nc.tensor.matmul(b[:, 0:T], w[:, k, :], h_ml[:, k, :], start=k == 0, stop=k == KT - 1)
                    return mm

                def onto(q, w, b, i):
                    for k in range(KT):
                        mm = nc.tensor.matmul(b[:, 0:T], w[:, k, :], mixed[:, k, :], start=k == 0, stop=k == KT - 1)
                    return mm

                project(pe, (7, 4), (0, 1), 1, gate)
                pe.wait_ge(S("s5_gated"), 1)
                for n, slots in enumerate(combos):
                    project(pe, slots, ((2, 3, 4), (5, 6, 7))[n % 2], 1, branches)
                pe.wait_ge(S("mixed"), 4)
                project(pe, cycle, range(4), 1, onto)

            @block.scalar
            def _(act):
                def sigmoids(q, b, i):
                    for n in range(2):
                        ins = nc.scalar.activation(glu[:, 2 * q + n, :], b[:, n * T:(n + 1) * T], ACT.Sigmoid,
                                                   bias=col("ssm_b_glu_2", 2 * q + n))
                    return ins
                evacuate(act, (7, 4), (0, 1), 1, sigmoids)

            @block.vector
            def _(dve):
                v = nc.vector
                for b in range(2):
                    dve.wait_ge(drained[b], ev_at.banks[b] + 1)
                vec.tell(v.tensor_tensor(y5, y5, glu, ALU.mult), S("s5_gated"))
                for n, slots in enumerate(combos):
                    def mix(q, b, i):
                        if q == 0:
                            return v.tensor_tensor(part[:, 0:2, :], b[:, :].rearrange("p (c t) -> p c t", c=2),
                                                   gs_g[:, 2 * n:2 * n + 2, :], ALU.mult)
                        return v.tensor_tensor(part[:, 1 + q, :], b[:, 0:T], gm_g[:, 2 * n + q - 1, :], ALU.mult)
                    banks = ((2, 3, 4), (5, 6, 7))[n % 2]
                    evacuate(dve, slots, banks, 1, mix)
                    for b in banks:
                        dve.wait_ge(drained[b], ev_at.banks[b] + 1)
                    vec.tell(v.tensor_tensor(mixed[:, 2 * n:2 * n + 2, :], part[:, 0:2, :], part[:, 2:4, :], ALU.add),
                             S("mixed"), n + 1)
                evacuate(dve, cycle, range(4), 1, lambda q, b, i: v.tensor_tensor(
                    x[:, q, :], x[:, q, :], b[:, 0:T], ALU.add))
                dve.wait_ge(drained[3], ev_at.banks[3] + 1)

        rms_norm(lambda k: x[:, k, :], lambda k: h[:, k, 0:T], "norm2_g_2", RMS_EPS, Area(arena).take(KT, T))
        ge = Area(arena)
        G = ge.take(P, T)
        early = ge.take(EARLY, T)
        parts = Area(arena_parts, ge.at)
        h_high = parts.take(KT, T)
        h_low = h_parts[:, :, 0:T]
        ge.at = parts.at
        high_at = ge.at
        chosen = ge.take(3, T)
        ap_ = Area(arena)
        qp = ap_.take(16, T)
        sc = ap_.take(2, 16, P)
        work = ap_.take(T)
        sv, si = ap_.take(16, 16), ap_.take(16, 16)
        cand = ap_.take(8, T)
        cs, ci = ap_.take(8, 16), ap_.take(8, 16)
        which, which_f, hot = ap_.take(2, P), ap_.take(2, P), ap_.take(P, 16)
        picked = ap_.take(2, 3, P)
        tops, sums = ap_.take(8, 16), ap_.take(2, 8)
        si_u = ap_.take(16, 16).bitcast(U32)
        ci_u, which_u = ci.bitcast(U32), which.bitcast(U32)
        hot_a = x[:, 0:4, :].rearrange("p a t -> p (a t)").rearrange("p (b q n) -> p b q n", b=2, q=4)
        hot_b = x[:, 4:8, :].rearrange("p a t -> p (a t)").rearrange("p (b q n) -> p b q n", b=2, q=4)

        with nc.Block() as block:
            @block.sync
            def _(sp):
                load(sp, cycle)
                load(sp, (1, 2))
                load(sp, (3, 4, 5, 6, 7, 0))

            @block.tensor
            def _(pe):
                project(pe, cycle, range(4, 8), 2, channels(T))
                for b in range(4):
                    pe.wait_ge(drained[b], pe_at.banks[b] + 1)
                    for c in range(4):
                        k = 4 * (b % 2) + c
                        mm = nc.tensor.matmul(bank[b][:, c * P:(c + 1) * P], x[:, k, b // 2 * P:(b // 2 + 1) * P], ident,
                                              start=c == 0, stop=False)
                    mm.then_inc(S("seeded"), 1)
                for b in range(4, 8):
                    pe.wait_ge(drained[b], pe_at.banks[b] + 1)
                pe.wait_ge(full[1], 16 * (pe_at.rounds[1] + 1))
                pe.wait_ge(full[2], 16 * (pe_at.rounds[2] + 1))
                for tt in range(2):
                    for b in range(4):
                        if tt:
                            pe.wait_ge(S("scores_read"), b + 1)
                        for n in range(4 * b, 4 * b + 4):
                            o = n % 8 * P
                            mm = nc.tensor.matmul(bank[4 + b][:, n % 4 * P:(n % 4 + 1) * P], qp[:, n, tt * P:(tt + 1) * P],
                                                  ring[:, 1 + n // 8, o:o + P], start=True, stop=True)
                        mm.then_inc(S("scores_done"), 1)
                pe.wait_ge(S("scores_read"), 8)
                pe.sem_inc(used[1], 1)
                pe.sem_inc(used[2], 1)

            @block.scalar
            def _(act):
                evacuate(act, cycle, range(4, 8), 2, lambda q, b, i: nc.scalar.activation(
                    qp[:, bass.ds(i * 8 + q, 1), :].rearrange("p a t -> p (a t)"), b[:, 0:T], ACT.Copy))
                for n in range(8):
                    act.wait_ge(S("scores_done"), n + 1)
                    nc.scalar.activation(sc[:, n // 4, n % 4 * 4:n % 4 * 4 + 4, :], b3(4 + n % 4, P), ACT.Copy)\
                        .then_inc(S("scores_read"), 1)
            pe_at.advance((1, 2), 1, None)
            ev_at.advance((1, 2), 1, None)

        ER = (3, 4, 5, 6, 7, 0, 1, 2)
        PEER_BANKS = (4, 5, 6, 7)

        def act_products(q, w, b, i):
            for k in range(KT):
                mm = nc.tensor.matmul(b[:, 0:T], w[:, k, :], h[:, k, 0:T], start=k == 0, stop=k == KT - 1)
            return mm

        with nc.Block() as block:
            @block.sync
            def _(sp):
                load(sp, (1, 2))
                load(sp, ER)

            @block.tensor
            def _(pe):
                project(pe, ER, PEER_BANKS, 1, act_products)
                for b in PEER_BANKS[0:2]:
                    pe.wait_ge(drained[b], pe_at.banks[b] + 1)
                pe.wait_ge(S("picked"), 2)
                for tt in range(2):
                    for n in range(3):
                        mm = nc.tensor.transpose(bank[4 + tt][:, n * P:(n + 1) * P], picked[:, tt, n, :], ident)
                mm.then_inc(S("chosen_t"), 1)

            @block.scalar
            def _(act):
                evacuate(act, ER[0:7], PEER_BANKS, 1, lambda q, b, i: nc.scalar.activation(
                    early[:, q, :], b[:, 0:T], ACT.Gelu_apprx_tanh))
                act.wait_ge(used[ER[7]], ev_at.rounds[ER[7]] + 1)
                nc.scalar.activation(h_high, h[:, :, 0:T], ACT.Copy).then_inc(S("h_high"), 1)
                for tt in range(2):
                    act.wait_ge(S("soft_arg"), tt + 1)
                    nc.scalar.activation(tops, tops, ACT.Exp).then_inc(S("soft_exp"), 1)

            @block.gpsimd
            def _(pool):
                pool.wait_ge(S("h_high"), 1)
                nc.gpsimd.tensor_tensor(h_low, h[:, :, 0:T], h_high.bitcast(F32), ALU.subtract)\
                    .then_inc(S("h_split"), 1)
                pool.wait_ge(S("h_split"), 1)

            @block.vector
            def _(dve):
                v = nc.vector

                def top16(values, indices, src, buf):
                    vec.link(v.max(values[:, 0:8], src))
                    vec.link(v.max_index(indices[:, 0:8], values[:, 0:8], src))
                    vec.link(v.match_replace(buf, values[:, 0:8], src, -3e38))
                    vec.link(v.max(values[:, 8:16], buf))
                    vec.link(v.max_index(indices[:, 8:16], values[:, 8:16], buf))

                for tt in range(2):
                    for n in range(16):
                        top16(sv[:, n, :], si_u[:, n, :], sc[:, tt, n, :], work[:, 0:P])
                    vec.link(v.tensor_copy(si, si_u))
                    by_half = sv.rearrange("p (h s) k -> p h s k", s=2)
                    first_s = by_half[:, :, 0, :].unsqueeze(3).broadcast_to([P, 8, 16, 16])
                    second_s = by_half[:, :, 1, :].unsqueeze(2).broadcast_to([P, 8, 16, 16])
                    vec.link(v.tensor_tensor(cand.rearrange("p h (a b) -> p h a b", a=16), first_s, second_s, ALU.add))
                    for n in range(8):
                        top16(cs[:, n, :], ci_u[:, n, :], cand[:, n, :], work)
                    vec.tell(v.tensor_tensor(tops, cs, cs[:, :, 0:1].broadcast_to([P, 8, 16]), ALU.subtract),
                             S("soft_arg"), tt + 1)
                    flat = ci_u.rearrange("p h k -> p (h k)")
                    vec.link(v.tensor_scalar(which_u[:, 0, :], flat, 4, None, ALU.logical_shift_right))
                    vec.link(v.tensor_scalar(which_u[:, 1, :], flat, 15, None, ALU.bitwise_and))
                    vec.link(v.tensor_copy(which_f, which_u))
                    ki = si.rearrange("p (h s) k -> p h s k", s=2)
                    for s in range(2):
                        vec.link(v.tensor_tensor(hot, which_f[:, s, :].unsqueeze(2).broadcast_to([P, P, 16]),
                                                 iota[:, 0:16].unsqueeze(1).broadcast_to([P, P, 16]), ALU.is_equal))
                        hot4 = hot.rearrange("p (h k) a -> p h k a", h=8)
                        vec.link(v.tensor_tensor(hot4, hot4, ki[:, :, s, :].unsqueeze(2).broadcast_to([P, 8, 16, 16]),
                                                 ALU.mult))
                        vec.link(v.tensor_reduce(picked[:, tt, s, :], hot, AX, ALU.add))
                    dve.wait_ge(S("soft_exp"), tt + 1)
                    vec.link(v.tensor_reduce(sums[:, 0, :], tops, AX, ALU.add))
                    vec.link(v.reciprocal(sums[:, 1, :], sums[:, 0, :]))
                    vec.tell(v.tensor_tensor(picked[:, tt, 2, :].rearrange("p (h k) -> p h k", h=8), tops,
                                             sums[:, 1, :].unsqueeze(2).broadcast_to([P, 8, 16]), ALU.mult),
                             S("picked"), tt + 1)
                dve.wait_ge(S("chosen_t"), 1)
                for tt in range(2):
                    ins = v.tensor_copy(chosen[:, :, tt * P:(tt + 1) * P],
                                        bank[4 + tt][:, 0:3 * P].rearrange("p (n t) -> p n t", n=3))
                vec.link(ins)

        with nc.Block() as block:
            @block.vector
            def _(dve):
                v = nc.vector
                with dve.Fori(0, T // 8) as i:
                    for b in range(2):
                        dve.wait_ge(S("rows_free"), i * 2 + (b + 1))
                        for q in range(4):
                            t = i * 8 + (4 * b + q)

                            def at_t(n):
                                return chosen[:, n, bass.ds(t, 1)]
                            v.tensor_scalar(hot_a[:, b, q, :], iota, at_t(0), at_t(2), ALU.is_equal, ALU.mult)
                            ins = v.tensor_scalar(hot_b[:, b, q, :], iota, at_t(1), None, ALU.is_equal)
                        ins.then_inc(S("rows_ready"), 1)

            @block.tensor
            def _(pe):
                pe.sem_inc(S("rows_free"), 2)
                with pe.Fori(0, T // 8) as i:
                    for b in range(2):
                        pe.wait_ge(S("rows_ready"), i * 2 + (b + 1))
                        pe.wait_ge(S("gates_read"), i * 2 + (b + 1))
                        for q in range(4):
                            mm = nc.tensor.matmul(bank[4 + b][:, q * P:(q + 1) * P], hot_a[:, b, q, :], hot_b[:, b, q, :],
                                                  start=True, stop=True)
                        mm.then_inc(S("rows_free"), 1)

            @block.scalar
            def _(act):
                act.sem_inc(S("gates_read"), 2)
                with act.Fori(0, T // 8) as i:
                    for b in range(2):
                        act.wait_ge(S("rows_free"), i * 2 + (b + 3))
                        nc.scalar.activation(G[:, :, bass.ds(i * 8 + 4 * b, 4)],
                                             bank[4 + b][:, :].rearrange("p (q n) -> p n q", q=4), ACT.Copy)\
                            .then_inc(S("gates_read"), 1)

        high = Area(arena_parts, high_at).take(2, D)
        low = ring_parts
        gate_high, gate_low = x_parts[:, 0:4, :], x_parts[:, 4:8, :]
        rounds = (P - EARLY) // 8
        slot_base = {s: pe_at.rounds[s] for s in ER}
        bank_base = {b: pe_at.banks[b] - 2 for b in PEER_BANKS}
        HALF = D // 2

        def uses(m, i, ahead=0):
            return i * 2 + (slot_base[ER[m % 8]] + m // 8 + ahead)

        with nc.Block() as block:
            @block.sync
            def _(sp):
                load(sp, ER, 2 * rounds)

            @block.tensor
            def _(pe):
                mm = nc.tensor.matmul

                def experts(m, i, s):
                    slot, b = ER[m % 8], PEER_BANKS[s % 4]
                    pe.wait_ge(drained[b], i * 2 + (bank_base[b] + s // 4 + 3))
                    for k in range(KT):
                        if k % 4 == 0:
                            pe.wait_ge(S("low"), i * 32 + (2 * m + k // 4 + 1))
                        w = slice(k * P, (k + 1) * P)
                        mm(bank[b][:, 0:T], high[:, m % 2, w], h_high[:, k, :], start=k == 0, stop=False)
                        mm(bank[b][:, 0:T], high[:, m % 2, w], h_low[:, k, :], start=False, stop=False)
                        ins = mm(bank[b][:, 0:T], low[:, slot, w], h_high[:, k, :], start=False, stop=k == KT - 1)
                        if k == 3:
                            ins.then_inc(S("half_used"), 1)
                    ins.then_inc(used[slot], 1)

                def values(m, i, s, last_one=False):
                    slot = ER[m % 8]
                    pe.wait_ge(S("gated"), i * 8 + (s + 2))
                    for half in range(2):
                        pe.wait_ge(S("low"), i * 32 + (2 * m + half + 1))
                        w = slice(half * HALF, (half + 1) * HALF)
                        for tt in range(2):
                            b, t = bank[2 * tt + half][:, :], slice(tt * P, (tt + 1) * P)
                            mm(b, gate_high[:, s % 4, t], high[:, m % 2, w], start=False, stop=False)
                            mm(b, gate_high[:, s % 4, t], low[:, slot, w], start=False, stop=False)
                            ins = mm(b, gate_low[:, s % 4, t], high[:, m % 2, w], start=False, stop=last_one)
                        if half == 0:
                            ins.then_inc(S("half_used"), 1)
                    ins.then_inc(used[slot], 1)

                pe.sem_inc(S("half_used"), 2)
                with pe.Fori(0, rounds) as i:
                    for s in range(8):
                        experts(2 * s, i, s)
                        values(2 * s + 1, i, s)
                for s in range(8):
                    values(s, rounds, s, s == 7)

            @block.scalar
            def _(act):
                def split_high(m, i):
                    slot = ER[m % 8]
                    act.wait_ge(full[slot], i * 32 + 16 * (slot_base[slot] + m // 8 + 1))
                    act.wait_ge(S("half_used"), i * 16 + (m + 1))
                    nc.scalar.activation(high[:, m % 2, 0:HALF], ring[:, slot, 0:HALF], ACT.Copy).then_inc(S("high"), 1)
                    act.wait_ge(used[ER[(m - 2) % 8]], uses(m - 2, i, 1))
                    nc.scalar.activation(high[:, m % 2, HALF:D], ring[:, slot, HALF:D], ACT.Copy).then_inc(S("high"), 1)

                def gelu(s, i):
                    act.wait_ge(used[ER[(2 * s - 2) % 8]], uses(2 * s - 2, i, 1))
                    act.wait_ge(S("gated"), i * 8 + (s + 1))
                    b = PEER_BANKS[(s - 1) % 4]
                    nc.scalar.activation(early[:, (s - 1) % 8, :], bank[b][:, 0:T], ACT.Gelu_apprx_tanh)\
                        .then_inc(drained[b], 1)

                with act.Fori(0, rounds) as i:
                    for s in range(8):
                        split_high(2 * s, i)
                        gelu(s, i)
                        split_high(2 * s + 1, i)
                gelu(0, rounds)
                for m in range(8):
                    split_high(m, rounds)

            @block.vector
            def _(dve):
                def split_low(m, i):
                    for half in range(2):
                        dve.wait_ge(S("high"), i * 32 + (2 * m + half + 1))
                        w = slice(half * HALF, (half + 1) * HALF)
                        nc.vector.tensor_tensor(low[:, ER[m % 8], w], ring[:, ER[m % 8], w],
                                                high[:, m % 2, w].bitcast(F32), ALU.subtract).then_inc(S("low"), 1)

                with dve.Fori(0, rounds) as i:
                    for m in range(16):
                        split_low(m, i)
                for m in range(8):
                    split_low(m, rounds)

            @block.gpsimd
            def _(pool):
                p = nc.gpsimd
                pool.sem_inc(S("gated"), 1)

                def gate(s, i, m):
                    b = PEER_BANKS[s % 4]
                    pool.wait_ge(drained[b], i * 2 + (bank_base[b] + s // 4 + 2))
                    pool.wait_ge(used[ER[m % 8]], uses(m, i, 1))
                    e = early[:, s, :]
                    j = i * 8 + s
                    g = G[:, j, :] if isinstance(j, int) else G[:, bass.ds(j, 1), :].rearrange("p a t -> p (a t)")
                    p.tensor_tensor(e, e, g, ALU.mult).then_inc(S("gate_step"), 1)
                    pool.wait_ge(S("gate_step"), i * 16 + (2 * s + 1))
                    p.tensor_tensor(gate_high[:, s % 4, :].rearrange("p (a t) -> p a t", a=2),
                                    e.rearrange("p (a t) -> p a t", a=2),
                                    ones.unsqueeze(1).broadcast_to([P, 2, P]), ALU.mult).then_inc(S("gate_step"), 1)
                    pool.wait_ge(S("gate_step"), i * 16 + (2 * s + 2))
                    p.tensor_tensor(gate_low[:, s % 4, :], e, gate_high[:, s % 4, :].bitcast(F32), ALU.subtract)\
                        .then_inc(S("gated"), 1)

                with pool.Fori(0, rounds) as i:
                    for s in range(8):
                        gate(s, i, 2 * s + 1 - 8)
                for s in range(8):
                    gate(s, rounds, s - 4 if s >= 4 else 2 * s - 7)

        a_end = Area(arena)
        square, result, stat = a_end.take(4, 512), a_end.take(4, 512), a_end.take(2, 4)
        last_g = a_end.take(D)
        with nc.Block() as block:
            @block.scalar
            def _(act):
                act.dma_start(last_g, last).then_inc(S("last_in"), 16)
                for b in range(4):
                    nc.scalar.activation(square[:, b, :], bank[b][:, :], ACT.Square).then_inc(S("last_squares"), 1)
                act.wait_ge(S("last_mean"), 1)
                nc.scalar.activation(stat[:, :, 1:2], stat[:, :, 1:2], ACT.Sqrt).then_inc(S("last_root"), 1)

            @block.vector
            def _(dve):
                v = nc.vector
                dve.wait_ge(S("last_squares"), 4)
                vec.link(v.tensor_reduce(stat[:, :, 0:1], square.rearrange("p (t c) n -> p t (c n)", t=2), AX, ALU.add))
                vec.link(v.tensor_scalar(stat[:, :, 1:2], stat[:, :, 0:1], 1.0 / D, RMS_EPS, ALU.mult, ALU.add))
                vec.tell(v.reciprocal(stat[:, :, 1:2], stat[:, :, 1:2]), S("last_mean"))
                dve.wait_ge(S("last_root"), 1)
                dve.wait_ge(S("last_in"), 16)
                for b in range(4):
                    c = b % 2 * 512
                    v.scalar_tensor_tensor(result[:, b, :], bank[b][:, :], stat[:, b // 2, 1:2], last_g[:, c:c + 512],
                                           ALU.mult, ALU.mult).then_inc(S("result"), 1)

            @block.sync
            def _(sp):
                for b in range(4):
                    c = b % 2 * 512
                    sp.wait_ge(S("result"), b + 1)
                    sp.dma_start(out[b // 2 * P:(b // 2 + 1) * P, c:c + 512], result[:, b, :]).then_inc(S("written"), 16)
                sp.wait_ge(S("written"), 64)


def _blocks(w):
    k, n = w.shape
    return w.reshape(k // P, P, n // P, P).transpose(2, 1, 0, 3).reshape(n // P, P, k)


def _columns(v):
    return v.reshape(-1, P).T


def lay_out(a):
    import numpy as np

    f32 = np.float32
    a = {k: np.asarray(v) for k, v in a.items()}
    w_in, w_in2 = a["w_in"][0], a["w_in_2"][0]
    sc, sb, rw, sg, gate = 0, 768, 1536, 2560, 3072
    order = [w_in[:, rw:rw + 1024], w_in[:, sc:sc + 768], w_in[:, sb:sb + 512], w_in[:, sg:sg + 256],
             w_in[:, sb + 512:sb + 768], w_in[:, sg + 256:sg + 512], w_in[:, gate:]]
    parts = [_blocks(w) for w in order]
    outs = np.stack([a[n][0] for n in ("sc_out", "sb_out", "rw_out", "sg_out")])
    parts.append(outs.reshape(4, 2, P, KT, P).transpose(3, 2, 0, 1, 4).reshape(KT, P, D))
    parts.append(_blocks(a["w_o"][0]))
    up = _blocks(a["w_up"][0])
    ffn = np.stack([up[:FT], up[FT:], a["w_down"][0].reshape(FT, P, D)], 1)
    parts.append(ffn.reshape(3 * FT, P, D))
    parts.append(_blocks(w_in2[:, :1536]))
    for n in ("ml_wq_2", "ml_wk_2", "ml_wv_2"):
        w = a[n][0]
        m = np.zeros((D // 4, 4, D // 4, 4), f32)
        r = np.arange(D // 4)
        m[r, :, r, :] = w
        m = m.reshape(KT, P, KT, P)
        parts.append(np.stack([m[k, :, k, :] for k in range(KT)], 1).reshape(1, P, D))
    parts.append(_blocks(w_in2[:, 1536:]))
    glu = a["ssm_w_glu_2"][0].reshape(4, P, 2, 2, P).transpose(2, 1, 3, 0, 4).reshape(2, P, D)
    parts.append(glu)
    ssm = a["w_ssm_out_2"][0].reshape(4, P, 4, 2, P).transpose(2, 1, 3, 0, 4).reshape(4, P, D)
    ml, wo = _blocks(a["w_ml_out_2"][0]), _blocks(a["w_out_2"][0])
    for n in range(4):
        parts += [ssm[n:n + 1], ml[2 * n:2 * n + 2]]
    parts.append(wo)
    parts.append(_blocks(a["peer_w_q_2"][0]))
    keys = a["peer_sub_keys_2"][0].reshape(16, P, P).transpose(2, 0, 1).reshape(P, 2, D)
    parts.append(keys.transpose(1, 0, 2))
    u = a["peer_u_2"][0].reshape(P, P, KT, P).transpose(1, 3, 2, 0).reshape(P, P, D)
    v = a["peer_v_2"][0].reshape(P, P, D).transpose(1, 0, 2)
    parts += [u[:EARLY], np.stack([u[EARLY:], v[:-EARLY]], 1).reshape(-1, P, D), v[-EARLY:]]
    stream = np.concatenate(parts)

    cols = {}
    for n in ("mix_norm_g", "gate_b", "rw_mu", "rw_w0", "rw_a0", "rw_k_k", "rw_k_a", "rw_gn_g", "rw_gn_b",
              "ffn_norm_g", "norm1_g_2", "ssm_d_2", "ssm_b_glu_2", "ml_conv_b_2", "ml_norm_g_2", "ml_skip_2",
              "norm2_g_2"):
        cols[n] = _columns(a[n][0])
    cols["final_norm_g"] = _columns(a["final_norm_g"])
    cols["rw_r_k"] = _columns(a["rw_r_k"][0].reshape(-1))
    for n in ("sc_conv_w", "ffn_conv_w", "ml_conv_w_2"):
        cols[n] = np.concatenate([_columns(w) for w in a[n][0]], 1)
    cols["ssm_a_re_2"] = _columns(a["ssm_a_re_2"][0].reshape(-1))
    cols["ssm_a_im_2"] = _columns(a["ssm_a_im_2"][0].reshape(-1))
    cols["ssm_log_dt_2"] = _columns(np.repeat(a["ssm_log_dt_2"][0], 64))
    b_if = np.zeros((P, 2), f32)
    b_if[:4, 0], b_if[:4, 1] = a["ml_b_if_2"][0][:4], a["ml_b_if_2"][0][4:]
    cols["ml_b_if_2"] = b_if
    assert {k: v.shape[1] for k, v in cols.items()} == COLS
    cols = np.concatenate([cols[k] for k in COLS], 1)

    lora = np.concatenate([np.concatenate([a["rw_w2"][0], a["rw_a2"][0]], 0), a["rw_g2"][0]], 1)
    ln_rows = np.broadcast_to(np.concatenate([a["sg_ln_g"][0], a["sg_ln_b"][0]])[None], (P, 512))
    sgw = a["sg_w"][0].transpose(2, 0, 1).reshape(P, 512)
    sgb = np.tile(np.repeat(a["sg_b"][0], 64, axis=0).reshape(2, P, 1, P), (1, 1, 2, 1)).transpose(1, 0, 2, 3)
    i = np.arange(P)
    s_, t_ = i[:, None], i[None, :]
    t2 = np.arange(T)[None, :]
    same = (s_ // 64) == (t_ // 64)
    masks = [same, same & (s_ < t_), same & (s_ <= t_)]
    levels = []
    for w in (1, 2, 4, 8, 16, 32):
        m = (s_ // (2 * w) == t_ // (2 * w)) & (s_ // w % 2 == 1) & (t_ // w % 2 == 0)
        levels.append(m)
    masks += levels[:1] + [m.T for m in levels]
    masks += [s_ > t_, s_ <= t_, s_ < t2, s_ < t2[:, P:] - P, (t2 % 64 != 0) & (s_ >= 0)]
    eye2 = np.concatenate([np.eye(64), np.eye(64)], 0)
    first = [lora, ln_rows, sgw, sgb.reshape(P, 512)] + [m.astype(f32) for m in masks] + [eye2]
    first = np.concatenate([x.astype(f32, copy=False) for x in first], 1)
    assert first.shape[1] == sum(FIRST.values())

    bmats, cmats = [], []
    for n in ("ssm_b_re_2", "ssm_b_im_2"):
        b = a[n][0].reshape(4, 4, 2, 64, 16)
        m = np.zeros((4, 2, 16, 4, 2, 64), f32)
        for g in range(2):
            m[:, g, :, :, g, :] = b[:, :, g].transpose(1, 3, 0, 2)
        bmats.append(m.reshape(P, 512))
    for n in ("ssm_c_re_2", "ssm_c_im_2"):
        c = a[n][0].reshape(16, 2, 16, 64)
        m = np.zeros((2, 64, 16, 2, 16), f32)
        for g in range(2):
            m[g, :, :, g, :] = c[:, g].transpose(2, 0, 1)
        cmats.append(m.reshape(P, 512))
    wif = a["ml_w_if_2"][0].reshape(24, P, 8).transpose(1, 0, 2).reshape(P, 192)
    neg = [np.where(s_ <= t2, 0.0, -1e30), np.where(s_ + P <= t2, 0.0, -1e30)]
    sel = np.zeros((P, 4, P))
    sel[i[:4], i[:4]] = 1
    second = np.concatenate([x.astype(f32, copy=False) for x in bmats + cmats + [wif] + neg + [sel.reshape(P, 512)]], 1)
    assert second.shape[1] == sum(SECOND.values())
    last = np.broadcast_to(a["final_norm_g_2"][None], (P, D))
    keep = np.concatenate([np.eye(P), np.ones((P, P)), np.broadcast_to(i[None], (P, P))], 1).astype(f32)
    return {
        "stream": stream, "x_t": a["x"][0].T.reshape(KT, P, T).transpose(1, 0, 2),
        "meta_t": a["meta_tokens_2"].T.reshape(KT, P, M).transpose(1, 0, 2),
        "cols": cols, "first": first, "second": second, "last": last, "keep": keep,
    }


def kernel(**inputs):
    import numpy as np
    import concourse.bacc as bacc
    from concourse.bass_utils import run_bass_kernel_spmd

    arrays = {k: np.ascontiguousarray(v) for k, v in lay_out(inputs).items()}
    nc = bacc.Bacc("TRN2", target_bir_lowering=False, num_devices=1)
    args = {n: nc.dram_tensor(n, a.shape, mybir.dt.from_np(a.dtype), kind="ExternalInput").ap()
            for n, a in arrays.items()}
    out = nc.dram_tensor("out", (T, D), F32, kind="ExternalOutput").ap()
    build(nc, out, **args)
    r = run_bass_kernel_spmd(nc, [arrays], core_ids=[0])
    return r.results[0]["out"].reshape(1, T, D)
```

```python
from contextlib import ExitStack

import concourse.bass as bass
from concourse import mybir

P = 128
T = 256
M = 16
TT = T + M
D = 1024
KT = D // P
FT = 2816 // P
EARLY = 8
ARENA_PARTS = (0, 5888, 17152, (P + EARLY) * T)
SLOTS = 8
RMS_EPS = 1e-6
LN_EPS = 1e-5
GN_EPS = 64e-5
DECAY_SCALE = 0.6065306597126334
TWO_PI = 6.283185307179586

ALU = mybir.AluOpType
ACT = mybir.ActivationFunctionType
F32 = mybir.dt.float32
F32R = mybir.dt.float32r
U32 = mybir.dt.uint32
AX = mybir.AxisListType.X

COLS = {"mix_norm_g": 8, "gate_b": 32, "rw_mu": 8, "rw_w0": 2, "rw_a0": 2, "rw_k_k": 2, "rw_k_a": 2,
        "rw_gn_g": 2, "rw_gn_b": 2, "ffn_norm_g": 8, "norm1_g_2": 8, "ssm_d_2": 4, "ssm_b_glu_2": 4,
        "ml_conv_b_2": 8, "ml_norm_g_2": 8, "ml_skip_2": 8, "norm2_g_2": 8, "final_norm_g": 8, "rw_r_k": 2,
        "sc_conv_w": 6, "ffn_conv_w": 3 * 44, "ml_conv_w_2": 32, "ssm_a_re_2": 16, "ssm_a_im_2": 16,
        "ssm_log_dt_2": 16, "ml_b_if_2": 2}
FIRST = {"lora": 512, "ln_rows": 512, "sgw": 512, "sgb": 512, "same": P, "upper": P, "upper_eq": P,
         "level0": P, "levels_t": 6 * P, "after": P, "causal": P, "sb_mask0": T, "sb_mask1": P, "carry": T,
         "eye2": 64}
SECOND = {"b_re": 512, "b_im": 512, "c_re": 512, "c_im": 512, "w_if": 192, "neg0": T, "neg1": T, "sel": 512}


def offsets(sizes):
    out, at = {}, 0
    for name, n in sizes.items():
        out[name] = at
        at += n
    return out, at


class Area:

    def __init__(self, tensor, at=0):
        self.tensor, self.at = tensor, at

    def take(self, *dims):
        n = 1
        for d in dims:
            n *= d
        v = self.tensor[:, self.at:self.at + n]
        self.at += n
        assert self.at <= self.tensor.shape[1], self.at
        if len(dims) == 2:
            v = v.rearrange("p (a b) -> p a b", a=dims[0])
        if len(dims) == 3:
            v = v.rearrange("p (a b c) -> p a b c", a=dims[0], b=dims[1])
        return v


class Ring:

    def __init__(self):
        self.rounds = [0] * SLOTS
        self.block = 0


class Own:

    def __init__(self, eng, steps):
        self.eng, self.steps, self.n = eng, steps, 0

    def link(self, ins):
        self.n += 1
        ins.then_inc(self.steps, 1)
        self.eng.wait_ge(self.steps, self.n)

    def tell(self, ins, sem, value=1):
        ins.then_inc(sem, 1)
        self.eng.wait_ge(sem, value)


def build(nc, out, stream, x_t, meta_t, cols, first, second, last, keep):
    with ExitStack() as ctx:
        sems = {}

        def S(name):
            if name not in sems:
                sems[name] = ctx.enter_context(nc.semaphore(name))
            return sems[name]

        def sb(name, shape, dt=F32):
            return ctx.enter_context(nc.sbuf_tensor(name, shape, dt))

        def split_place(name, shape, starts=(0,)):
            with nc.sbuf_tensor(name, shape, F32) as whole:
                pass
            if len(starts) == 1:
                return whole, ctx.enter_context(nc.sbuf_tensor(name + "_parts", shape, F32R))
            ends = list(starts[1:]) + [shape[1]]
            return whole, {a: ctx.enter_context(nc.sbuf_tensor(f"{name}_parts{a}", [shape[0], b - a], F32R))
                           for a, b in zip(starts, ends)}

        ring, ring_parts = split_place("ring", [P, SLOTS, D])
        par = sb("par", [P, sum(COLS.values())])
        cst = sb("cst", [P, 3 * P])
        x, x_parts = split_place("x", [P, KT, T])
        h, h_parts = split_place("h", [P, KT, TT])
        scale = sb("scale", [P, TT])
        arena, arena_parts = split_place("arena", [P, 38912], ARENA_PARTS)
        bank = [ctx.enter_context(nc.psum_tensor(f"bank{i}", [P, 512], F32)) for i in range(8)]
        ident, ones, iota = cst[:, 0:P], cst[:, P:2 * P], cst[:, 2 * P:3 * P]
        at, _ = offsets(COLS)

        def col(name, i):
            return par[:, at[name] + i:at[name] + i + 1]

        full = [S(f"slot_full{s}") for s in range(SLOTS)]
        used = [S(f"slot_used{s}") for s in range(SLOTS)]
        drained = [S(f"bank_free{b}") for b in range(8)]
        fill = Ring()
        vec, sca, poo = Own(nc.vector, S("vector_step")), Own(nc.scalar, S("scalar_step")), Own(nc.gpsimd, S("pool_step"))

        def load(sp, slots, rounds=1):
            n, base = len(slots), fill.block

            def one(i):
                for q, s in enumerate(slots):
                    sp.wait_ge(used[s], fill.rounds[s] + i) if fill.rounds[s] else None
                    src = stream[bass.ds(base + i * n + q, 1)].rearrange("a p n -> (a p) n")
                    sp.dma_start(ring[:, s, :], src).then_inc(full[s], 16)

            if rounds == 1:
                one(0)
            else:
                assert all(fill.rounds[s] for s in slots)
                with sp.Fori(0, rounds) as i:
                    one(i)
            for s in slots:
                fill.rounds[s] += rounds
            fill.block += n * rounds

        class Tiles:

            def __init__(self):
                self.rounds = [0] * SLOTS
                self.banks = [0] * 8

            def advance(self, slots, rounds, banks):
                for q, s in enumerate(slots):
                    self.rounds[s] += rounds
                    if banks:
                        self.banks[banks[q % len(banks)]] += rounds

        pe_at, ev_at = Tiles(), Tiles()

        def use_of(banks, q, n):
            b = banks[q % len(banks)]
            mine = [r for r in range(n) if banks[r % len(banks)] == b]
            return b, len(mine), mine.index(q)

        def project(pe, slots, banks, rounds, mats):
            def one(i):
                for q, s in enumerate(slots):
                    b, per, before = use_of(banks, q, len(slots))
                    pe.wait_ge(full[s], (i + pe_at.rounds[s] + 1) * 16)
                    pe.wait_ge(drained[b], i * per + pe_at.banks[b] + before + 1)
                    mats(q, ring[:, s, :].rearrange("p (k n) -> p k n", n=P), bank[b], i).then_inc(used[s], 1)

            if rounds == 1:
                one(0)
            else:
                with pe.Fori(0, rounds) as i:
                    one(i)
            pe_at.advance(slots, rounds, banks)

        def evacuate(eng, slots, banks, rounds, take):
            def one(i):
                for q, s in enumerate(slots):
                    b, _, _ = use_of(banks, q, len(slots))
                    eng.wait_ge(used[s], i + ev_at.rounds[s] + 1)
                    take(q, bank[b], i).then_inc(drained[b], 1)

            if rounds == 1:
                one(0)
            else:
                with eng.Fori(0, rounds) as i:
                    one(i)
            ev_at.advance(slots, rounds, banks)

        def channels(width, lo=0):
            def mats(q, w, b, i):
                for k in range(KT):
                    mm = nc.tensor.matmul(b[:, 0:width], w[:, k, :], h[:, k, lo:lo + width],
                                          start=k == 0, stop=k == KT - 1)
                return mm
            return mats

        def tokens(q, w, b, i):
            for tt in range(2):
                for k in range(KT):
                    mm = nc.tensor.matmul(b[:, tt * P:(tt + 1) * P], h[:, k, tt * P:(tt + 1) * P], w[:, k, :],
                                          start=k == 0, stop=k == KT - 1)
            return mm

        normed = {"n": 0}

        def rms_norm(src, dst, gain, eps, squares, width=T, beside=None):
            n = normed["n"]
            normed["n"] += 1
            sq, total, mean, root = S("norm_squares"), S("norm_total"), S("norm_mean"), S("norm_root")
            with nc.Block() as block:
                @block.scalar
                def _(act):
                    for k in range(KT):
                        nc.scalar.activation(squares[:, k, 0:width], src(k), ACT.Square).then_inc(sq, 1)
                    if beside:
                        beside[0](act)
                    act.wait_ge(mean, n + 1)
                    nc.scalar.activation(scale[:, 0:width], scale[:, 0:width], ACT.Sqrt).then_inc(root, 1)

                @block.tensor
                def _(pe):
                    for k in range(KT):
                        pe.wait_ge(sq, n * KT + k + 1)
                        mm = nc.tensor.matmul(bank[7][:, 0:width], ones, squares[:, k, 0:width],
                                              start=k == 0, stop=k == KT - 1)
                    mm.then_inc(total, 1)

                @block.vector
                def _(dve):
                    if beside:
                        beside[1](dve)
                    dve.wait_ge(total, n + 1)
                    vec.link(nc.vector.tensor_scalar(scale[:, 0:width], bank[7][:, 0:width], 1.0 / D, eps,
                                                     ALU.mult, ALU.add))
                    vec.tell(nc.vector.reciprocal(scale[:, 0:width], scale[:, 0:width]), mean, n + 1)
                    dve.wait_ge(root, n + 1)
                    for k in range(KT):
                        last_one = nc.vector.scalar_tensor_tensor(dst(k), src(k), col(gain, k), scale[:, 0:width],
                                                                  ALU.mult, ALU.mult)
                    vec.link(last_one)

        a1 = Area(arena)
        z = a1.take(20, T)
        v_sb, v_sg = a1.take(2, T), a1.take(2, T)
        gates = a1.take(32, T)
        f_at, f_size = offsets(FIRST)
        fst = a1.take(f_size)
        y = a1.take(8, T)
        scratch_at = a1.at
        squares = Area(arena, scratch_at).take(KT, TT)

        def f(name, n=None):
            return fst[:, f_at[name]:f_at[name] + (n or FIRST[name])]

        with nc.Block() as block:
            @block.sync
            def _(sp):
                sp.dma_start(x[:], x_t).then_inc(S("inputs_in"), 16)
                load(sp, range(SLOTS))

            @block.scalar
            def _(act):
                act.dma_start(cst[:], keep).then_inc(S("inputs_in"), 16)
                act.dma_start(par[:], cols).then_inc(S("inputs_in"), 16)
                act.dma_start(fst, first).then_inc(S("inputs_in"), 16)
                act.wait_ge(S("inputs_in"), 64)

            @block.vector
            def _(dve):
                for b in range(8):
                    dve.sem_inc(drained[b], 1)

        rms_norm(lambda k: x[:, k, :], lambda k: h[:, k, 0:T], "mix_norm_g", RMS_EPS, squares)

        with nc.Block() as block:
            @block.sync
            def _(sp):
                load(sp, range(SLOTS), 2)
                load(sp, range(4))

            @block.tensor
            def _(pe):
                project(pe, range(8), range(4), 2, channels(T))
                project(pe, range(4), range(4), 1, channels(T))
                project(pe, range(4, 8), range(4), 1, tokens)

            @block.scalar
            def _(act):
                evacuate(act, range(8), range(4), 2, lambda q, b, i: nc.scalar.activation(
                    z[:, bass.ds(i * 8 + q, 1), :].rearrange("p a t -> p (a t)"), b[:, 0:T], ACT.Copy))
                evacuate(act, range(4), range(4), 1, lambda q, b, i: nc.scalar.activation(
                    z[:, 16 + q, :], b[:, 0:T], ACT.Copy))
                evacuate(act, range(4, 8), range(4), 1, lambda q, b, i: nc.scalar.activation(
                    (v_sb if q < 2 else v_sg)[:, :, q % 2 * P:(q % 2 + 1) * P],
                    b[:, 0:T].rearrange("p (a n) -> p a n", a=2), ACT.Copy))

        a2 = Area(arena, scratch_at)
        shift = a2.take(8, T)
        a_t, b_t, k_t, r_t = (shift[:, 2 * i:2 * i + 2, :] for i in range(4))
        lora_h = a2.take(T)
        w_sig, cum, d_inv, d_prev, kk, kk2, kmod, a_sig, decay, g_rw, bonus = (a2.take(2, T) for _ in range(11))
        tm = a2.take(4, 2, T)
        pairs_at = a2.at
        X, XT, Z, NT, MT, MTak, MTrb, MTrk = (a2.take(8, P) for _ in range(8))
        a3 = Area(arena, pairs_at)
        sb_l, sb_b, sb_k = a3.take(1536), a3.take(1536), a3.take(1536)
        sg_d, sg_q, sg_st = a3.take(2, T), a3.take(2, T), a3.take(8)
        sg_wt = a3.take(4, P)
        a4 = Area(arena, scratch_at + 2048 + T)
        AM, GH = a4.take(8, P), a4.take(8, P)
        n0, phi = a4.take(8, 64), a4.take(8, 64)
        assert a4.at <= scratch_at + 2048 + T + 7 * 512
        rp, y0, yd2, state, sc_c, sc_t = X[:, 0:4, :], X[:, 4:8, :], Z[:, 0:4, :], NT[:, 0, :], y[:, 6:8, :], Z
        rp, y0, yd2 = (v.rearrange("p a b -> p (a b)").rearrange("p (c t) -> p c t", c=2) for v in (rp, y0, yd2))
        st2 = NT.rearrange("p a b -> p (a b)")[:, 0:256].rearrange("p (n c v) -> p n c v", n=2, c=2)
        stp = NT.rearrange("p a b -> p (a b)")[:, 256:384].rearrange("p (c v) -> p c v", c=2)
        B3 = {"p": P, "h": 4}
        r_z, k_z, v_z, g_z = z[:, 0:2, :], z[:, 2:4, :], z[:, 4:6, :], z[:, 7, :]
        q_z, kk_z, u_z = z[:, 14:16, :], z[:, 16:18, :], z[:, 18:20, :]
        LEVELS = 5
        turns = {"n": 0}
        gate_n = {"pe": 0, "act": 0}

        def turn(pe, ins):
            turns["n"] += 1
            ins.then_inc(S("tensor_turn"), 1)
            pe.wait_ge(S("tensor_turn"), turns["n"])

        def four(m):
            return m.unsqueeze(1).broadcast_to([P, 4, m.shape[1]])

        def eight(m):
            return m.unsqueeze(1).broadcast_to([P, 8, m.shape[1]])

        def b3(b, w=T):
            return bank[b][:, :].rearrange("p (c t) -> p c t", t=w)

        def gate_products(pe, n):
            for _ in range(n):
                s = gate_n["pe"] % 4
                project(pe, [s], [s % 2], 1, channels(T))
                gate_n["pe"] += 1

        def gate_reads(act, n):
            for _ in range(n):
                g = gate_n["act"]
                evacuate(act, [g % 4], [g % 2], 1, lambda q, b, i: nc.scalar.activation(
                    gates[:, g, :], b[:, 0:T], ACT.Identity, bias=col("gate_b", g)))
                gate_n["act"] += 1

        with nc.Block() as block:
            @block.sync
            def _(sp):
                load(sp, range(4), 7)
                load(sp, range(4, 8))

            @block.gpsimd
            def _(pool):
                g = nc.gpsimd
                for c in range(2):
                    cx, acc, tap = sc_c[:, c, :], y[:, c, :], y[:, 2 + c, :]
                    poo.link(g.tensor_tensor(cx, z[:, 10 + c, :], z[:, 12 + c, :], ALU.mult))
                    poo.link(g.tensor_scalar(acc, cx, col("sc_conv_w", 4 + c), None, ALU.mult))
                    for back in (1, 2):
                        poo.link(g.tensor_scalar(tap, cx, col("sc_conv_w", 2 * (2 - back) + c), None, ALU.mult))
                        poo.link(g.tensor_tensor(acc[:, back:T], acc[:, back:T], tap[:, 0:T - back], ALU.add))
                    poo.link(g.tensor_tensor(acc, acc, z[:, 8 + c, :], ALU.mult))
                poo.eng.sem_inc(S("short_conv"), 1)

            def grow(dve, v, lev):
                dve.wait_ge(S("level_x"), lev)
                for half in range(2):
                    q4 = slice(4 * half, 4 * half + 4)
                    if lev < LEVELS:
                        vec.link(v.tensor_tensor(X[:, q4, :], X[:, q4, :], b3(4 + half, P), ALU.add))
                    ins = v.tensor_tensor(XT[:, q4, :], XT[:, q4, :], b3(6 + half, P), ALU.add)
                    vec.link(ins) if half == 0 else vec.tell(ins, S("level_grown"), lev)

            @block.vector
            def _(dve):
                v = nc.vector
                vec.link(v.tensor_tensor(shift[:, :, 1:T], z[:, 0:8, 0:T - 1], z[:, 0:8, 1:T], ALU.subtract))
                vec.link(v.tensor_scalar(shift[:, :, 0:1], z[:, 0:8, 0:1], -1.0, None, ALU.mult))
                for c in range(8):
                    ins = v.scalar_tensor_tensor(z[:, c, :], shift[:, c, :], col("rw_mu", c), z[:, c, :],
                                                 ALU.mult, ALU.add)
                vec.tell(ins, S("rw_mixed"))
                for c in range(2):
                    vec.link(v.tensor_scalar(kk[:, c, :], k_z[:, c, :], col("rw_k_k", c), None, ALU.mult))
                vec.tell(v.tensor_tensor(kk2, kk, kk, ALU.mult), S("kk_squares"))

                dve.wait_ge(S("sg_v"), 1)
                mean, rstd = sg_st[:, 0:2], sg_st[:, 2:4]
                vec.link(v.tensor_tensor(sg_wt, f("sgw").rearrange("p (g t) -> p g t", g=4), four(f("causal")), ALU.mult))
                vec.link(v.tensor_reduce(mean, v_sg, AX, ALU.add))
                vec.link(v.tensor_scalar(mean, mean, 1.0 / T, None, ALU.mult))
                for tt in range(2):
                    vec.link(v.tensor_scalar(sg_d[:, tt, :], v_sg[:, tt, :], mean[:, tt:tt + 1], None, ALU.subtract))
                vec.link(v.tensor_tensor(sg_q, sg_d, sg_d, ALU.mult))
                vec.link(v.tensor_reduce(rstd, sg_q, AX, ALU.add))
                vec.link(v.tensor_scalar(rstd, rstd, 1.0 / T, LN_EPS, ALU.mult, ALU.add))
                vec.tell(v.reciprocal(rstd, rstd), S("sg_var"))

                dve.wait_ge(S("sb_logs"), 1)
                parts = [(3, 0), (4, 512), (5, 1024)]
                for b, o in parts:
                    vec.link(v.tensor_scalar(sb_b[:, o:o + 512], bank[b][:, :], 0.125, 0.0, ALU.mult, ALU.min))
                vec.link(v.tensor_tensor(sb_b, sb_b, sb_l, ALU.subtract))
                for b, o in parts:
                    vec.link(v.scalar_tensor_tensor(sb_k[:, o:o + 512], bank[b][:, :], -0.125, sb_b[:, o:o + 512],
                                                    ALU.mult, ALU.add))
                halves = [(sb_k[:, 0:1024].rearrange("p (h t) -> p h t", h=4), four(f("sb_mask0"))),
                          (sb_k[:, 1024:1536].rearrange("p (h t) -> p h t", h=4), four(f("sb_mask1")))]
                vec.link(v.tensor_tensor(halves[0][0], halves[0][0], halves[0][1], ALU.mult))
                vec.tell(v.tensor_tensor(halves[1][0], halves[1][0], halves[1][1], ALU.mult), S("sb_keep"))

                dve.wait_ge(S("rw_sigmoids"), 1)
                for c in range(2):
                    vec.link(v.tensor_tensor_scan(cum[:, c, :], f("carry"), w_sig[:, c, :], 0.0, ALU.mult, ALU.add))
                vec.tell(v.tensor_tensor(d_prev, cum, w_sig, ALU.subtract), S("rw_cum"))
                for c in range(2):
                    vec.link(v.tensor_scalar(kmod[:, c, :], a_sig[:, c, :], -1.0, col("rw_k_a", c), ALU.add, ALU.mult))
                vec.link(v.scalar_tensor_tensor(kmod, kmod, 1.0, k_z, ALU.add, ALU.mult))
                dve.wait_ge(S("kk_root"), 1)
                vec.link(v.tensor_scalar(kk2, kk2, 1e-12, None, ALU.max))
                vec.link(v.reciprocal(kk2, kk2))
                vec.link(v.tensor_tensor(kk, kk, kk2, ALU.mult))
                for c in range(2):
                    ins = v.scalar_tensor_tensor(kk2[:, c, :], r_z[:, c, :], col("rw_r_k", c), kmod[:, c, :],
                                                 ALU.mult, ALU.mult)
                vec.tell(ins, S("rw_rk"))
                dve.wait_ge(S("rw_decays"), 1)
                vec.link(v.scalar_tensor_tensor(a_t, kk, -1.0, d_prev, ALU.mult, ALU.mult))
                vec.link(v.tensor_tensor(kk, kk, a_sig, ALU.mult))
                vec.link(v.tensor_tensor(b_t, kk, d_inv, ALU.mult))
                vec.link(v.tensor_tensor(k_t, kmod, d_inv, ALU.mult))
                vec.tell(v.tensor_tensor(r_t, r_z, decay, ALU.mult), S("rw_scaled"))

                dve.wait_ge(S("sg_root"), 1)
                for tt in range(2):
                    vec.link(v.scalar_tensor_tensor(sg_q[:, tt, :], sg_d[:, tt, :], rstd[:, tt:tt + 1],
                                                    f("ln_rows")[:, 0:T], ALU.mult, ALU.mult))
                vec.tell(v.tensor_tensor(sg_q, sg_q, f("ln_rows")[:, T:2 * T].unsqueeze(1).broadcast_to([P, 2, T]),
                                         ALU.add), S("sg_normed"))

                dve.wait_ge(S("sb_suffix"), 1)
                for b, o in ((5, 0), (6, 512), (7, 1024)):
                    ins = v.tensor_tensor(sb_b[:, o:o + 512], sb_b[:, o:o + 512], bank[b][:, :], ALU.add)
                vec.tell(ins, S("sb_arg"))
                dve.wait_ge(S("rw_bonus"), 1)
                vec.tell(v.tensor_tensor(bonus, b3(4), v_z, ALU.mult), S("rw_bonus_read"))
                dve.wait_ge(S("sb_exp"), 1)
                vec.link(v.tensor_tensor(halves[0][0], halves[0][0], halves[0][1], ALU.mult))
                vec.tell(v.tensor_tensor(halves[1][0], halves[1][0], halves[1][1], ALU.mult), S("sb_weights"))
                dve.wait_ge(S("sg_mixed"), 1)
                dve.wait_ge(S("short_conv"), 1)
                vec.link(v.tensor_tensor(y[:, 6:8, :], b3(2), f("sgb").rearrange("p (c t) -> p c t", c=2), ALU.add))
                vec.link(v.tensor_tensor(y[:, 6:8, :], y[:, 6:8, :], u_z, ALU.mult))
                dve.wait_ge(S("sb_out"), 1)
                vec.tell(v.tensor_copy(y[:, 2:4, :], b3(3)), S("early_read"))

                n = 0
                lv = f("levels_t").rearrange("p (l t) -> p l t", l=6)
                for odd in range(2):
                    q4 = slice(4 * odd, 4 * odd + 4)
                    for kind in range(5):
                        b = 2 + n % 6
                        dve.wait_ge(S("pair_done"), n + 1)
                        src = b3(b, P)
                        if kind == 0:
                            vec.tell(v.tensor_tensor(X[:, q4, :], src, four(f("level0")), ALU.mult), S("pair_read"), n + 1)
                            vec.link(v.tensor_tensor(X[:, q4, :], X[:, q4, :], four(ident), ALU.add))
                        elif kind == 1:
                            vec.tell(v.tensor_copy(MT[:, q4, :], src), S("pair_read"), n + 1)
                            vec.link(v.tensor_tensor(XT[:, q4, :], MT[:, q4, :], four(lv[:, 0, :]), ALU.mult))
                            vec.link(v.tensor_tensor(XT[:, q4, :], XT[:, q4, :], four(ident), ALU.add))
                        else:
                            dst, m = ((MTak, "upper"), (MTrb, "upper_eq"), (MTrk, "upper_eq"))[kind - 2]
                            vec.tell(v.tensor_tensor(dst[:, q4, :], src, four(f(m)), ALU.mult), S("pair_read"), n + 1)
                        n += 1

                for lev in range(1, LEVELS + 1):
                    if lev > 1:
                        dve.wait_ge(S("level_z"), lev - 1)
                    vec.tell(v.tensor_tensor(NT, MT, eight(lv[:, lev, :]), ALU.mult), S("level_nt"), lev)
                    if lev > 1:
                        grow(dve, v, lev - 1)
                grow(dve, v, LEVELS)
                dve.wait_ge(S("mv_done"), 1)
                vec.tell(v.tensor_copy(AM[:, :, 64:P], b3(2, 64)), S("mv_read"))
                dve.wait_ge(S("chunk_ops"), 1)
                vec.link(v.tensor_tensor(rp, b3(5), r_t, ALU.add))
                vec.link(v.tensor_tensor(phi, b3(7, 64), eight(f("eye2")), ALU.add))
                vec.link(v.tensor_copy(n0, b3(2, 64)))
                vec.link(v.tensor_copy(y0, b3(6)))
                for c in range(4):
                    last_decay = decay[:, :, 64 * c + 63:64 * c + 64].broadcast_to([P, 2, 64])
                    if c == 0:
                        vec.tell(v.tensor_tensor(st2[:, 1], n0[:, 0:2, :], last_decay, ALU.mult), S("rw_state"), 1)
                    elif c < 3:
                        dve.wait_ge(S("state_step"), c)
                        vec.link(v.tensor_tensor(stp, bank[4][:, 0:P].rearrange("p (c v) -> p c v", c=2),
                                                 n0[:, 2 * c:2 * c + 2, :], ALU.add))
                        vec.tell(v.tensor_tensor(st2[:, (c + 1) % 2], stp, last_decay, ALU.mult), S("rw_state"), c + 1)
                dve.wait_ge(S("state_step"), 3)
                vec.tell(v.tensor_tensor(y0[:, :, 64:T], y0[:, :, 64:T], b3(3)[:, :, 64:T], ALU.add), S("rw_y"))

                dve.wait_ge(S("gn_mean"), 1)
                vec.link(v.scalar_tensor_tensor(y0, b3(5), -1.0 / 64, y0, ALU.mult, ALU.add))
                vec.tell(v.tensor_tensor(yd2, y0, y0, ALU.mult), S("gn_squares"))
                dve.wait_ge(S("gn_var"), 1)
                vec.link(v.tensor_scalar(yd2, b3(6), 1.0 / 64, GN_EPS, ALU.mult, ALU.add))
                vec.tell(v.reciprocal(yd2, yd2), S("gn_inverse"))
                dve.wait_ge(S("gn_root"), 1)
                vec.link(v.tensor_tensor(y0, y0, yd2, ALU.mult))
                for c in range(2):
                    vec.link(v.tensor_scalar(y0[:, c, :], y0[:, c, :], col("rw_gn_g", c), col("rw_gn_b", c),
                                             ALU.mult, ALU.add))
                vec.link(v.tensor_tensor(y0, y0, bonus, ALU.add))
                vec.link(v.tensor_tensor(y[:, 4:6, :], y0, g_rw, ALU.mult))

            @block.scalar
            def _(act):
                a = nc.scalar
                sca.tell(a.activation(v_sg, v_sg, ACT.Gelu_apprx_tanh), S("sg_v"))
                a.activation(u_z, u_z, ACT.Gelu_apprx_tanh)
                act.wait_ge(S("sb_scores"), 1)
                for b, o in ((3, 0), (4, 512), (5, 1024)):
                    ins = a.activation(sb_l[:, o:o + 512], bank[b][:, :], ACT.Abs, scale=0.125)
                sca.link(ins)
                sca.link(a.activation(sb_l, sb_l, ACT.Exp, scale=-1.0))
                sca.tell(a.activation(sb_l, sb_l, ACT.Ln, bias=ones[:, 0:1]), S("sb_logs"))
                act.wait_ge(S("rw_mixed"), 1)
                a.activation(z[0:64, 6, :], z[0:64, 6, :], ACT.Tanh)
                sca.tell(a.activation(lora_h, g_z, ACT.Sigmoid), S("lora_in"))
                gate_reads(act, 2)
                act.wait_ge(S("rw_lora"), 1)
                for c in range(2):
                    a.activation(w_sig[:, c, :], b3(6)[:, c, :], ACT.Sigmoid, bias=col("rw_w0", c))
                    a.activation(a_sig[:, c, :], b3(7)[:, c, :], ACT.Sigmoid, bias=col("rw_a0", c))
                sca.tell(a.activation(g_rw, b3(2), ACT.Copy), S("rw_sigmoids"))
                act.wait_ge(S("kk_sum"), 1)
                sca.tell(a.activation(kk2, b3(3), ACT.Sqrt), S("kk_root"))
                act.wait_ge(S("sg_var"), 1)
                sca.tell(a.activation(sg_st[:, 2:4], sg_st[:, 2:4], ACT.Sqrt), S("sg_root"))
                act.wait_ge(S("rw_cum"), 1)
                a.activation(decay, cum, ACT.Exp, scale=-DECAY_SCALE)
                a.activation(d_inv, cum, ACT.Exp, scale=DECAY_SCALE)
                sca.tell(a.activation(d_prev, d_prev, ACT.Exp, scale=-DECAY_SCALE), S("rw_decays"))
                gate_reads(act, 3)
                act.wait_ge(S("sb_arg"), 1)
                sca.tell(a.activation(sb_k, sb_b, ACT.Exp), S("sb_exp"))
                gate_reads(act, 3)
                act.wait_ge(S("tm_done"), 1)
                for n in range(4):
                    ins = a.activation(tm[:, n], b3(4 + n), ACT.Copy)
                sca.tell(ins, S("tm_read"))
                gate_reads(act, 3)
                for lev in range(1, LEVELS + 1):
                    act.wait_ge(S("level_z"), lev)
                    a.activation(Z[:, 0:4, :], b3(2, P), ACT.Copy)
                    sca.tell(a.activation(Z[:, 4:8, :], b3(3, P), ACT.Copy), S("level_zc"), lev)
                    gate_reads(act, 2)
                for odd in range(2):
                    ins = a.activation(AM[:, 4 * odd:4 * odd + 4, 0:64].rearrange("p (a c) k -> p a c k", a=2),
                                       tm[:, 0].rearrange("p a (c r k) -> p r a c k", c=2, r=2)[:, odd], ACT.Copy)
                ins.then_inc(S("am_a"), 1)
                act.wait_ge(S("gh_done"), 1)
                a.activation(GH[:, 0:4, :], b3(3, P), ACT.Copy)
                sca.tell(a.activation(GH[:, 4:8, :], b3(4, P), ACT.Copy), S("gh_read"))
                gate_reads(act, 5)
                act.wait_ge(S("gn_inverse"), 1)
                sca.tell(a.activation(yd2, yd2, ACT.Sqrt), S("gn_root"))
                gate_reads(act, 6)
                for b in range(2):
                    act.wait_ge(drained[b], ev_at.banks[b] + 1)
                sca.link(a.activation(gates.rearrange("p g t -> p (g t)"), gates.rearrange("p g t -> p (g t)"),
                                      ACT.Sigmoid))

            @block.tensor
            def _(pe):
                mm = nc.tensor.matmul

                def pair(m):
                    odd, tt, c = m // 4, m % 4 // 2, m % 2
                    return 2 * c + odd, c, 64 * odd, tt

                def head(hh):
                    return hh // 2, 64 * (hh % 2)

                for hh in (0, 2, 1, 3):
                    c, p = head(hh)
                    if hh == 1:
                        turn(pe, ins)
                    mm(bank[3 + hh // 2][:, hh % 2 * T:(hh % 2 + 1) * T], kk_z[p:p + 64, c, 0:P], q_z[p:p + 64, c, :],
                       start=True, stop=True)
                    ins = mm(bank[5][:, hh * P:(hh + 1) * P], kk_z[p:p + 64, c, P:T], q_z[p:p + 64, c, P:T],
                             start=True, stop=True)
                ins.then_inc(S("sb_scores"), 1)
                gate_products(pe, 2)
                pe.wait_ge(S("lora_in"), 1)
                lw = f("lora")
                for c in range(2):
                    o = slice(c * T, (c + 1) * T)
                    mm(bank[6][:, o], lw[0:64, c * P:(c + 1) * P], z[0:64, 6, :], start=True, stop=True)
                    mm(bank[7][:, o], lw[64:P, c * P:(c + 1) * P], z[64:P, 6, :], start=True, stop=True)
                    ins = mm(bank[2][:, o], lw[:, T + c * P:T + (c + 1) * P], lora_h, start=True, stop=True)
                ins.then_inc(S("rw_lora"), 1)
                pe.wait_ge(S("kk_squares"), 1)
                pe.wait_ge(S("sb_keep"), 1)
                mm(bank[3][:, :], f("same"), kk2.rearrange("p c t -> p (c t)"), start=True, stop=True)\
                    .then_inc(S("kk_sum"), 1)
                pe.wait_ge(S("rw_sigmoids"), 1)
                k0, k1 = sb_k[:, 0:1024], sb_k[:, 1024:1536]
                mm(bank[7][:, :], f("after"), k1, start=True, stop=True)
                for half in range(2):
                    b = bank[5 + half]
                    mm(b[:, :], f("after"), k0[:, half * 512:(half + 1) * 512], start=True, stop=False)
                    for q in range(2):
                        hh = 2 * half + q
                        ins = mm(b[:, q * T + P:(q + 1) * T], ones, k1[:, hh * P:(hh + 1) * P],
                                 start=False, stop=q == 1)
                ins.then_inc(S("sb_suffix"), 1)
                gate_products(pe, 3)
                pe.wait_ge(S("rw_rk"), 1)
                mm(bank[4][:, :], f("same"), kk2.rearrange("p c t -> p (c t)"), start=True, stop=True)\
                    .then_inc(S("rw_bonus"), 1)
                pe.wait_ge(S("sg_normed"), 1)
                for g in range(4):
                    c, p = head(g)
                    for tt in range(2):
                        ins = mm(bank[2][p:p + 64, c * T + tt * P:c * T + (tt + 1) * P],
                                 sg_q[:, tt, g * 64:(g + 1) * 64], sg_wt[:, g, :], start=True, stop=True)
                ins.then_inc(S("sg_mixed"), 1)
                pe.wait_ge(S("sb_weights"), 1)
                for hh in range(4):
                    c, p = head(hh)
                    mm(bank[3][p:p + 64, c * T:(c + 1) * T], v_sb[:, 0, hh * 64:(hh + 1) * 64],
                       k0[:, hh * T:(hh + 1) * T], start=True, stop=False)
                    ins = mm(bank[3][p:p + 64, c * T + P:(c + 1) * T], v_sb[:, 1, hh * 64:(hh + 1) * 64],
                             k1[:, hh * P:(hh + 1) * P], start=False, stop=True)
                ins.then_inc(S("sb_out"), 1)
                gate_products(pe, 3)
                pe.wait_ge(S("rw_scaled"), 1)
                pe.wait_ge(S("sb_arg"), 1)
                pe.wait_ge(S("rw_bonus_read"), 1)
                for n, m in enumerate((a_t, b_t, k_t, v_z)):
                    for tt in range(2):
                        for c in range(2):
                            o = tt * T + c * P
                            ins = nc.tensor.transpose(bank[4 + n][:, o:o + P], m[:, c, tt * P:(tt + 1) * P], ident)
                ins.then_inc(S("tm_done"), 1)
                gate_products(pe, 3)
                pe.wait_ge(S("early_read"), 1)
                pe.wait_ge(S("tm_read"), 1)
                n = 0
                for odd in range(2):
                    for lhs, rhs in ((a_t, b_t), (b_t, a_t), (k_t, a_t), (b_t, r_t), (k_t, r_t)):
                        if n >= 6:
                            pe.wait_ge(S("pair_read"), n - 5)
                        for m in range(4):
                            _, c, p, tt = pair(4 * odd + m)
                            o = slice(tt * P, (tt + 1) * P)
                            ins = mm(bank[2 + n % 6][:, m * P:(m + 1) * P], lhs[p:p + 64, c, o], rhs[p:p + 64, c, o],
                                     start=True, stop=True)
                        ins.then_inc(S("pair_done"), 1)
                        n += 1
                for lev in range(1, LEVELS + 1):
                    pe.wait_ge(S("level_nt"), lev)
                    if lev == 1:
                        pe.wait_ge(S("pair_read"), 10)
                    else:
                        pe.wait_ge(S("level_grown"), lev - 1)
                    for m in range(8):
                        ins = mm(bank[2 + m // 4][:, m % 4 * P:(m % 4 + 1) * P], NT[:, m, :], X[:, m, :],
                                 start=True, stop=True)
                    ins.then_inc(S("level_z"), 1)
                    gate_products(pe, 1)
                    pe.wait_ge(S("level_zc"), lev)
                    for m in range(8):
                        o = slice(m % 4 * P, (m % 4 + 1) * P)
                        if lev < LEVELS:
                            mm(bank[4 + m // 4][:, o], XT[:, m, :], Z[:, m, :], start=True, stop=True)
                        ins = mm(bank[6 + m // 4][:, o], Z[:, m, :], XT[:, m, :], start=True, stop=True)
                    ins.then_inc(S("level_x"), 1)
                    gate_products(pe, 1)
                for m in range(8):
                    hh, _, _, tt = pair(m)
                    ins = mm(bank[2][:, m * 64:(m + 1) * 64], MTak[:, m, :],
                             tm[:, 3, tt, hh * 64:(hh + 1) * 64], start=True, stop=True)
                ins.then_inc(S("mv_done"), 1)
                pe.wait_ge(S("level_grown"), LEVELS)
                pe.wait_ge(S("mv_read"), 1)
                pe.wait_ge(S("am_a"), 1)
                for m in range(8):
                    ins = mm(bank[3 + m // 4][:, m % 4 * P:(m % 4 + 1) * P], XT[:, m, :], AM[:, m, :],
                             start=True, stop=True)
                ins.then_inc(S("gh_done"), 1)
                gate_products(pe, 2)
                pe.wait_ge(S("gh_read"), 1)
                for m in range(8):
                    hh, c, p, tt = pair(m)
                    o = slice(c * T + tt * P, c * T + (tt + 1) * P)
                    mm(bank[5][p:p + 64, o], GH[:, m, 0:64], MTrb[:, m, :], start=True, stop=True)
                    mm(bank[6][p:p + 64, o], GH[:, m, 64:P], MTrb[:, m, :], start=True, stop=False)
                    mm(bank[6][p:p + 64, o], tm[:, 3, tt, hh * 64:(hh + 1) * 64], MTrk[:, m, :], start=False, stop=True)
                for ch in (0, 2, 1, 3):
                    if ch == 1:
                        turn(pe, ins)
                    tt, r = ch // 2, slice(64 * (ch % 2), 64 * (ch % 2) + 64)
                    for hh in range(4):
                        c, p = head(hh)
                        m, o, hs = 4 * (hh % 2) + 2 * tt + c, slice((2 * ch + c) * 64, (2 * ch + c + 1) * 64), slice(hh * 64, (hh + 1) * 64)
                        mm(bank[7][p:p + 64, o], GH[r, m, 0:64], tm[r, 1, tt, hs], start=True, stop=True)
                        mm(bank[2][p:p + 64, o], tm[r, 1, tt, hs], GH[r, m, 64:P], start=True, stop=False)
                        ins = mm(bank[2][p:p + 64, o], tm[r, 2, tt, hs], tm[r, 3, tt, hs], start=False, stop=True)
                ins.then_inc(S("chunk_ops"), 1)
                gate_products(pe, 3)
                for ch in range(1, 4):
                    pe.wait_ge(S("rw_state"), ch)
                    for hh in range(4):
                        c, p = head(hh)
                        ins = mm(bank[3][p:p + 64, c * T + 64 * ch:c * T + 64 * (ch + 1)], st2[p:p + 64, ch % 2, c, :],
                                 rp[p:p + 64, c, 64 * ch:64 * (ch + 1)], start=True, stop=True)
                    if ch < 3:
                        for hh in range(4):
                            c, p = head(hh)
                            ins = mm(bank[4][p:p + 64, c * 64:(c + 1) * 64], phi[p:p + 64, 2 * ch + c, :],
                                     st2[p:p + 64, ch % 2, c, :], start=True, stop=True)
                    ins.then_inc(S("state_step"), 1)
                pe.wait_ge(S("rw_y"), 1)
                mm(bank[5][:, :], f("same"), y0.rearrange("p c t -> p (c t)"), start=True, stop=True)\
                    .then_inc(S("gn_mean"), 1)
                pe.wait_ge(S("gn_squares"), 1)
                mm(bank[6][:, :], f("same"), yd2.rearrange("p c t -> p (c t)"), start=True, stop=True)\
                    .then_inc(S("gn_var"), 1)
                gate_products(pe, 6)

        a5 = Area(arena, scratch_at)
        merged, prod = a5.take(8, T), a5.take(4, T)
        FF_FIRST, FF_SLOTS, FF_LAST = (0, 1, 3, 4), (0, 1, 2, 3, 4, 5), (6, 7)
        by_branch = gates.rearrange("p (b n) t -> p b n t", b=4)
        with nc.Block() as block:
            @block.sync
            def _(sp):
                load(sp, range(4))
                load(sp, range(4, 8))
                load(sp, range(4))
                load(sp, FF_FIRST)

            @block.tensor
            def _(pe):
                def branches(q, w, b, i):
                    for br in range(4):
                        dst = (b if br < 2 else bank[4 + q])[:, br % 2 * T:(br % 2 + 1) * T]
                        for k in range(2):
                            mm = nc.tensor.matmul(dst, w[:, 2 * br + k, :], y[:, 2 * br + k, :],
                                                  start=k == 0, stop=k == 1)
                    return mm

                def onto(q, w, b, i):
                    for k in range(KT):
                        mm = nc.tensor.matmul(b[:, 0:T], w[:, k, :], merged[:, k, :], start=k == 0, stop=k == KT - 1)
                    return mm

                project(pe, range(4, 8), range(4), 1, branches)
                project(pe, range(4), range(4), 1, branches)
                pe.wait_ge(S("merged"), KT)
                project(pe, range(4, 8), range(4), 1, onto)
                project(pe, range(4), range(4), 1, onto)

            @block.vector
            def _(dve):
                v = nc.vector

                def merge_one(n, q, b):
                    vec.link(v.tensor_tensor(prod[:, 0:2, :], b[:, :].rearrange("p (c t) -> p c t", c=2),
                                             by_branch[:, 0:2, n, :], ALU.mult))
                    return v.tensor_tensor(prod[:, 2:4, :], b3(4 + q), by_branch[:, 2:4, n, :], ALU.mult)

                for half, slots in enumerate((range(4, 8), range(4))):
                    for q, s in enumerate(slots):
                        evacuate(dve, [s], [q], 1, lambda _, b, i: merge_one(4 * half + q, q, b))
                        dve.wait_ge(drained[q], ev_at.banks[q] + 1)
                        vec.link(v.tensor_tensor(prod[:, 0:2, :], prod[:, 0:2, :], prod[:, 2:4, :], ALU.add))
                        vec.tell(v.tensor_tensor(merged[:, 4 * half + q, :], prod[:, 0, :], prod[:, 1, :], ALU.add),
                                 S("merged"), 4 * half + q + 1)
                for half, slots in enumerate((range(4, 8), range(4))):
                    evacuate(dve, slots, range(4), 1, lambda q, b, i: v.tensor_tensor(
                        x[:, 4 * half + q, :], x[:, 4 * half + q, :], b[:, 0:T], ALU.add))
                dve.wait_ge(drained[3], ev_at.banks[3] + 1)

        a6 = Area(arena)
        conv = a6.take(2, 2, T)
        hidden = a6.take(2, T)
        xin = a6.take(KT, TT)
        sq2 = a6.take(KT, TT)
        a6p = Area(arena_parts[a6.at])
        high, h_high = a6p.take(SLOTS, D), a6p.take(KT, T)
        hid_high, hid_low = a6p.take(2, T), a6p.take(2, T)
        low, h_low = ring_parts, h_parts[:, :, 0:T]
        assert a6.at + a6p.at <= scratch_at
        pairs = FT // 2 - 1
        before = {s: pe_at.rounds[s] for s in range(SLOTS)}

        def ff_block(n, i=0):
            if n < 0:
                return FF_FIRST[n + 4], before[FF_FIRST[n + 4]] + 1, n + 5
            if isinstance(i, int) and i == pairs:
                s = FF_LAST[n]
                return s, before[s] + 1, 4 + 6 * pairs + n + 1
            s = FF_SLOTS[n]
            return s, i + (before[s] + (s in FF_FIRST) + 1), i * 6 + (4 + n + 1)

        def ff_high(act, n, i=0):
            s, filled, number = ff_block(n, i)
            act.wait_ge(full[s], filled * 16)
            nc.scalar.activation(high[:, s, :], ring[:, s, :], ACT.Copy).then_inc(S("ff_high"), 1)

        def ff_low(dve, n, i=0):
            s, filled, number = ff_block(n, i)
            dve.wait_ge(S("ff_high"), number)
            nc.vector.tensor_tensor(low[:, s, :], ring[:, s, :], high[:, s, :].bitcast(F32), ALU.subtract)\
                .then_inc(S("ff_low"), 1)

        rms_norm(lambda k: x[:, k, :], lambda k: h[:, k, 0:T], "ffn_norm_g", RMS_EPS, squares,
                 beside=(lambda act: [ff_high(act, n) for n in (-4, -3)], lambda dve: [ff_low(dve, n) for n in (-4, -3)]))
        with nc.Block() as block:
            @block.sync
            def _(sp):
                sp.dma_start(xin[:, :, 0:M], meta_t).then_inc(S("meta_in"), 16)
                load(sp, FF_SLOTS, pairs)
                load(sp, FF_LAST)
                load(sp, range(4))
                sp.wait_ge(S("meta_in"), 16)

            @block.tensor
            def _(pe):
                mm = nc.tensor.matmul
                for b in range(4):
                    pe.wait_ge(drained[b], pe_at.banks[b] + 1)
                    mm(bank[b][:, :], ident, x[:, 2 * b:2 * b + 2, :].rearrange("p c t -> p (c t)"), start=True, stop=False)

                def up(n, i=0):
                    j = n // 3 % 2 if n >= 0 else n // 2 % 2
                    if n >= 0:
                        pe.wait_ge(S("up_read"), i * 2 + (j + 1))
                    for part in range(2):
                        s, _, number = ff_block(n + part, i)
                        b = bank[4 + 2 * j + part][:, 0:T]
                        pe.wait_ge(S("ff_low"), number)
                        for k in range(KT):
                            w = slice(k * P, (k + 1) * P)
                            if n == -4 and part == 0 and k % 4 == 0:
                                pe.wait_ge(S("ff_h_low"), k // 4 + 1)
                            mm(b, high[:, s, w], h_high[:, k, :], start=k == 0, stop=False)
                            mm(b, high[:, s, w], h_low[:, k, :], start=False, stop=False)
                            ins = mm(b, low[:, s, w], h_high[:, k, :], start=False, stop=k == KT - 1)
                        ins.then_inc(used[s], 1)

                def down(n, i, j, last_one=False):
                    s, _, number = ff_block(n, i)
                    pe.wait_ge(S("ff_low"), number)
                    pe.wait_ge(S("ff_hidden"), i * 2 + (j + 3))
                    for c in range(KT):
                        b, w = bank[c // 2][:, c % 2 * T:(c % 2 + 1) * T], slice(c * P, (c + 1) * P)
                        mm(b, high[:, s, w], hid_high[:, j, :], start=False, stop=False)
                        mm(b, high[:, s, w], hid_low[:, j, :], start=False, stop=False)
                        ins = mm(b, low[:, s, w], hid_high[:, j, :], start=False, stop=last_one and c % 2 == 1)
                    ins.then_inc(used[s], 1)

                up(-4)
                up(-2)
                with pe.Fori(0, pairs) as i:
                    for j in range(2):
                        up(3 * j, i)
                        down(3 * j + 2, i, j)
                for j in range(2):
                    down(j, pairs, j, j == 1)

            @block.vector
            def _(dve):
                v = nc.vector

                def tap(k, c):
                    return par[:, bass.ds(c + (at["ffn_conv_w"] + 2 * FT * k), 1)]

                def convolve(i, j):
                    dve.wait_ge(S("ff_hidden"), i * 2 + (j + 1))
                    for part in range(2):
                        s = FF_SLOTS[3 * j + part]
                        dve.wait_ge(used[s], i + (before[s] + 1))
                    for back in range(3):
                        for part in range(2):
                            src, dst, c = bank[4 + 2 * j + part], conv[:, j, part, :], i * 2 + (j + FT * part)
                            if back == 0:
                                ins = v.tensor_scalar(dst, src[:, 0:T], tap(2, c), None, ALU.mult)
                            else:
                                dve.wait_ge(S("ff_step"), i * 12 + (6 * j + 2 * back + part - 1))
                                ins = v.scalar_tensor_tensor(dst[:, back:T], src[:, 0:T - back], tap(2 - back, c),
                                                             dst[:, back:T], ALU.mult, ALU.add)
                            ins.then_inc(S("ff_step"), 1)
                    dve.wait_ge(S("ff_step"), i * 12 + (6 * j + 6))
                    dve.sem_inc(S("up_read"), 1)

                for half in range(2):
                    dve.wait_ge(S("ff_h_high"), half + 1)
                    k = slice(4 * half, 4 * half + 4)
                    v.tensor_tensor(h_low[:, k, :], h[:, k, 0:T], h_high[:, k, :].bitcast(F32), ALU.subtract)\
                        .then_inc(S("ff_h_low"), 1)
                for n in (-2, -1):
                    ff_low(dve, n)
                with dve.Fori(0, pairs) as i:
                    for j in range(2):
                        ff_low(dve, 3 * j, i)
                        ff_low(dve, 3 * j + 1, i)
                        convolve(i, j)
                        ff_low(dve, 3 * j + 2, i)
                for j in range(2):
                    ff_low(dve, j, pairs)
                for j in range(2):
                    convolve(pairs, j)
                dve.wait_ge(used[FF_LAST[1]], before[FF_LAST[1]] + 1)
                for b in range(4):
                    ins = v.tensor_copy(x[:, 2 * b:2 * b + 2, :], b3(b))
                    ins.then_inc(drained[b], 1)
                for b in range(4):
                    dve.wait_ge(drained[b], pe_at.banks[b] + 2)

            @block.scalar
            def _(act):
                def silu(i, j):
                    act.wait_ge(S("up_read"), i * 2 + (j + 1))
                    nc.scalar.activation(conv[:, j, 0, :], conv[:, j, 0, :], ACT.Silu).then_inc(S("ff_silu"), 1)

                for half in range(2):
                    k = slice(4 * half, 4 * half + 4)
                    nc.scalar.activation(h_high[:, k, :], h[:, k, 0:T], ACT.Copy).then_inc(S("ff_h_high"), 1)
                for n in (-2, -1):
                    ff_high(act, n)
                with act.Fori(0, pairs) as i:
                    for j in range(2):
                        ff_high(act, 3 * j, i)
                        ff_high(act, 3 * j + 1, i)
                        ff_high(act, 3 * j + 2, i)
                        silu(i, j)
                for j in range(2):
                    ff_high(act, j, pairs)
                for j in range(2):
                    silu(pairs, j)

            @block.gpsimd
            def _(pool):
                p = nc.gpsimd
                pool.sem_inc(S("ff_hidden"), 2)

                def hide(i, j):
                    pool.wait_ge(S("ff_silu"), i * 2 + (j + 1))
                    s = FF_SLOTS[3 * j + 2]
                    pool.wait_ge(used[s], i + before[s])
                    hid = hidden[:, j, :]
                    p.tensor_tensor(hid, conv[:, j, 0, :], conv[:, j, 1, :], ALU.mult).then_inc(S("hid_step"), 1)
                    pool.wait_ge(S("hid_step"), i * 4 + (2 * j + 1))
                    p.tensor_tensor(hid_high[:, j, :].rearrange("p (a t) -> p a t", a=2),
                                    hid.rearrange("p (a t) -> p a t", a=2),
                                    ones.unsqueeze(1).broadcast_to([P, 2, P]), ALU.mult).then_inc(S("hid_step"), 1)
                    pool.wait_ge(S("hid_step"), i * 4 + (2 * j + 2))
                    p.tensor_tensor(hid_low[:, j, :], hid, hid_high[:, j, :].bitcast(F32), ALU.subtract)\
                        .then_inc(S("ff_hidden"), 1)

                with pool.Fori(0, pairs) as i:
                    hide(i, 0)
                    hide(i, 1)
                hide(pairs, 0)
                hide(pairs, 1)
            for tiles in (pe_at, ev_at):
                tiles.advance(FF_FIRST, 1, None)
                tiles.advance(FF_SLOTS, pairs, None)
                tiles.advance(FF_LAST, 1, None)
                for b in range(4):
                    tiles.banks[b] += 1
        rms_norm(lambda k: x[:, k, :], lambda k: xin[:, k, M:TT], "final_norm_g", RMS_EPS, squares_b := sq2)

        rms_norm(lambda k: xin[:, k, :], lambda k: h[:, k, :], "norm1_g_2", RMS_EPS, squares_b, TT)
        a7 = Area(arena, a6.at)
        us, xm = a7.take(4, TT), a7.take(8, TT)
        zg = a7.take(24, T)
        s_at, s_size = offsets(SECOND)
        snd = a7.take(s_size)

        def g2(name, lo=0, n=None):
            return snd[:, s_at[name] + lo:s_at[name] + lo + (n or SECOND[name])]

        with nc.Block() as block:
            @block.sync
            def _(sp):
                sp.dma_start(snd, second).then_inc(S("second_in"), 16)
                load(sp, range(4), 2)
                load(sp, (4, 5, 6))
                load(sp, range(4))
                sp.wait_ge(S("second_in"), 16)

            @block.gpsimd
            def _(pool):
                poo.link(nc.gpsimd.tensor_copy(x[:], xin[:, :, M:TT]))

            @block.tensor
            def _(pe):
                project(pe, range(4), range(4), 3, channels(TT))

            @block.scalar
            def _(act):
                both = arena[:, a6.at:a6.at + 12 * TT].rearrange("p (c t) -> p c t", t=TT)
                evacuate(act, range(4), range(4), 3, lambda q, b, i: nc.scalar.activation(
                    both[:, bass.ds(i * 4 + q, 1), :].rearrange("p a t -> p (a t)"), b[:, 0:TT], ACT.Copy))

        r1 = Area(arena)
        e_t = r1.take(2, 1024)
        rows = r1.take(6, TT)
        small = r1.take(20, 16)
        colb = r1.take(3, 4)
        rs4 = r1.take(4, T)
        dmat = [r1.take(640)]
        assert r1.at <= a6.at
        a8 = Area(arena, a7.at)
        er, ei = a8.take(16, TT), a8.take(16, TT)
        xc = a8.take(8, TT)
        dmat.append(a8.take(640))
        s5_at = a8.at
        kc, vc, vt = a8.take(8, TT), a8.take(8, TT), a8.take(3, D)
        qc, h_ml = xm, xm[:, :, M:TT]
        a9 = Area(arena, s5_at)
        bu = a9.take(2, 4, TT)
        zt = a9.take(2, 4, TT)
        rot, rt = a9.take(2, 2 * TT), a9.take(2, 2 * TT)
        s_out = e_t[:, 0, :].rearrange("p (c s t) -> p c s t", c=2, s=2)
        s_tmp = e_t[:, 1, :].rearrange("p (c s t) -> p c s t", c=2, s=2)
        proj_n = {"pe": 0, "act": 0}
        zsig, gs_g, gm_g = zg[:, 0:8, :], zg[:, 8:16, :], zg[:, 16:24, :]
        PAIRS = 8

        def z_products(pe, n):
            for _ in range(n):
                s = proj_n["pe"] % 4
                project(pe, [s], [s % 2], 1, channels(T, M))
                proj_n["pe"] += 1

        def z_reads(act, n):
            for _ in range(n):
                g = proj_n["act"]
                evacuate(act, [g % 4], [g % 2], 1, lambda q, b, i: nc.scalar.activation(zg[:, g, :], b[:, 0:T], ACT.Copy))
                proj_n["act"] += 1

        def sm(n):
            return small[:, n, :]

        (S_DT, S_X, S_TH, S_K, S_R, S_SIN, S_HALF, S_COS, S_TANH, S_EM, S_NR, S_NI, S_DEN, S_CR, S_CI, S_T, S_ER, S_EI,
         S_E2R, S_E2I) = range(20)

        with nc.Block() as block:
            bd = [pe_at.rounds[s] for s in (4, 5, 6)]

            @block.sync
            def _(sp):
                load(sp, range(4), 5)
                load(sp, (7,))
                for s in (4, 5, 6):
                    load(sp, (s,))

            @block.vector
            def _(dve):
                v = nc.vector
                are, aim = par[:, at["ssm_a_re_2"]:at["ssm_a_re_2"] + 16], par[:, at["ssm_a_im_2"]:at["ssm_a_im_2"] + 16]
                dve.wait_ge(S("s5_dt"), 1)
                vec.link(v.tensor_tensor(sm(S_X), are, sm(S_DT), ALU.mult))
                vec.link(v.tensor_tensor(sm(S_TH), aim, sm(S_DT), ALU.mult))
                vec.link(v.tensor_scalar(sm(S_K), sm(S_TH), 1.0 / TWO_PI, None, ALU.mult))
                vec.link(v.tensor_scalar(sm(S_K), sm(S_K), 12582912.0, None, ALU.add))
                vec.link(v.tensor_scalar(sm(S_K), sm(S_K), 12582912.0, None, ALU.subtract))
                vec.link(v.scalar_tensor_tensor(sm(S_TH), sm(S_K), -6.28125, sm(S_TH), ALU.mult, ALU.add))
                vec.link(v.scalar_tensor_tensor(sm(S_TH), sm(S_K), -0.0019353071795864769, sm(S_TH), ALU.mult, ALU.add))
                vec.tell(v.tensor_scalar(sm(S_TH), sm(S_TH), 3.1415925, -3.1415925, ALU.min, ALU.max), S("s5_angle"))
                w0 = at["ml_conv_w_2"]
                for c in range(8):
                    vec.link(v.tensor_scalar(xc[:, c, :], xm[:, c, :], par[:, w0 + 24 + c:w0 + 25 + c],
                                             col("ml_conv_b_2", c), ALU.mult, ALU.add))
                    for back in (1, 2, 3):
                        j = w0 + 8 * (3 - back) + c
                        ins = v.scalar_tensor_tensor(xc[:, c, back:TT], xm[:, c, 0:TT - back], par[:, j:j + 1],
                                                     xc[:, c, back:TT], ALU.mult, ALU.add)
                        vec.link(ins) if back < 3 else vec.tell(ins, S("ml_conv"), c + 1)
                dve.wait_ge(S("s5_sines"), 1)
                vec.link(v.tensor_tensor(sm(S_T), sm(S_HALF), sm(S_HALF), ALU.mult))
                vec.link(v.tensor_scalar(sm(S_COS), sm(S_T), -2.0, 1.0, ALU.mult, ALU.add))
                vec.link(v.tensor_copy(sm(S_ER), sm(S_COS)))
                vec.tell(v.tensor_copy(sm(S_EI), sm(S_SIN)), S("s5_unit"))
                vec.link(v.tensor_scalar(sm(S_DEN), sm(S_TANH), -1.0, 1.0, ALU.mult, ALU.add))
                vec.link(v.reciprocal(sm(S_DEN), sm(S_DEN)))
                vec.link(v.scalar_tensor_tensor(sm(S_EM), sm(S_TANH), 2.0, sm(S_DEN), ALU.mult, ALU.mult))
                vec.link(v.tensor_tensor(sm(S_NR), sm(S_EM), sm(S_COS), ALU.mult))
                vec.link(v.scalar_tensor_tensor(sm(S_NR), sm(S_T), -2.0, sm(S_NR), ALU.mult, ALU.add))
                vec.link(v.tensor_tensor(sm(S_NI), sm(S_R), sm(S_SIN), ALU.mult))
                vec.link(v.tensor_tensor(sm(S_DEN), are, are, ALU.mult))
                vec.link(v.tensor_tensor(sm(S_T), aim, aim, ALU.mult))
                vec.link(v.tensor_tensor(sm(S_DEN), sm(S_DEN), sm(S_T), ALU.add))
                vec.link(v.reciprocal(sm(S_DEN), sm(S_DEN)))
                vec.link(v.tensor_tensor(sm(S_CR), sm(S_NR), are, ALU.mult))
                vec.link(v.tensor_tensor(sm(S_T), sm(S_NI), aim, ALU.mult))
                vec.link(v.tensor_tensor(sm(S_CR), sm(S_CR), sm(S_T), ALU.add))
                vec.link(v.tensor_tensor(sm(S_CR), sm(S_CR), sm(S_DEN), ALU.mult))
                vec.link(v.tensor_tensor(sm(S_CI), sm(S_NI), are, ALU.mult))
                vec.link(v.tensor_tensor(sm(S_T), sm(S_NR), aim, ALU.mult))
                vec.link(v.tensor_tensor(sm(S_CI), sm(S_CI), sm(S_T), ALU.subtract))
                vec.link(v.tensor_tensor(sm(S_CI), sm(S_CI), sm(S_DEN), ALU.mult))
                c_re, c_im = (g2(n).rearrange("p (s c) -> p s c", s=16) for n in ("c_re", "c_im"))
                t0, t1, t2 = (rs4.rearrange("p a b -> p (a b)")[:, 0:512].rearrange("p (s c) -> p s c", s=16),
                              dmat[0][:, 0:512].rearrange("p (s c) -> p s c", s=16),
                              dmat[1][:, 0:512].rearrange("p (s c) -> p s c", s=16))
                cr, ci = (sm(n).unsqueeze(2).broadcast_to([P, 16, 32]) for n in (S_CR, S_CI))
                vec.link(v.tensor_tensor(t0, c_re, cr, ALU.mult))
                vec.link(v.tensor_tensor(t1, c_im, ci, ALU.mult))
                vec.link(v.tensor_tensor(t0, t0, t1, ALU.subtract))
                vec.link(v.tensor_tensor(t1, c_re, ci, ALU.mult))
                vec.link(v.tensor_tensor(t2, c_im, cr, ALU.mult))
                vec.link(v.tensor_copy(c_re, t0))
                vec.link(v.scalar_tensor_tensor(c_im, t1, -1.0, t2, ALU.mult, ALU.subtract))

                dve.wait_ge(S("if_sum"), 1)
                vec.tell(v.tensor_copy(rows[0:8, 5, :], bank[6][0:8, 0:TT]), S("if_rows"))
                dve.wait_ge(S("if_split"), 1)
                ig, lf, cf, mx, ab, tr = (rows[0:4, n, :] for n in range(6))
                vec.link(v.tensor_scalar(ig, bank[7][0:4, 0:TT], col("ml_b_if_2", 0)[0:4], None, ALU.add))
                vec.link(v.tensor_scalar(lf, bank[6][0:4, 0:TT], col("ml_b_if_2", 1)[0:4], None, ALU.add))
                vec.tell(v.scalar_tensor_tensor(ab, lf, -1.0, lf, ALU.mult, ALU.max), S("ml_abs"))
                dve.wait_ge(S("ml_log"), 1)
                vec.link(v.tensor_scalar(lf, lf, 0.0, None, ALU.min))
                vec.link(v.tensor_tensor(lf, lf, ab, ALU.subtract))
                one_row = ones[0:4, 0:1].broadcast_to([4, TT])
                vec.link(v.tensor_tensor_scan(cf, one_row, lf, 0.0, ALU.mult, ALU.add))
                vec.link(v.tensor_tensor_scan(mx, lf, ig, 0.0, ALU.add, ALU.max))
                vec.link(v.tensor_tensor(ig, ig, cf, ALU.subtract))
                vec.tell(v.tensor_tensor(cf, cf, mx, ALU.subtract), S("ml_rows"))
                dve.wait_ge(S("ml_cols"), 1)
                vec.tell(v.tensor_copy(colb, bank[5][:, 0:12].rearrange("p (s h) -> p s h", s=3)), S("ml_cols_read"))
                for hh in range(4):
                    d = dmat[hh % 2]
                    d1, d2, dm = d[:, 0:T], d[:, T:T + P], d[0:M, 384:640]
                    dve.wait_ge(S("head_scores"), hh + 1)
                    vec.link(v.scalar_tensor_tensor(d1, bank[2][:, 0:T], colb[:, 1, hh:hh + 1], g2("neg0"),
                                                    ALU.add, ALU.add))
                    vec.link(v.scalar_tensor_tensor(d2, bank[2][:, P:T], colb[:, 2, hh:hh + 1], g2("neg1", P, P),
                                                    ALU.add, ALU.add))
                    vec.tell(v.tensor_scalar(dm, bank[2][0:M, 0:T], colb[0:M, 0, hh:hh + 1], None, ALU.add),
                             S("head_logs"), hh + 1)
                    dve.wait_ge(S("head_exp"), hh + 1)
                    vec.link(v.scalar_tensor_tensor(d[:, 0:384], bank[3][:, 0:384], 0.0625, d[:, 0:384], ALU.mult, ALU.mult))
                    vec.tell(v.scalar_tensor_tensor(dm, bank[4][0:M, 0:T], 0.0625, dm, ALU.mult, ALU.mult),
                             S("head_weights"), hh + 1)
                    dve.wait_ge(S("head_sums"), hh + 1)
                    rd = rs4[:, 0, :]
                    vec.link(v.tensor_scalar(rd, bank[6][:, 0:T], -1.0, None, ALU.mult))
                    vec.link(v.tensor_tensor(rd, rd, bank[6][:, 0:T], ALU.max))
                    vec.link(v.tensor_tensor(rd, rd, bank[2][:, T:2 * T], ALU.max))
                    vec.link(v.reciprocal(rd, rd))
                    vec.tell(v.tensor_tensor(h_ml[:, 2 * hh:2 * hh + 2, :], b3(5), rd.unsqueeze(1).broadcast_to([P, 2, T]),
                                             ALU.mult), S("head_read"), hh + 1)
                dve.wait_ge(S("z_sigmoid"), 1)
                vec.link(v.tensor_tensor(h_ml, h_ml, zsig, ALU.mult))
                hsq = vc[:, :, 0:T]
                vec.tell(v.tensor_tensor(hsq, h_ml, h_ml, ALU.mult), S("ml_squares"))
                dve.wait_ge(S("ml_sums"), 1)
                for half in range(2):
                    vec.link(v.tensor_scalar(rs4[:, 2 * half:2 * half + 2, :], b3(2 + half), 1.0 / T, RMS_EPS,
                                             ALU.mult, ALU.add))
                vec.tell(v.reciprocal(rs4, rs4), S("ml_inverse"))
                dve.wait_ge(S("ml_root"), 1)
                for c in range(8):
                    vec.link(v.scalar_tensor_tensor(h_ml[:, c, :], h_ml[:, c, :], col("ml_norm_g_2", c), rs4[:, c // 2, :],
                                                    ALU.mult, ALU.mult))
                    vec.link(v.scalar_tensor_tensor(h_ml[:, c, :], xc[:, c, M:TT], col("ml_skip_2", c), h_ml[:, c, :],
                                                    ALU.mult, ALU.add))
                dve.sem_inc(S("ml_out"), 1)

                dve.wait_ge(S("tables"), 1)
                for p in range(PAIRS):
                    dve.wait_ge(S("bu_ready"), 4 * p + 4)
                    cs, sn = er[:, 2 * p:2 * p + 2, :], ei[:, 2 * p:2 * p + 2, :]
                    src = bu[:, p % 2].rearrange("p (s c) t -> p c s t", s=2)
                    re, im = src[:, 0], src[:, 1]
                    xr, xi = (rot[:, n, :].rearrange("p (s t) -> p s t", s=2) for n in range(2))
                    q0, q1 = (rt[:, n, :].rearrange("p (s t) -> p s t", s=2) for n in range(2))
                    vec.link(v.tensor_tensor(q0, im, sn, ALU.mult))
                    vec.link(v.tensor_tensor(xr, re, cs, ALU.mult))
                    vec.link(v.tensor_tensor(xr, xr, q0, ALU.add))
                    vec.link(v.tensor_tensor(q1, re, sn, ALU.mult))
                    vec.link(v.tensor_tensor(xi, im, cs, ALU.mult))
                    vec.tell(v.tensor_tensor(xi, xi, q1, ALU.subtract), S("bu_turned"), p + 1)
                    if p >= 2:
                        dve.wait_ge(S("s_ready"), p - 1)
                    for s in range(2):
                        r = sm(S_R)[:, 2 * p + s:2 * p + s + 1].broadcast_to([P, TT])
                        for c, xx in ((0, xr), (1, xi)):
                            ins = v.tensor_tensor_scan(zt[:, p % 2, 2 * c + s, :], r, xx[:, s, :], 0.0, ALU.mult, ALU.add)
                    vec.tell(ins, S("z_ready"), p + 1)
                dve.wait_ge(S("c_done"), PAIRS)
                for c in range(4):
                    ins = v.scalar_tensor_tensor(us[:, c, M:TT], us[:, c, M:TT], col("ssm_d_2", c),
                                                 bank[6 + c // 2][:, c % 2 * T:(c % 2 + 1) * T], ALU.mult, ALU.add)
                vec.tell(ins, S("s5_y"))

            @block.gpsimd
            def _(pool):
                g = nc.gpsimd
                pool.wait_ge(S("s5_unit"), 1)
                poo.link(g.memset(er[:, :, 0:1], 1.0))
                poo.link(g.memset(ei[:, :, 0:1], 0.0))
                n = 1
                while n < TT:
                    w = min(n, TT - n)
                    for half in range(2):
                        o = slice(8 * half, 8 * half + 8)
                        br = sm(S_ER)[:, o].unsqueeze(2).broadcast_to([P, 8, w])
                        bi = sm(S_EI)[:, o].unsqueeze(2).broadcast_to([P, 8, w])
                        ta, tb = (e_t[:, k, 0:8 * min(w, P)].rearrange("p (s t) -> p s t", s=8) for k in range(2))
                        lo_r, lo_i, hi_r, hi_i = er[:, o, 0:w], ei[:, o, 0:w], er[:, o, n:n + w], ei[:, o, n:n + w]
                        poo.link(g.tensor_tensor(hi_r, lo_r, br, ALU.mult))
                        poo.link(g.tensor_tensor(ta, lo_i, bi, ALU.mult))
                        poo.link(g.tensor_tensor(hi_r, hi_r, ta, ALU.subtract))
                        poo.link(g.tensor_tensor(hi_i, lo_i, br, ALU.mult))
                        poo.link(g.tensor_tensor(tb, lo_r, bi, ALU.mult))
                        poo.link(g.tensor_tensor(hi_i, hi_i, tb, ALU.add))
                    poo.link(g.tensor_tensor(sm(S_E2R), sm(S_ER), sm(S_ER), ALU.mult))
                    poo.link(g.tensor_tensor(sm(S_E2I), sm(S_EI), sm(S_EI), ALU.mult))
                    poo.link(g.tensor_tensor(sm(S_EI), sm(S_ER), sm(S_EI), ALU.mult))
                    poo.link(g.tensor_tensor(sm(S_EI), sm(S_EI), sm(S_EI), ALU.add))
                    poo.link(g.tensor_tensor(sm(S_ER), sm(S_E2R), sm(S_E2I), ALU.subtract))
                    n *= 2
                pool.sem_inc(S("tables"), 1)
                for p in range(PAIRS):
                    cs, sn = er[:, 2 * p:2 * p + 2, M:TT], ei[:, 2 * p:2 * p + 2, M:TT]
                    zr, zi = zt[:, p % 2, 0:2, M:TT], zt[:, p % 2, 2:4, M:TT]
                    pool.wait_ge(S("z_ready"), p + 1)
                    if p >= 1:
                        pool.wait_ge(S("c_done"), p)
                    poo.link(g.tensor_tensor(s_out[:, 0], zr, cs, ALU.mult))
                    poo.link(g.tensor_tensor(s_tmp[:, 0], zi, sn, ALU.mult))
                    poo.link(g.tensor_tensor(s_out[:, 0], s_out[:, 0], s_tmp[:, 0], ALU.subtract))
                    poo.link(g.tensor_tensor(s_out[:, 1], zr, sn, ALU.mult))
                    poo.link(g.tensor_tensor(s_tmp[:, 1], zi, cs, ALU.mult))
                    poo.tell(g.tensor_tensor(s_out[:, 1], s_out[:, 1], s_tmp[:, 1], ALU.add), S("s_ready"), p + 1)

            @block.scalar
            def _(act):
                a = nc.scalar
                qn = {"n": 0}

                def read_unit(dst, src):
                    act.wait_ge(S("qkv_done"), qn["n"] + 1)
                    a.activation(dst, src, ACT.Copy).then_inc(S("qkv_read"), 1)
                    qn["n"] += 1

                ldt = par[:, at["ssm_log_dt_2"]:at["ssm_log_dt_2"] + 16]
                sca.tell(a.activation(sm(S_DT), ldt, ACT.Exp), S("s5_dt"))
                z_reads(act, 2)
                act.wait_ge(S("s5_angle"), 1)
                a.activation(sm(S_R), sm(S_X), ACT.Exp)
                a.activation(sm(S_TANH), sm(S_X), ACT.Tanh, scale=0.5)
                a.activation(sm(S_SIN), sm(S_TH), ACT.Sin)
                sca.tell(a.activation(sm(S_HALF), sm(S_TH), ACT.Sin, scale=0.5), S("s5_sines"))
                for k in range(8):
                    read_unit(vc[:, k, :], bank[2 + qn["n"] % 4][:, 0:TT])
                for st in range(3):
                    for half in range(2):
                        n = M if st == 0 else P
                        read_unit(vt[0:n, st, half * 512:(half + 1) * 512], bank[2 + qn["n"] % 4][0:n, :])
                z_reads(act, 2)
                for c in range(8):
                    act.wait_ge(S("ml_conv"), c + 1)
                    a.activation(xc[:, c, :], xc[:, c, :], ACT.Silu).then_inc(S("xc_ready"), 1)
                for dst in (qc, kc):
                    for k in range(8):
                        read_unit(dst[:, k, :], bank[2 + qn["n"] % 4][:, 0:TT])
                z_reads(act, 4)
                for b in range(2):
                    act.wait_ge(drained[b], ev_at.banks[b] + 1)
                sca.tell(a.activation(zsig.rearrange("p c t -> p (c t)"), zsig.rearrange("p c t -> p (c t)"), ACT.Sigmoid),
                         S("z_sigmoid"))
                act.wait_ge(S("ml_abs"), 1)
                ab, mx = rows[0:4, 4, :], rows[0:4, 3, :]
                sca.link(a.activation(ab, ab, ACT.Exp, scale=-1.0))
                sca.tell(a.activation(ab, ab, ACT.Ln, bias=ones[0:4, 0:1]), S("ml_log"))
                act.wait_ge(S("ml_rows"), 1)
                sca.tell(a.activation(mx, mx, ACT.Exp, scale=-1.0), S("ml_expm"))
                z_reads(act, 2)
                for hh in range(4):
                    d = dmat[hh % 2]
                    act.wait_ge(S("head_logs"), hh + 1)
                    a.activation(d[:, 0:384], d[:, 0:384], ACT.Exp)
                    sca.tell(a.activation(d[0:M, 384:640], d[0:M, 384:640], ACT.Exp), S("head_exp"), hh + 1)
                    z_reads(act, 1)
                z_reads(act, 2)
                act.wait_ge(S("ml_inverse"), 1)
                sca.tell(a.activation(rs4, rs4, ACT.Sqrt), S("ml_root"))
                act.wait_ge(S("ml_out"), 1)
                for p in range(PAIRS):
                    act.wait_ge(S("bu_done"), p + 1)
                    if p >= 2:
                        act.wait_ge(S("bu_turned"), p - 1)
                    for n in range(4):
                        a.activation(bu[:, p % 2, n, :], bank[2 + n][:, 0:TT], ACT.Copy).then_inc(S("bu_ready"), 1)
                    z_reads(act, 1)
                for b in range(2):
                    act.wait_ge(drained[b], ev_at.banks[b] + 1)
                sca.link(a.activation(zg[:, 8:24, :].rearrange("p c t -> p (c t)"),
                                      zg[:, 8:24, :].rearrange("p c t -> p (c t)"), ACT.Sigmoid))
                act.wait_ge(S("s5_y"), 1)
                sca.link(a.activation(us[:, :, M:TT], us[:, :, M:TT], ACT.Gelu_apprx_tanh))

            @block.tensor
            def _(pe):
                mm = nc.tensor.matmul
                blockdiag = [ring[:, s, :].rearrange("p (k n) -> p k n", n=P) for s in (4, 5, 6)]
                un = {"n": 0}

                def unit_bank():
                    n = un["n"]
                    if n >= 4:
                        pe.wait_ge(S("qkv_read"), n - 3)
                    un["n"] += 1
                    return bank[2 + n % 4]

                spans = ((0, M), (M, P), (M + P, P))
                z_products(pe, 2)
                pe.wait_ge(full[6], 16 * (bd[2] + 1))
                for k in range(8):
                    ins = mm(unit_bank()[:, 0:TT], blockdiag[2][:, k, :], xm[:, k, :], start=True, stop=True)
                    ins.then_inc(S("qkv_done"), 1)
                for st, (lo, n) in enumerate(spans):
                    for half in range(2):
                        b = unit_bank()
                        for k in range(4):
                            ins = mm(b[0:n, k * P:(k + 1) * P], xm[:, 4 * half + k, lo:lo + n],
                                     blockdiag[2][:, 4 * half + k, :], start=True, stop=True)
                        ins.then_inc(S("qkv_done"), 1)
                z_products(pe, 2)
                pe.wait_ge(S("xc_ready"), 8)
                for w in range(2):
                    pe.wait_ge(full[4 + w], 16 * (bd[w] + 1))
                    for k in range(8):
                        ins = mm(unit_bank()[:, 0:TT], blockdiag[w][:, k, :], xc[:, k, :], start=True, stop=True)
                        ins.then_inc(S("qkv_done"), 1)
                z_products(pe, 4)
                pe.wait_ge(S("qkv_read"), 30)
                w_if = g2("w_if").rearrange("p (k n) -> p k n", n=8)
                for n in range(24):
                    src = (qc, kc, vc)[n // 8][:, n % 8, :]
                    ins = mm(bank[6][0:8, 0:TT], w_if[:, n, :], src, start=n == 0, stop=n == 23)
                ins.then_inc(S("if_sum"), 1)
                for w in range(3):
                    pe.sem_inc(used[4 + w], 1)
                pe.wait_ge(S("if_rows"), 1)
                mm(bank[7][0:4, 0:TT], ident[0:8, 0:4], rows[0:8, 5, :], start=True, stop=True)
                mm(bank[6][0:4, 0:TT], ident[0:8, 4:8], rows[0:8, 5, :], start=True, stop=True).then_inc(S("if_split"), 1)
                z_products(pe, 2)
                pe.wait_ge(S("ml_rows"), 1)
                for st, (lo, n) in enumerate(spans):
                    ins = mm(bank[5][0:n, 4 * st:4 * st + 4], rows[0:4, 0, lo:lo + n], ident[0:4, 0:4], start=True, stop=True)
                ins.then_inc(S("ml_cols"), 1)
                pe.wait_ge(S("ml_expm"), 1)
                pe.wait_ge(S("ml_cols_read"), 1)
                sel = g2("sel").rearrange("p (h n) -> p h n", h=4)
                for hh in range(4):
                    if hh:
                        pe.wait_ge(S("head_read"), hh)
                    mm(bank[2][:, 0:T], sel[0:4, hh, :], rows[0:4, 2, M:TT], start=True, stop=True)
                    mm(bank[2][:, T:2 * T], sel[0:4, hh, :], rows[0:4, 3, M:TT], start=True, stop=True)
                    for st, (b, off, tlo) in enumerate(((4, 0, 0), (3, 0, 0), (3, T, P))):
                        lo, n = spans[st]
                        for c in (2 * hh, 2 * hh + 1):
                            ins = mm(bank[b][0:n, off:off + T - tlo], kc[:, c, lo:lo + n], qc[:, c, M + tlo:TT],
                                     start=c % 2 == 0, stop=c % 2 == 1)
                    ins.then_inc(S("head_scores"), 1)
                    z_products(pe, 1)
                    pe.wait_ge(S("head_weights"), hh + 1)
                    d = dmat[hh % 2]
                    wts = ((d[:, 0:T], 1, P, 0), (d[:, T:T + P], 2, P, P), (d[0:M, 384:640], 0, M, 0))
                    for e in range(3):
                        for j, (w, st, n, tlo) in enumerate(wts):
                            lhs = ones[0:n, :] if e == 2 else vt[0:n, st, hh * T + e * P:hh * T + (e + 1) * P]
                            dst = bank[6][:, tlo:T] if e == 2 else bank[5][:, e * T + tlo:(e + 1) * T]
                            ins = mm(dst, lhs, w, start=j == 0, stop=j == 2)
                    ins.then_inc(S("head_sums"), 1)
                z_products(pe, 2)
                pe.wait_ge(S("ml_squares"), 1)
                for c in range(8):
                    hh = c // 2
                    ins = mm(bank[2 + hh // 2][:, hh % 2 * T:(hh % 2 + 1) * T], ones, vc[:, c, 0:T],
                             start=c % 2 == 0, stop=c % 2 == 1)
                ins.then_inc(S("ml_sums"), 1)
                pe.wait_ge(S("ml_inverse"), 1)
                b_re, b_im = (g2(n).rearrange("p (c n) -> p c n", c=4) for n in ("b_re", "b_im"))
                c_re, c_im = (g2(n).rearrange("p (s c) -> p s c", s=16) for n in ("c_re", "c_im"))

                def states(p):
                    pe.wait_ge(S("s_ready"), p + 1)
                    for s in range(2):
                        j = 2 * p + s
                        c, r = j // 4, 32 * (j % 4)
                        dst = bank[6 + c // 2][r:r + 32, c % 2 * T:(c % 2 + 1) * T]
                        mm(dst, c_re[:, j, :], s_out[:, 0, s, :], start=True, stop=False)
                        ins = mm(dst, c_im[:, j, :], s_out[:, 1, s, :], start=False, stop=True)
                    ins.then_inc(S("c_done"), 1)

                for p in range(PAIRS):
                    if p:
                        pe.wait_ge(S("bu_ready"), 4 * p)
                    for s in range(2):
                        j = 2 * p + s
                        c, r = j // 4, 32 * (j % 4)
                        for k, w in enumerate((b_re, b_im)):
                            ins = mm(bank[2 + 2 * s + k][:, 0:TT], w[r:r + 32, c, :], us[r:r + 32, c, :], start=True, stop=True)
                        if s == 0:
                            turn(pe, ins)
                    ins.then_inc(S("bu_done"), 1)
                    z_products(pe, 1)
                    if p:
                        states(p - 1)
                states(PAIRS - 1)
            pe_at.advance((4, 5, 6), 1, None)
            ev_at.advance((4, 5, 6), 1, None)

        a10 = Area(arena)
        glu, mixed, part = a10.take(4, T), a10.take(8, T), a10.take(4, T)
        assert a10.at <= a6.at
        y5 = us[:, :, M:TT]
        combos = ((5, 6, 7), (0, 1, 2), (3, 4, 5), (6, 7, 0))
        cycle = (1, 2, 3, 4, 5, 6, 7, 0)
        QS = (3, 4, 5, 6, 7, 0) * 2 + (3, 4, 5, 6)
        with nc.Block() as block:
            @block.sync
            def _(sp):
                load(sp, (7,))
                for slots in combos[1:]:
                    load(sp, slots)
                load(sp, cycle)
                load(sp, (1, 2))
                load(sp, QS[0:6])

            @block.tensor
            def _(pe):
                def gate(q, w, b, i):
                    for n in range(2):
                        for k in range(4):
                            mm = nc.tensor.matmul(b[:, n * T:(n + 1) * T], w[:, 4 * n + k, :], y5[:, k, :],
                                                  start=k == 0, stop=k == 3)
                    return mm

                def branches(q, w, b, i):
                    if q == 0:
                        return gate(q, w, b, i)
                    for k in range(KT):
                        mm = nc.tensor.matmul(b[:, 0:T], w[:, k, :], h_ml[:, k, :], start=k == 0, stop=k == KT - 1)
                    return mm

                def onto(q, w, b, i):
                    for k in range(KT):
                        mm = nc.tensor.matmul(b[:, 0:T], w[:, k, :], mixed[:, k, :], start=k == 0, stop=k == KT - 1)
                    return mm

                project(pe, (7, 4), (0, 1), 1, gate)
                pe.wait_ge(S("s5_gated"), 1)
                for n, slots in enumerate(combos):
                    project(pe, slots, ((2, 3, 4), (5, 6, 7))[n % 2], 1, branches)
                pe.wait_ge(S("mixed"), 4)
                project(pe, cycle, range(4), 1, onto)

            @block.scalar
            def _(act):
                def sigmoids(q, b, i):
                    for n in range(2):
                        ins = nc.scalar.activation(glu[:, 2 * q + n, :], b[:, n * T:(n + 1) * T], ACT.Sigmoid,
                                                   bias=col("ssm_b_glu_2", 2 * q + n))
                    return ins
                evacuate(act, (7, 4), (0, 1), 1, sigmoids)

            @block.vector
            def _(dve):
                v = nc.vector
                for b in range(2):
                    dve.wait_ge(drained[b], ev_at.banks[b] + 1)
                vec.tell(v.tensor_tensor(y5, y5, glu, ALU.mult), S("s5_gated"))
                for n, slots in enumerate(combos):
                    def mix(q, b, i):
                        if q == 0:
                            return v.tensor_tensor(part[:, 0:2, :], b[:, :].rearrange("p (c t) -> p c t", c=2),
                                                   gs_g[:, 2 * n:2 * n + 2, :], ALU.mult)
                        return v.tensor_tensor(part[:, 1 + q, :], b[:, 0:T], gm_g[:, 2 * n + q - 1, :], ALU.mult)
                    banks = ((2, 3, 4), (5, 6, 7))[n % 2]
                    evacuate(dve, slots, banks, 1, mix)
                    for b in banks:
                        dve.wait_ge(drained[b], ev_at.banks[b] + 1)
                    vec.tell(v.tensor_tensor(mixed[:, 2 * n:2 * n + 2, :], part[:, 0:2, :], part[:, 2:4, :], ALU.add),
                             S("mixed"), n + 1)
                evacuate(dve, cycle, range(4), 1, lambda q, b, i: v.tensor_tensor(
                    x[:, q, :], x[:, q, :], b[:, 0:T], ALU.add))
                dve.wait_ge(drained[3], ev_at.banks[3] + 1)

        rms_norm(lambda k: x[:, k, :], lambda k: h[:, k, 0:T], "norm2_g_2", RMS_EPS, Area(arena).take(KT, T))
        ge = Area(arena)
        G = ge.take(P, T)
        early = ge.take(EARLY, T)
        parts = Area(arena_parts[ge.at])
        h_high = parts.take(KT, T)
        h_low = h_parts[:, :, 0:T]
        ge.at += parts.at
        expert_high = parts.take(2, D)
        chosen = ge.take(3, T)
        ap_ = Area(arena)
        qp = ap_.take(16, T)
        sc = ap_.take(2, 16, P)
        work = ap_.take(4, T)
        sv, si = ap_.take(2, 16, 16), ap_.take(16, 16)
        cand = ap_.take(8, T)
        cs, ci = ap_.take(8, 16), ap_.take(8, 16)
        which, which_f, hot = ap_.take(2, P), ap_.take(2, P), ap_.take(P, 16)
        picked = ap_.take(2, 3, P)
        tops, sums = ap_.take(8, 16), ap_.take(2, 8)
        si_u = ap_.take(2, 16, 16).bitcast(U32)
        ci_u, which_u = ci.bitcast(U32), which.bitcast(U32)

        ER = (7, 0, 1, 2, 3, 4, 5, 6)
        PEER_BANKS = (4, 5, 6, 7)

        def act_products(q, w, b, i):
            for k in range(KT):
                mm = nc.tensor.matmul(b[:, 0:T], w[:, k, :], h[:, k, 0:T], start=k == 0, stop=k == KT - 1)
            return mm

        with nc.Block() as block:
            @block.sync
            def _(sp):
                load(sp, QS[6:12])
                load(sp, QS[12:16])
                load(sp, ER)
                load(sp, ER)

            @block.tensor
            def _(pe):
                def scores(n):
                    if n >= 2:
                        pe.wait_ge(S("scores_read"), n - 1)
                    w = ring[:, 1 + n // 8, n % 8 * P:(n % 8 + 1) * P]
                    for tt in range(2):
                        mm = nc.tensor.matmul(bank[2 + n % 2][:, tt * P:(tt + 1) * P], qp[:, n, tt * P:(tt + 1) * P], w,
                                              start=True, stop=True)
                    mm.then_inc(S("scores_done"), 1)

                keys_in = [16 * (pe_at.rounds[s] + 1) for s in (1, 2)]
                for b in (2, 3):
                    pe.wait_ge(drained[b], pe_at.banks[b] + 1)
                for n in range(16):
                    project(pe, QS[n:n + 1], (n % 2,), 1, channels(T))
                    if n % 8 == 1:
                        pe.wait_ge(full[1 + n // 8], keys_in[n // 8])
                    if n:
                        b = (n - 1) % 2
                        pe.wait_ge(drained[b], pe_at.banks[b] + 1)
                        scores(n - 1)
                pe.wait_ge(drained[1], pe_at.banks[1] + 1)
                scores(15)
                pe.wait_ge(S("scores_read"), 16)
                for s in (1, 2):
                    pe.sem_inc(used[s], 1)
                pe_at.advance((1, 2), 1, None)
                for b in range(4):
                    pe.wait_ge(drained[b], pe_at.banks[b] + 1)
                    for c in range(4):
                        k = 4 * (b % 2) + c
                        mm = nc.tensor.matmul(bank[b][:, c * P:(c + 1) * P], x[:, k, b // 2 * P:(b // 2 + 1) * P], ident,
                                              start=c == 0, stop=False)
                project(pe, ER, PEER_BANKS, 1, act_products)
                for b in PEER_BANKS[0:2]:
                    pe.wait_ge(drained[b], pe_at.banks[b] + 1)
                pe.wait_ge(S("picked"), 2)
                for tt in range(2):
                    for n in range(3):
                        mm = nc.tensor.transpose(bank[4 + tt][:, n * P:(n + 1) * P], picked[:, tt, n, :], ident)
                mm.then_inc(S("chosen_t"), 1)

            @block.scalar
            def _(act):
                def read_scores(n):
                    act.wait_ge(S("scores_done"), n + 1)
                    nc.scalar.activation(sc[:, :, n, :], bank[2 + n % 2][:, 0:T].rearrange("p (a n) -> p a n", a=2),
                                         ACT.Copy).then_inc(S("scores_read"), 1)

                for n in range(16):
                    evacuate(act, QS[n:n + 1], (n % 2,), 1, lambda q, b, i: nc.scalar.activation(
                        qp[:, n, :], b[:, 0:T], ACT.Copy))
                    if n:
                        read_scores(n - 1)
                read_scores(15)
                ev_at.advance((1, 2), 1, None)
                evacuate(act, ER[0:7], PEER_BANKS, 1, lambda q, b, i: nc.scalar.activation(
                    early[:, q, :], b[:, 0:T], ACT.Gelu_apprx_tanh))
                act.wait_ge(used[ER[7]], ev_at.rounds[ER[7]] + 1)
                nc.scalar.activation(h_high, h[:, :, 0:T], ACT.Copy).then_inc(S("h_high"), 1)
                for tt in range(2):
                    act.wait_ge(S("soft_arg"), tt + 1)
                    nc.scalar.activation(tops, tops, ACT.Exp).then_inc(S("soft_exp"), 1)

            @block.gpsimd
            def _(pool):
                pool.wait_ge(S("h_high"), 1)
                poo.link(nc.gpsimd.tensor_tensor(h_low, h[:, :, 0:T], h_high.bitcast(F32), ALU.subtract))

            @block.vector
            def _(dve):
                v = nc.vector

                def step(ins):
                    vec.n += 1
                    ins.then_inc(vec.steps, 1)
                    return vec.n

                def top16(values, indices, src, width):
                    for first_row in range(0, src.shape[1], 4):
                        group = range(first_row, first_row + 4)
                        found = [step(v.max(values[:, n, 0:8], src[:, n, :])) for n in group]
                        for r, n in enumerate(group):
                            dve.wait_ge(vec.steps, found[r])
                            step(v.max_index(indices[:, n, 0:8], values[:, n, 0:8], src[:, n, :]))
                            found[r] = step(v.match_replace(work[:, r, 0:width], values[:, n, 0:8], src[:, n, :], -3e38))
                        for r, n in enumerate(group):
                            dve.wait_ge(vec.steps, found[r])
                            found[r] = step(v.max(values[:, n, 8:16], work[:, r, 0:width]))
                        for r, n in enumerate(group):
                            dve.wait_ge(vec.steps, found[r])
                            last_one = step(v.max_index(indices[:, n, 8:16], values[:, n, 8:16], work[:, r, 0:width]))
                    dve.wait_ge(vec.steps, last_one)

                for n in range(0, 16, 4):
                    dve.wait_ge(S("scores_read"), n + 4)
                    for tt in range(2):
                        top16(sv[:, tt, n:n + 4], si_u[:, tt, n:n + 4], sc[:, tt, n:n + 4], P)
                for tt in range(2):
                    vec.link(v.tensor_copy(si, si_u[:, tt]))
                    by_half = sv[:, tt].rearrange("p (h s) k -> p h s k", s=2)
                    first_s = by_half[:, :, 0, :].unsqueeze(3).broadcast_to([P, 8, 16, 16])
                    second_s = by_half[:, :, 1, :].unsqueeze(2).broadcast_to([P, 8, 16, 16])
                    vec.link(v.tensor_tensor(cand.rearrange("p h (a b) -> p h a b", a=16), first_s, second_s, ALU.add))
                    top16(cs, ci_u, cand, T)
                    vec.tell(v.tensor_tensor(tops, cs, cs[:, :, 0:1].broadcast_to([P, 8, 16]), ALU.subtract),
                             S("soft_arg"), tt + 1)
                    flat = ci_u.rearrange("p h k -> p (h k)")
                    vec.link(v.tensor_scalar(which_u[:, 0, :], flat, 4, None, ALU.logical_shift_right))
                    vec.link(v.tensor_scalar(which_u[:, 1, :], flat, 15, None, ALU.bitwise_and))
                    vec.link(v.tensor_copy(which_f, which_u))
                    ki = si.rearrange("p (h s) k -> p h s k", s=2)
                    for s in range(2):
                        vec.link(v.tensor_tensor(hot, which_f[:, s, :].unsqueeze(2).broadcast_to([P, P, 16]),
                                                 iota[:, 0:16].unsqueeze(1).broadcast_to([P, P, 16]), ALU.is_equal))
                        hot4 = hot.rearrange("p (h k) a -> p h k a", h=8)
                        vec.link(v.tensor_tensor(hot4, hot4, ki[:, :, s, :].unsqueeze(2).broadcast_to([P, 8, 16, 16]),
                                                 ALU.mult))
                        vec.link(v.tensor_reduce(picked[:, tt, s, :], hot, AX, ALU.add))
                    dve.wait_ge(S("soft_exp"), tt + 1)
                    vec.link(v.tensor_reduce(sums[:, 0, :], tops, AX, ALU.add))
                    vec.link(v.reciprocal(sums[:, 1, :], sums[:, 0, :]))
                    vec.tell(v.tensor_tensor(picked[:, tt, 2, :].rearrange("p (h k) -> p h k", h=8), tops,
                                             sums[:, 1, :].unsqueeze(2).broadcast_to([P, 8, 16]), ALU.mult),
                             S("picked"), tt + 1)
                dve.wait_ge(S("chosen_t"), 1)
                for tt in range(2):
                    ins = v.tensor_copy(chosen[:, :, tt * P:(tt + 1) * P],
                                        bank[4 + tt][:, 0:3 * P].rearrange("p (n t) -> p n t", n=3))
                vec.link(ins)

        quads = T // 4
        hots = [x[:, 4 * n:4 * n + 4, :].rearrange("p a t -> p (a t)").rearrange("p (c q n) -> p c q n", c=2, q=4)
                for n in range(2)] + [ge.take(2, 4, P)]
        with nc.Block() as block:
            def all_quads(eng, one):
                with eng.Fori(0, quads // 3) as i:
                    for b in range(3):
                        one(b, i)
                for b in range(quads % 3):
                    one(b, quads // 3)

            def of_tokens(n, i, b):
                return chosen[:, n, bass.ds(i * 12 + 4 * b, 4)].unsqueeze(2).broadcast_to([P, 4, P])

            @block.vector
            def _(dve):
                keys = iota.unsqueeze(1).broadcast_to([P, 4, P])

                def one(b, i):
                    dve.wait_ge(S("rows_free"), i * 3 + (b + 1))
                    nc.vector.tensor_tensor(hots[b][:, 1], keys, of_tokens(1, i, b), ALU.is_equal)
                    nc.vector.tensor_tensor(hots[b][:, 0], keys, of_tokens(0, i, b), ALU.is_equal)\
                        .then_inc(S("rows_made"), 1)
                all_quads(dve, one)

            @block.gpsimd
            def _(pool):
                def one(b, i):
                    pool.wait_ge(S("rows_made"), i * 3 + (b + 1))
                    nc.gpsimd.tensor_tensor(hots[b][:, 0], hots[b][:, 0], of_tokens(2, i, b), ALU.mult)\
                        .then_inc(S("rows_ready"), 1)
                all_quads(pool, one)

            @block.tensor
            def _(pe):
                def one(b, i):
                    pe.wait_ge(S("rows_ready"), i * 3 + (b + 1))
                    pe.wait_ge(S("gates_read"), i * 3 + (b + 1))
                    for q in range(4):
                        mm = nc.tensor.matmul(bank[4 + b][:, q * P:(q + 1) * P], hots[b][:, 0, q, :], hots[b][:, 1, q, :],
                                              start=True, stop=True)
                    mm.then_inc(S("rows_free"), 1)
                pe.sem_inc(S("rows_free"), 3)
                all_quads(pe, one)

            @block.scalar
            def _(act):
                def one(b, i):
                    act.wait_ge(S("rows_free"), i * 3 + (b + 4))
                    nc.scalar.activation(G[:, :, bass.ds(i * 12 + 4 * b, 4)],
                                         bank[4 + b][:, :].rearrange("p (q n) -> p n q", q=4), ACT.Copy)\
                        .then_inc(S("gates_read"), 1)
                act.sem_inc(S("gates_read"), 3)
                all_quads(act, one)

        high = expert_high
        low = ring_parts
        gate_high, gate_low = x_parts[:, 0:4, :], x_parts[:, 4:8, :]
        rounds = (P - EARLY) // 8
        slot_base = {s: pe_at.rounds[s] for s in ER}
        bank_base = {b: pe_at.banks[b] - 2 for b in PEER_BANKS}
        HALF = D // 2

        def uses(m, i, ahead=0):
            return i * 2 + (slot_base[ER[m % 8]] + m // 8 + ahead)

        with nc.Block() as block:
            @block.sync
            def _(sp):
                load(sp, ER, 2 * rounds)

            @block.tensor
            def _(pe):
                mm = nc.tensor.matmul

                def experts(m, i, s):
                    slot, b = ER[m % 8], PEER_BANKS[s % 4]
                    pe.wait_ge(drained[b], i * 2 + (bank_base[b] + s // 4 + 3))
                    for k in range(KT):
                        if k % 4 == 0:
                            pe.wait_ge(S("low"), i * 32 + (2 * m + k // 4 + 1))
                        w = slice(k * P, (k + 1) * P)
                        mm(bank[b][:, 0:T], high[:, m % 2, w], h_high[:, k, :], start=k == 0, stop=False)
                        mm(bank[b][:, 0:T], high[:, m % 2, w], h_low[:, k, :], start=False, stop=False)
                        ins = mm(bank[b][:, 0:T], low[:, slot, w], h_high[:, k, :], start=False, stop=k == KT - 1)
                        if k == 3:
                            ins.then_inc(S("half_used"), 1)
                    ins.then_inc(used[slot], 1)

                def values(m, i, s, last_one=False):
                    slot = ER[m % 8]
                    pe.wait_ge(S("gated"), i * 8 + (s + 2))
                    for half in range(2):
                        pe.wait_ge(S("low"), i * 32 + (2 * m + half + 1))
                        w = slice(half * HALF, (half + 1) * HALF)
                        for tt in range(2):
                            b, t = bank[2 * tt + half][:, :], slice(tt * P, (tt + 1) * P)
                            mm(b, gate_high[:, s % 4, t], high[:, m % 2, w], start=False, stop=False)
                            mm(b, gate_high[:, s % 4, t], low[:, slot, w], start=False, stop=False)
                            ins = mm(b, gate_low[:, s % 4, t], high[:, m % 2, w], start=False, stop=last_one)
                        if half == 0:
                            ins.then_inc(S("half_used"), 1)
                    ins.then_inc(used[slot], 1)

                pe.sem_inc(S("half_used"), 2)
                with pe.Fori(0, rounds) as i:
                    for s in range(8):
                        experts(2 * s, i, s)
                        values(2 * s + 1, i, s)
                for s in range(8):
                    values(s, rounds, s, s == 7)

            @block.scalar
            def _(act):
                def split_high(m, i):
                    slot = ER[m % 8]
                    act.wait_ge(full[slot], i * 32 + 16 * (slot_base[slot] + m // 8 + 1))
                    act.wait_ge(S("half_used"), i * 16 + (m + 1))
                    nc.scalar.activation(high[:, m % 2, 0:HALF], ring[:, slot, 0:HALF], ACT.Copy).then_inc(S("high"), 1)
                    act.wait_ge(used[ER[(m - 2) % 8]], uses(m - 2, i, 1))
                    nc.scalar.activation(high[:, m % 2, HALF:D], ring[:, slot, HALF:D], ACT.Copy).then_inc(S("high"), 1)

                def gelu(s, i):
                    act.wait_ge(used[ER[(2 * s - 2) % 8]], uses(2 * s - 2, i, 1))
                    act.wait_ge(S("gated"), i * 8 + (s + 1))
                    b = PEER_BANKS[(s - 1) % 4]
                    nc.scalar.activation(early[:, (s - 1) % 8, :], bank[b][:, 0:T], ACT.Gelu_apprx_tanh)\
                        .then_inc(drained[b], 1)

                with act.Fori(0, rounds) as i:
                    for s in range(8):
                        split_high(2 * s, i)
                        gelu(s, i)
                        split_high(2 * s + 1, i)
                gelu(0, rounds)
                for m in range(8):
                    split_high(m, rounds)

            @block.vector
            def _(dve):
                def split_low(m, i):
                    for half in range(2):
                        dve.wait_ge(S("high"), i * 32 + (2 * m + half + 1))
                        w = slice(half * HALF, (half + 1) * HALF)
                        nc.vector.tensor_tensor(low[:, ER[m % 8], w], ring[:, ER[m % 8], w],
                                                high[:, m % 2, w].bitcast(F32), ALU.subtract).then_inc(S("low"), 1)

                with dve.Fori(0, rounds) as i:
                    for m in range(16):
                        split_low(m, i)
                for m in range(8):
                    split_low(m, rounds)

            @block.gpsimd
            def _(pool):
                p = nc.gpsimd
                pool.sem_inc(S("gated"), 1)

                def gate(s, i, m):
                    b = PEER_BANKS[s % 4]
                    pool.wait_ge(drained[b], i * 2 + (bank_base[b] + s // 4 + 2))
                    pool.wait_ge(used[ER[m % 8]], uses(m, i, 1))
                    e = early[:, s, :]
                    j = i * 8 + s
                    g = G[:, j, :] if isinstance(j, int) else G[:, bass.ds(j, 1), :].rearrange("p a t -> p (a t)")
                    p.tensor_tensor(e, e, g, ALU.mult).then_inc(S("gate_step"), 1)
                    pool.wait_ge(S("gate_step"), i * 16 + (2 * s + 1))
                    p.tensor_tensor(gate_high[:, s % 4, :].rearrange("p (a t) -> p a t", a=2),
                                    e.rearrange("p (a t) -> p a t", a=2),
                                    ones.unsqueeze(1).broadcast_to([P, 2, P]), ALU.mult).then_inc(S("gate_step"), 1)
                    pool.wait_ge(S("gate_step"), i * 16 + (2 * s + 2))
                    p.tensor_tensor(gate_low[:, s % 4, :], e, gate_high[:, s % 4, :].bitcast(F32), ALU.subtract)\
                        .then_inc(S("gated"), 1)

                with pool.Fori(0, rounds) as i:
                    for s in range(8):
                        gate(s, i, 2 * s + 1 - 8)
                for s in range(8):
                    gate(s, rounds, s - 4 if s >= 4 else 2 * s - 7)

        a_end = Area(arena)
        square, result, stat = a_end.take(4, 512), a_end.take(4, 512), a_end.take(2, 4)
        last_g = a_end.take(D)
        with nc.Block() as block:
            @block.scalar
            def _(act):
                act.dma_start(last_g, last).then_inc(S("last_in"), 16)
                for b in range(4):
                    nc.scalar.activation(square[:, b, :], bank[b][:, :], ACT.Square).then_inc(S("last_squares"), 1)
                act.wait_ge(S("last_mean"), 1)
                nc.scalar.activation(stat[:, :, 1:2], stat[:, :, 1:2], ACT.Sqrt).then_inc(S("last_root"), 1)

            @block.vector
            def _(dve):
                v = nc.vector
                dve.wait_ge(S("last_squares"), 4)
                vec.link(v.tensor_reduce(stat[:, :, 0:1], square.rearrange("p (t c) n -> p t (c n)", t=2), AX, ALU.add))
                vec.link(v.tensor_scalar(stat[:, :, 1:2], stat[:, :, 0:1], 1.0 / D, RMS_EPS, ALU.mult, ALU.add))
                vec.tell(v.reciprocal(stat[:, :, 1:2], stat[:, :, 1:2]), S("last_mean"))
                dve.wait_ge(S("last_root"), 1)
                dve.wait_ge(S("last_in"), 16)
                for b in range(4):
                    c = b % 2 * 512
                    v.scalar_tensor_tensor(result[:, b, :], bank[b][:, :], stat[:, b // 2, 1:2], last_g[:, c:c + 512],
                                           ALU.mult, ALU.mult).then_inc(S("result"), 1)

            @block.sync
            def _(sp):
                for b in range(4):
                    c = b % 2 * 512
                    sp.wait_ge(S("result"), b + 1)
                    sp.dma_start(out[b // 2 * P:(b // 2 + 1) * P, c:c + 512], result[:, b, :]).then_inc(S("written"), 16)
                sp.wait_ge(S("written"), 64)


def _blocks(w):
    k, n = w.shape
    return w.reshape(k // P, P, n // P, P).transpose(2, 1, 0, 3).reshape(n // P, P, k)


def _columns(v):
    return v.reshape(-1, P).T


def lay_out(a):
    import numpy as np

    f32 = np.float32
    a = {k: np.asarray(v) for k, v in a.items()}
    w_in, w_in2 = a["w_in"][0], a["w_in_2"][0]
    sc, sb, rw, sg, gate = 0, 768, 1536, 2560, 3072
    order = [w_in[:, rw:rw + 1024], w_in[:, sc:sc + 768], w_in[:, sb:sb + 512], w_in[:, sg:sg + 256],
             w_in[:, sb + 512:sb + 768], w_in[:, sg + 256:sg + 512], w_in[:, gate:]]
    parts = [_blocks(w) for w in order]
    outs = np.stack([a[n][0] for n in ("sc_out", "sb_out", "rw_out", "sg_out")])
    parts.append(outs.reshape(4, 2, P, KT, P).transpose(3, 2, 0, 1, 4).reshape(KT, P, D))
    parts.append(_blocks(a["w_o"][0]))
    up = _blocks(a["w_up"][0])
    gv, down = np.stack([up[:FT], up[FT:]], 1), a["w_down"][0].reshape(FT, 1, P, D)
    parts += [gv[:2].reshape(4, P, D), np.concatenate([gv[2:], down[:-2]], 1).reshape(-1, P, D), down[-2:, 0]]
    parts.append(_blocks(w_in2[:, :1536]))
    for n in ("ml_wq_2", "ml_wk_2", "ml_wv_2"):
        w = a[n][0]
        m = np.zeros((D // 4, 4, D // 4, 4), f32)
        r = np.arange(D // 4)
        m[r, :, r, :] = w
        m = m.reshape(KT, P, KT, P)
        parts.append(np.stack([m[k, :, k, :] for k in range(KT)], 1).reshape(1, P, D))
    parts.append(_blocks(w_in2[:, 1536:]))
    glu = a["ssm_w_glu_2"][0].reshape(4, P, 2, 2, P).transpose(2, 1, 3, 0, 4).reshape(2, P, D)
    parts.append(glu)
    ssm = a["w_ssm_out_2"][0].reshape(4, P, 4, 2, P).transpose(2, 1, 3, 0, 4).reshape(4, P, D)
    ml, wo = _blocks(a["w_ml_out_2"][0]), _blocks(a["w_out_2"][0])
    for n in range(4):
        parts += [ssm[n:n + 1], ml[2 * n:2 * n + 2]]
    parts.append(wo)
    keys = a["peer_sub_keys_2"][0].reshape(16, P, P).transpose(2, 0, 1).reshape(P, 2, D)
    parts.append(keys.transpose(1, 0, 2))
    parts.append(_blocks(a["peer_w_q_2"][0]))
    u = a["peer_u_2"][0].reshape(P, P, KT, P).transpose(1, 3, 2, 0).reshape(P, P, D)
    v = a["peer_v_2"][0].reshape(P, P, D).transpose(1, 0, 2)
    parts += [u[:EARLY], np.stack([u[EARLY:], v[:-EARLY]], 1).reshape(-1, P, D), v[-EARLY:]]
    stream = np.concatenate(parts)

    cols = {}
    for n in ("mix_norm_g", "gate_b", "rw_mu", "rw_w0", "rw_a0", "rw_k_k", "rw_k_a", "rw_gn_g", "rw_gn_b",
              "ffn_norm_g", "norm1_g_2", "ssm_d_2", "ssm_b_glu_2", "ml_conv_b_2", "ml_norm_g_2", "ml_skip_2",
              "norm2_g_2"):
        cols[n] = _columns(a[n][0])
    cols["final_norm_g"] = _columns(a["final_norm_g"])
    cols["rw_r_k"] = _columns(a["rw_r_k"][0].reshape(-1))
    for n in ("sc_conv_w", "ffn_conv_w", "ml_conv_w_2"):
        cols[n] = np.concatenate([_columns(w) for w in a[n][0]], 1)
    cols["ssm_a_re_2"] = _columns(a["ssm_a_re_2"][0].reshape(-1))
    cols["ssm_a_im_2"] = _columns(a["ssm_a_im_2"][0].reshape(-1))
    cols["ssm_log_dt_2"] = _columns(np.repeat(a["ssm_log_dt_2"][0], 64))
    b_if = np.zeros((P, 2), f32)
    b_if[:4, 0], b_if[:4, 1] = a["ml_b_if_2"][0][:4], a["ml_b_if_2"][0][4:]
    cols["ml_b_if_2"] = b_if
    assert {k: v.shape[1] for k, v in cols.items()} == COLS
    cols = np.concatenate([cols[k] for k in COLS], 1)

    lora = np.concatenate([np.concatenate([a["rw_w2"][0], a["rw_a2"][0]], 0), a["rw_g2"][0]], 1)
    ln_rows = np.broadcast_to(np.concatenate([a["sg_ln_g"][0], a["sg_ln_b"][0]])[None], (P, 512))
    sgw = a["sg_w"][0].transpose(2, 0, 1).reshape(P, 512)
    sgb = np.tile(np.repeat(a["sg_b"][0], 64, axis=0).reshape(2, P, 1, P), (1, 1, 2, 1)).transpose(1, 0, 2, 3)
    i = np.arange(P)
    s_, t_ = i[:, None], i[None, :]
    t2 = np.arange(T)[None, :]
    same = (s_ // 64) == (t_ // 64)
    masks = [same, same & (s_ < t_), same & (s_ <= t_)]
    levels = []
    for w in (1, 2, 4, 8, 16, 32):
        m = (s_ // (2 * w) == t_ // (2 * w)) & (s_ // w % 2 == 1) & (t_ // w % 2 == 0)
        levels.append(m)
    masks += levels[:1] + [m.T for m in levels]
    masks += [s_ > t_, s_ <= t_, s_ < t2, s_ < t2[:, P:] - P, (t2 % 64 != 0) & (s_ >= 0)]
    eye2 = np.concatenate([np.eye(64), np.eye(64)], 0)
    first = [lora, ln_rows, sgw, sgb.reshape(P, 512)] + [m.astype(f32) for m in masks] + [eye2]
    first = np.concatenate([x.astype(f32, copy=False) for x in first], 1)
    assert first.shape[1] == sum(FIRST.values())

    bmats, cmats = [], []
    for n in ("ssm_b_re_2", "ssm_b_im_2"):
        b = a[n][0].reshape(4, 4, 2, 64, 16)
        m = np.zeros((4, 2, 16, 4, 2, 64), f32)
        for g in range(2):
            m[:, g, :, :, g, :] = b[:, :, g].transpose(1, 3, 0, 2)
        bmats.append(m.reshape(P, 512))
    for n in ("ssm_c_re_2", "ssm_c_im_2"):
        c = a[n][0].reshape(16, 2, 16, 64)
        m = np.zeros((2, 64, 16, 2, 16), f32)
        for g in range(2):
            m[g, :, :, g, :] = c[:, g].transpose(2, 0, 1)
        cmats.append(m.reshape(P, 512))
    wif = a["ml_w_if_2"][0].reshape(24, P, 8).transpose(1, 0, 2).reshape(P, 192)
    neg = [np.where(s_ <= t2, 0.0, -1e30), np.where(s_ + P <= t2, 0.0, -1e30)]
    sel = np.zeros((P, 4, P))
    sel[i[:4], i[:4]] = 1
    second = np.concatenate([x.astype(f32, copy=False) for x in bmats + cmats + [wif] + neg + [sel.reshape(P, 512)]], 1)
    assert second.shape[1] == sum(SECOND.values())
    last = np.broadcast_to(a["final_norm_g_2"][None], (P, D))
    keep = np.concatenate([np.eye(P), np.ones((P, P)), np.broadcast_to(i[None], (P, P))], 1).astype(f32)
    return {
        "stream": stream, "x_t": a["x"][0].T.reshape(KT, P, T).transpose(1, 0, 2),
        "meta_t": a["meta_tokens_2"].T.reshape(KT, P, M).transpose(1, 0, 2),
        "cols": cols, "first": first, "second": second, "last": last, "keep": keep,
    }


def kernel(**inputs):
    import numpy as np
    import concourse.bacc as bacc
    from concourse.bass_utils import run_bass_kernel_spmd

    arrays = {k: np.ascontiguousarray(v) for k, v in lay_out(inputs).items()}
    nc = bacc.Bacc("TRN2", target_bir_lowering=False, num_devices=1)
    args = {n: nc.dram_tensor(n, a.shape, mybir.dt.from_np(a.dtype), kind="ExternalInput").ap()
            for n, a in arrays.items()}
    out = nc.dram_tensor("out", (T, D), F32, kind="ExternalOutput").ap()
    build(nc, out, **args)
    r = run_bass_kernel_spmd(nc, [arrays], core_ids=[0])
    return r.results[0]["out"].reshape(1, T, D)
```

```python
from contextlib import ExitStack

import concourse.bass as bass
from concourse import mybir

P = 128
T = 256
M = 16
TT = T + M
D = 1024
KT = D // P
FT = 2816 // P
EARLY = 8
ARENA_PARTS = (0, 5888, 17152, 25344, (P + EARLY) * T)
SLOTS = 8
RMS_EPS = 1e-6
LN_EPS = 1e-5
GN_EPS = 64e-5
DECAY_SCALE = 0.6065306597126334
TWO_PI = 6.283185307179586

ALU = mybir.AluOpType
ACT = mybir.ActivationFunctionType
F32 = mybir.dt.float32
F32R = mybir.dt.float32r
U32 = mybir.dt.uint32
AX = mybir.AxisListType.X

COLS = {"mix_norm_g": 8, "gate_b": 32, "rw_mu": 8, "rw_w0": 2, "rw_a0": 2, "rw_k_k": 2, "rw_k_a": 2,
        "rw_gn_g": 2, "rw_gn_b": 2, "ffn_norm_g": 8, "norm1_g_2": 8, "ssm_d_2": 4, "ssm_b_glu_2": 4,
        "ml_conv_b_2": 8, "ml_norm_g_2": 8, "ml_skip_2": 8, "norm2_g_2": 8, "final_norm_g": 8, "rw_r_k": 2,
        "sc_conv_w": 6, "ffn_conv_w": 3 * 44, "ml_conv_w_2": 32, "ssm_a_re_2": 16, "ssm_a_im_2": 16,
        "ssm_log_dt_2": 16, "ml_b_if_2": 2}
FIRST = {"lora": 512, "ln_rows": 512, "sgw": 512, "sgb": 512, "same": P, "upper": P, "upper_eq": P,
         "level0": P, "levels_t": 6 * P, "after": P, "causal": P, "sb_mask0": T, "sb_mask1": P, "carry": T,
         "eye2": 64}
SECOND = {"b_re": 512, "b_im": 512, "c_re": 512, "c_im": 512, "w_if": 192, "neg0": T, "neg1": T, "sel": 512}


def offsets(sizes):
    out, at = {}, 0
    for name, n in sizes.items():
        out[name] = at
        at += n
    return out, at


class Area:

    def __init__(self, tensor, at=0):
        self.tensor, self.at = tensor, at

    def take(self, *dims):
        n = 1
        for d in dims:
            n *= d
        v = self.tensor[:, self.at:self.at + n]
        self.at += n
        assert self.at <= self.tensor.shape[1], self.at
        if len(dims) == 2:
            v = v.rearrange("p (a b) -> p a b", a=dims[0])
        if len(dims) == 3:
            v = v.rearrange("p (a b c) -> p a b c", a=dims[0], b=dims[1])
        return v


class Ring:

    def __init__(self):
        self.rounds = [0] * SLOTS
        self.block = 0


class Own:

    def __init__(self, eng, steps):
        self.eng, self.steps, self.n = eng, steps, 0

    def link(self, ins):
        self.n += 1
        ins.then_inc(self.steps, 1)
        self.eng.wait_ge(self.steps, self.n)

    def tell(self, ins, sem, value=1):
        ins.then_inc(sem, 1)
        self.eng.wait_ge(sem, value)


def build(nc, out, stream, x_t, meta_t, cols, first, second, last, keep):
    with ExitStack() as ctx:
        sems = {}

        def S(name):
            if name not in sems:
                sems[name] = ctx.enter_context(nc.semaphore(name))
            return sems[name]

        def sb(name, shape, dt=F32):
            return ctx.enter_context(nc.sbuf_tensor(name, shape, dt))

        def split_place(name, shape, starts=(0,)):
            with nc.sbuf_tensor(name, shape, F32) as whole:
                pass
            if len(starts) == 1:
                return whole, ctx.enter_context(nc.sbuf_tensor(name + "_parts", shape, F32R))
            ends = list(starts[1:]) + [shape[1]]
            return whole, {a: ctx.enter_context(nc.sbuf_tensor(f"{name}_parts{a}", [shape[0], b - a], F32R))
                           for a, b in zip(starts, ends)}

        ring, ring_parts = split_place("ring", [P, SLOTS, D])
        par = sb("par", [P, sum(COLS.values())])
        cst = sb("cst", [P, 3 * P])
        x, x_parts = split_place("x", [P, KT, T])
        h, h_parts = split_place("h", [P, KT, TT])
        scale = sb("scale", [P, TT])
        spare = sb("spare", [P, 1])
        arena, arena_parts = split_place("arena", [P, 38912], ARENA_PARTS)
        bank = [ctx.enter_context(nc.psum_tensor(f"bank{i}", [P, 512], F32)) for i in range(8)]
        ident, ones, iota = cst[:, 0:P], cst[:, P:2 * P], cst[:, 2 * P:3 * P]
        at, _ = offsets(COLS)

        def col(name, i):
            return par[:, at[name] + i:at[name] + i + 1]

        full = [S(f"slot_full{s}") for s in range(SLOTS)]
        used = [S(f"slot_used{s}") for s in range(SLOTS)]
        drained = [S(f"bank_free{b}") for b in range(8)]
        fill = Ring()
        vec, sca, poo = Own(nc.vector, S("vector_step")), Own(nc.scalar, S("scalar_step")), Own(nc.gpsimd, S("pool_step"))

        def load(sp, slots, rounds=1):
            n, base = len(slots), fill.block

            def one(i):
                for q, s in enumerate(slots):
                    sp.wait_ge(used[s], fill.rounds[s] + i) if fill.rounds[s] else None
                    src = stream[bass.ds(base + i * n + q, 1)].rearrange("a p n -> (a p) n")
                    sp.dma_start(ring[:, s, :], src).then_inc(full[s], 16)

            if rounds == 1:
                one(0)
            else:
                assert all(fill.rounds[s] for s in slots)
                with sp.Fori(0, rounds) as i:
                    one(i)
            for s in slots:
                fill.rounds[s] += rounds
            fill.block += n * rounds

        class Tiles:

            def __init__(self):
                self.rounds = [0] * SLOTS
                self.banks = [0] * 8

            def advance(self, slots, rounds, banks):
                for q, s in enumerate(slots):
                    self.rounds[s] += rounds
                    if banks:
                        self.banks[banks[q % len(banks)]] += rounds

        pe_at, ev_at = Tiles(), Tiles()

        def use_of(banks, q, n):
            b = banks[q % len(banks)]
            mine = [r for r in range(n) if banks[r % len(banks)] == b]
            return b, len(mine), mine.index(q)

        def project(pe, slots, banks, rounds, mats):
            def one(i):
                for q, s in enumerate(slots):
                    b, per, before = use_of(banks, q, len(slots))
                    pe.wait_ge(full[s], (i + pe_at.rounds[s] + 1) * 16)
                    pe.wait_ge(drained[b], i * per + pe_at.banks[b] + before + 1)
                    mats(q, ring[:, s, :].rearrange("p (k n) -> p k n", n=P), bank[b], i).then_inc(used[s], 1)

            if rounds == 1:
                one(0)
            else:
                with pe.Fori(0, rounds) as i:
                    one(i)
            pe_at.advance(slots, rounds, banks)

        def evacuate(eng, slots, banks, rounds, take):
            def one(i):
                for q, s in enumerate(slots):
                    b, _, _ = use_of(banks, q, len(slots))
                    eng.wait_ge(used[s], i + ev_at.rounds[s] + 1)
                    take(q, bank[b], i).then_inc(drained[b], 1)

            if rounds == 1:
                one(0)
            else:
                with eng.Fori(0, rounds) as i:
                    one(i)
            ev_at.advance(slots, rounds, banks)

        def channels(width, lo=0):
            def mats(q, w, b, i):
                for k in range(KT):
                    mm = nc.tensor.matmul(b[:, 0:width], w[:, k, :], h[:, k, lo:lo + width],
                                          start=k == 0, stop=k == KT - 1)
                return mm
            return mats

        def tokens(q, w, b, i):
            for tt in range(2):
                for k in range(KT):
                    mm = nc.tensor.matmul(b[:, tt * P:(tt + 1) * P], h[:, k, tt * P:(tt + 1) * P], w[:, k, :],
                                          start=k == 0, stop=k == KT - 1)
            return mm

        split = {"blocks": 0, "h": 0}
        low = ring_parts

        def part_high(act, high, s, filled):
            act.wait_ge(full[s], filled * 16)
            nc.scalar.activation(high[:, s, :], ring[:, s, :], ACT.Copy).then_inc(S("high"), 1)

        def part_low(eng, ns, high, s, number):
            eng.wait_ge(S("high"), number)
            ns.tensor_tensor(low[:, s, :], ring[:, s, :], high[:, s, :].bitcast(F32), ALU.subtract)\
                .then_inc(S("low"), 1)

        def three(dst, stationary, moving, first, last_one):
            nc.tensor.matmul(dst, stationary[0], moving[0], start=first, stop=False)
            nc.tensor.matmul(dst, stationary[0], moving[1], start=False, stop=False)
            return nc.tensor.matmul(dst, stationary[1], moving[0], start=False, stop=last_one)

        normed = {"n": 0}

        def rms_norm(src, dst, gain, eps, squares, width=T, beside=None):
            n = normed["n"]
            normed["n"] += 1
            sq, total, mean, root = S("norm_squares"), S("norm_total"), S("norm_mean"), S("norm_root")
            with nc.Block() as block:
                @block.scalar
                def _(act):
                    for k in range(4):
                        nc.scalar.activation(squares[:, k, 0:width], src(k), ACT.Square).then_inc(sca.steps, 1)
                    sca.n += 4
                    if beside:
                        beside[0](act)
                    nc.scalar.activation(spare[:], ones[:, 0:1], ACT.Sqrt)
                    act.wait_ge(mean, n + 1)
                    nc.scalar.activation(scale[:, 0:width], scale[:, 0:width], ACT.Sqrt).then_inc(root, 1)

                @block.tensor
                def _(pe):
                    for k in range(4):
                        pe.wait_ge(sq, n * 4 + k + 1)
                        mm = nc.tensor.matmul(bank[7][:, 0:width], ones, squares[:, 4 + k, 0:width],
                                              start=k == 0, stop=k == 3)
                    mm.then_inc(total, 1)

                @block.vector
                def _(dve):
                    for k in range(4, KT):
                        ins = nc.vector.tensor_tensor(squares[:, k, 0:width], src(k), src(k), ALU.mult)
                    vec.link(ins)
                    for k in range(4):
                        dve.wait_ge(sca.steps, sca.n - 3 + k)
                        nc.vector.tensor_tensor(squares[:, 4 + k, 0:width], squares[:, 4 + k, 0:width],
                                                squares[:, k, 0:width], ALU.add).then_inc(sq, 1)
                    if beside:
                        beside[1](dve)
                    dve.wait_ge(total, n + 1)
                    vec.link(nc.vector.tensor_scalar(scale[:, 0:width], bank[7][:, 0:width], 1.0 / D, eps,
                                                     ALU.mult, ALU.add))
                    vec.tell(nc.vector.reciprocal(scale[:, 0:width], scale[:, 0:width]), mean, n + 1)
                    dve.wait_ge(root, n + 1)
                    for k in range(KT):
                        last_one = nc.vector.scalar_tensor_tensor(dst(k), src(k), col(gain, k), scale[:, 0:width],
                                                                  ALU.mult, ALU.mult)
                    vec.link(last_one)

        a1 = Area(arena)
        z = a1.take(20, T)
        v_sb, v_sg = a1.take(2, T), a1.take(2, T)
        gates = a1.take(32, T)
        f_at, f_size = offsets(FIRST)
        fst = a1.take(f_size)
        y = a1.take(8, T)
        scratch_at = a1.at
        squares = Area(arena, scratch_at).take(KT, TT)

        def f(name, n=None):
            return fst[:, f_at[name]:f_at[name] + (n or FIRST[name])]

        with nc.Block() as block:
            @block.sync
            def _(sp):
                sp.dma_start(x[:], x_t).then_inc(S("inputs_in"), 16)
                load(sp, range(SLOTS))

            @block.scalar
            def _(act):
                act.dma_start(cst[:], keep).then_inc(S("inputs_in"), 16)
                act.dma_start(par[:], cols).then_inc(S("inputs_in"), 16)
                act.wait_ge(S("inputs_in"), 48)

            @block.vector
            def _(dve):
                for b in range(8):
                    dve.sem_inc(drained[b], 1)

        AHEAD = 3
        proj_high = Area(arena_parts[5888], 256).take(SLOTS, D)
        hp = Area(arena_parts[25344])
        h1_high, h1_low = hp.take(KT, T), hp.take(KT, T)

        def proj_part_high(act, n, i=0):
            if not (isinstance(i, int) and i * 8 + n >= 24):
                part_high(act, proj_high, n % 8, i + n // 8 + 1)

        rms_norm(lambda k: x[:, k, :], lambda k: h[:, k, 0:T], "mix_norm_g", RMS_EPS, squares,
                 beside=(lambda act: [proj_part_high(act, n) for n in range(AHEAD)], lambda dve: None))

        with nc.Block() as block:
            @block.sync
            def _(sp):
                sp.dma_start(fst, first).then_inc(S("inputs_in"), 16)
                load(sp, range(SLOTS), 2)
                load(sp, range(4))
                sp.wait_ge(S("inputs_in"), 64)

            @block.tensor
            def _(pe):
                def blocks(n, i):
                    b = bank[n % 4]
                    pe.wait_ge(S("low"), i * 8 + (n + 1))
                    pe.wait_ge(drained[n % 4], i * 2 + (n // 4 + 1))
                    for k in range(KT):
                        w = slice(k * P, (k + 1) * P)
                        block_k = (proj_high[:, n, w], low[:, n, w])
                        if isinstance(i, int) and n >= 4:
                            for tt in range(2):
                                t = slice(tt * P, (tt + 1) * P)
                                ins = three(bank[4 * tt + n % 4][:, 0:P], (h1_high[:, k, t], h1_low[:, k, t]), block_k,
                                            k == 0, k == KT - 1)
                        else:
                            ins = three(b[:, 0:T], block_k, (h1_high[:, k, :], h1_low[:, k, :]), k == 0, k == KT - 1)
                    ins.then_inc(used[n], 1)

                for half in range(2):
                    pe.wait_ge(S("h_parts"), half + 1)
                with pe.Fori(0, 2) as i:
                    for n in range(8):
                        blocks(n, i)
                for n in range(8):
                    blocks(n, 2)
                pe_at.advance(range(8), 3, range(4))

            @block.vector
            def _(dve):
                for half in range(2):
                    k = slice(4 * half, 4 * half + 4)
                    dve.wait_ge(S("h_rounded"), half + 1)
                    nc.vector.tensor_tensor(h1_low[:, k, :], h[:, k, 0:T], h1_high[:, k, :].bitcast(F32), ALU.subtract)\
                        .then_inc(S("h_parts"), 1)
                with dve.Fori(0, 3) as i:
                    for n in range(8):
                        part_low(dve, nc.vector, proj_high, n, i * 8 + (n + 1))

            @block.scalar
            def _(act):
                def read(n, i):
                    act.wait_ge(used[n], i + 1)
                    b = bank[n % 4]
                    if not isinstance(i, int):
                        ins = nc.scalar.activation(z[:, bass.ds(i * 8 + n, 1), :].rearrange("p a t -> p (a t)"),
                                                   b[:, 0:T], ACT.Copy)
                    elif n < 4:
                        ins = nc.scalar.activation(z[:, 16 + n, :], b[:, 0:T], ACT.Copy)
                    else:
                        for tt in range(2):
                            ins = nc.scalar.activation((v_sb if n < 6 else v_sg)[:, tt, n % 2 * P:(n % 2 + 1) * P],
                                                       bank[4 * tt + n % 4][:, 0:P], ACT.Copy)
                    ins.then_inc(drained[n % 4], 1)

                for half in range(2):
                    k = slice(4 * half, 4 * half + 4)
                    nc.scalar.activation(h1_high[:, k, :], h[:, k, 0:T], ACT.Copy).then_inc(S("h_rounded"), 1)
                with act.Fori(0, 2) as i:
                    for n in range(8):
                        proj_part_high(act, n + AHEAD, i)
                        read(n, i)
                for n in range(8):
                    proj_part_high(act, n + AHEAD, 2)
                    read(n, 2)
                ev_at.advance(range(8), 3, range(4))
            split["blocks"] += 24
            split["h"] += 2

        a2 = Area(arena, scratch_at)
        shift = a2.take(8, T)
        a_t, b_t, k_t, r_t = (shift[:, 2 * i:2 * i + 2, :] for i in range(4))
        lora_h = a2.take(T)
        w_sig, cum, d_inv, d_prev, kk, kk2, kmod, a_sig, decay, g_rw, bonus = (a2.take(2, T) for _ in range(11))
        tm = a2.take(4, 2, T)
        pairs_at = a2.at
        X, XT, Z, NT, MT, MTak, MTrb, MTrk = (a2.take(8, P) for _ in range(8))
        a3 = Area(arena, pairs_at)
        sb_l, sb_b, sb_k = a3.take(1536), a3.take(1536), a3.take(1536)
        sg_d, sg_q, sg_st = a3.take(2, T), a3.take(2, T), a3.take(8)
        sg_wt = a3.take(4, P)
        a4 = Area(arena, scratch_at + 2048 + T)
        AM, GH = a4.take(8, P), a4.take(8, P)
        n0, phi = a4.take(8, 64), a4.take(8, 64)
        assert a4.at <= scratch_at + 2048 + T + 7 * 512
        rp, y0, yd2, state, sc_c, sc_t = X[:, 0:4, :], X[:, 4:8, :], Z[:, 0:4, :], NT[:, 0, :], y[:, 6:8, :], Z
        rp, y0, yd2 = (v.rearrange("p a b -> p (a b)").rearrange("p (c t) -> p c t", c=2) for v in (rp, y0, yd2))
        st2 = NT.rearrange("p a b -> p (a b)")[:, 0:256].rearrange("p (n c v) -> p n c v", n=2, c=2)
        stp = NT.rearrange("p a b -> p (a b)")[:, 256:384].rearrange("p (c v) -> p c v", c=2)
        B3 = {"p": P, "h": 4}
        r_z, k_z, v_z, g_z = z[:, 0:2, :], z[:, 2:4, :], z[:, 4:6, :], z[:, 7, :]
        q_z, kk_z, u_z = z[:, 14:16, :], z[:, 16:18, :], z[:, 18:20, :]
        LEVELS = 5
        turns = {"n": 0}
        gate_n = {"pe": 0, "act": 0}

        def turn(pe, ins):
            turns["n"] += 1
            ins.then_inc(S("tensor_turn"), 1)
            pe.wait_ge(S("tensor_turn"), turns["n"])

        def four(m):
            return m.unsqueeze(1).broadcast_to([P, 4, m.shape[1]])

        def eight(m):
            return m.unsqueeze(1).broadcast_to([P, 8, m.shape[1]])

        def b3(b, w=T):
            return bank[b][:, :].rearrange("p (c t) -> p c t", t=w)

        def gate_products(pe, n):
            for _ in range(n):
                s = gate_n["pe"] % 4
                project(pe, [s], [s % 2], 1, channels(T))
                gate_n["pe"] += 1

        def gate_reads(act, n):
            for _ in range(n):
                g = gate_n["act"]
                evacuate(act, [g % 4], [g % 2], 1, lambda q, b, i: nc.scalar.activation(
                    gates[:, g, :], b[:, 0:T], ACT.Identity, bias=col("gate_b", g)))
                gate_n["act"] += 1

        with nc.Block() as block:
            @block.sync
            def _(sp):
                load(sp, range(4), 7)
                load(sp, range(4, 8))

            @block.gpsimd
            def _(pool):
                g = nc.gpsimd
                for c in range(2):
                    cx, acc, tap = sc_c[:, c, :], y[:, c, :], y[:, 2 + c, :]
                    poo.link(g.tensor_tensor(cx, z[:, 10 + c, :], z[:, 12 + c, :], ALU.mult))
                    poo.link(g.tensor_scalar(acc, cx, col("sc_conv_w", 4 + c), None, ALU.mult))
                    for back in (1, 2):
                        poo.link(g.tensor_scalar(tap, cx, col("sc_conv_w", 2 * (2 - back) + c), None, ALU.mult))
                        poo.link(g.tensor_tensor(acc[:, back:T], acc[:, back:T], tap[:, 0:T - back], ALU.add))
                    poo.link(g.tensor_tensor(acc, acc, z[:, 8 + c, :], ALU.mult))
                poo.eng.sem_inc(S("short_conv"), 1)

            def grow(dve, v, lev):
                dve.wait_ge(S("level_x"), lev)
                for half in range(2):
                    q4 = slice(4 * half, 4 * half + 4)
                    if lev < LEVELS:
                        vec.link(v.tensor_tensor(X[:, q4, :], X[:, q4, :], b3(4 + half, P), ALU.add))
                    ins = v.tensor_tensor(XT[:, q4, :], XT[:, q4, :], b3(6 + half, P), ALU.add)
                    vec.link(ins) if half == 0 else vec.tell(ins, S("level_grown"), lev)

            @block.vector
            def _(dve):
                v = nc.vector
                vec.link(v.tensor_tensor(shift[:, :, 1:T], z[:, 0:8, 0:T - 1], z[:, 0:8, 1:T], ALU.subtract))
                vec.link(v.tensor_scalar(shift[:, :, 0:1], z[:, 0:8, 0:1], -1.0, None, ALU.mult))
                for c in range(8):
                    ins = v.scalar_tensor_tensor(z[:, c, :], shift[:, c, :], col("rw_mu", c), z[:, c, :],
                                                 ALU.mult, ALU.add)
                vec.tell(ins, S("rw_mixed"))
                for c in range(2):
                    vec.link(v.tensor_scalar(kk[:, c, :], k_z[:, c, :], col("rw_k_k", c), None, ALU.mult))
                vec.tell(v.tensor_tensor(kk2, kk, kk, ALU.mult), S("kk_squares"))

                dve.wait_ge(S("sg_v"), 1)
                mean, rstd = sg_st[:, 0:2], sg_st[:, 2:4]
                vec.link(v.tensor_tensor(sg_wt, f("sgw").rearrange("p (g t) -> p g t", g=4), four(f("causal")), ALU.mult))
                vec.link(v.tensor_reduce(mean, v_sg, AX, ALU.add))
                vec.link(v.tensor_scalar(mean, mean, 1.0 / T, None, ALU.mult))
                for tt in range(2):
                    vec.link(v.tensor_scalar(sg_d[:, tt, :], v_sg[:, tt, :], mean[:, tt:tt + 1], None, ALU.subtract))
                vec.link(v.tensor_tensor(sg_q, sg_d, sg_d, ALU.mult))
                vec.link(v.tensor_reduce(rstd, sg_q, AX, ALU.add))
                vec.link(v.tensor_scalar(rstd, rstd, 1.0 / T, LN_EPS, ALU.mult, ALU.add))
                vec.tell(v.reciprocal(rstd, rstd), S("sg_var"))

                dve.wait_ge(S("sb_logs"), 1)
                parts = [(3, 0), (4, 512), (5, 1024)]
                for b, o in parts:
                    vec.link(v.tensor_scalar(sb_b[:, o:o + 512], bank[b][:, :], 0.125, 0.0, ALU.mult, ALU.min))
                vec.link(v.tensor_tensor(sb_b, sb_b, sb_l, ALU.subtract))
                for b, o in parts:
                    vec.link(v.scalar_tensor_tensor(sb_k[:, o:o + 512], bank[b][:, :], -0.125, sb_b[:, o:o + 512],
                                                    ALU.mult, ALU.add))
                halves = [(sb_k[:, 0:1024].rearrange("p (h t) -> p h t", h=4), four(f("sb_mask0"))),
                          (sb_k[:, 1024:1536].rearrange("p (h t) -> p h t", h=4), four(f("sb_mask1")))]
                vec.link(v.tensor_tensor(halves[0][0], halves[0][0], halves[0][1], ALU.mult))
                vec.tell(v.tensor_tensor(halves[1][0], halves[1][0], halves[1][1], ALU.mult), S("sb_keep"))

                dve.wait_ge(S("rw_sigmoids"), 1)
                for c in range(2):
                    vec.link(v.tensor_tensor_scan(cum[:, c, :], f("carry"), w_sig[:, c, :], 0.0, ALU.mult, ALU.add))
                vec.tell(v.tensor_tensor(d_prev, cum, w_sig, ALU.subtract), S("rw_cum"))
                for c in range(2):
                    vec.link(v.tensor_scalar(kmod[:, c, :], a_sig[:, c, :], -1.0, col("rw_k_a", c), ALU.add, ALU.mult))
                vec.link(v.scalar_tensor_tensor(kmod, kmod, 1.0, k_z, ALU.add, ALU.mult))
                dve.wait_ge(S("kk_root"), 1)
                vec.link(v.tensor_scalar(kk2, kk2, 1e-12, None, ALU.max))
                vec.link(v.reciprocal(kk2, kk2))
                vec.link(v.tensor_tensor(kk, kk, kk2, ALU.mult))
                for c in range(2):
                    ins = v.scalar_tensor_tensor(kk2[:, c, :], r_z[:, c, :], col("rw_r_k", c), kmod[:, c, :],
                                                 ALU.mult, ALU.mult)
                vec.tell(ins, S("rw_rk"))
                dve.wait_ge(S("rw_decays"), 1)
                vec.link(v.scalar_tensor_tensor(a_t, kk, -1.0, d_prev, ALU.mult, ALU.mult))
                vec.link(v.tensor_tensor(kk, kk, a_sig, ALU.mult))
                vec.link(v.tensor_tensor(b_t, kk, d_inv, ALU.mult))
                vec.link(v.tensor_tensor(k_t, kmod, d_inv, ALU.mult))
                vec.tell(v.tensor_tensor(r_t, r_z, decay, ALU.mult), S("rw_scaled"))

                dve.wait_ge(S("sg_root"), 1)
                for tt in range(2):
                    vec.link(v.scalar_tensor_tensor(sg_q[:, tt, :], sg_d[:, tt, :], rstd[:, tt:tt + 1],
                                                    f("ln_rows")[:, 0:T], ALU.mult, ALU.mult))
                vec.tell(v.tensor_tensor(sg_q, sg_q, f("ln_rows")[:, T:2 * T].unsqueeze(1).broadcast_to([P, 2, T]),
                                         ALU.add), S("sg_normed"))

                dve.wait_ge(S("sb_suffix"), 1)
                for b, o in ((5, 0), (6, 512), (7, 1024)):
                    ins = v.tensor_tensor(sb_b[:, o:o + 512], sb_b[:, o:o + 512], bank[b][:, :], ALU.add)
                vec.tell(ins, S("sb_arg"))
                dve.wait_ge(S("rw_bonus"), 1)
                vec.tell(v.tensor_tensor(bonus, b3(4), v_z, ALU.mult), S("rw_bonus_read"))
                dve.wait_ge(S("sb_exp"), 1)
                vec.link(v.tensor_tensor(halves[0][0], halves[0][0], halves[0][1], ALU.mult))
                vec.tell(v.tensor_tensor(halves[1][0], halves[1][0], halves[1][1], ALU.mult), S("sb_weights"))
                dve.wait_ge(S("sg_mixed"), 1)
                dve.wait_ge(S("short_conv"), 1)
                vec.link(v.tensor_tensor(y[:, 6:8, :], b3(2), f("sgb").rearrange("p (c t) -> p c t", c=2), ALU.add))
                vec.link(v.tensor_tensor(y[:, 6:8, :], y[:, 6:8, :], u_z, ALU.mult))
                dve.wait_ge(S("sb_out"), 1)
                vec.tell(v.tensor_copy(y[:, 2:4, :], b3(3)), S("early_read"))

                n = 0
                lv = f("levels_t").rearrange("p (l t) -> p l t", l=6)
                for odd in range(2):
                    q4 = slice(4 * odd, 4 * odd + 4)
                    for kind in range(5):
                        b = 2 + n % 6
                        dve.wait_ge(S("pair_done"), n + 1)
                        src = b3(b, P)
                        if kind == 0:
                            vec.tell(v.tensor_tensor(X[:, q4, :], src, four(f("level0")), ALU.mult), S("pair_read"), n + 1)
                            vec.link(v.tensor_tensor(X[:, q4, :], X[:, q4, :], four(ident), ALU.add))
                        elif kind == 1:
                            vec.tell(v.tensor_copy(MT[:, q4, :], src), S("pair_read"), n + 1)
                            vec.link(v.tensor_tensor(XT[:, q4, :], MT[:, q4, :], four(lv[:, 0, :]), ALU.mult))
                            vec.link(v.tensor_tensor(XT[:, q4, :], XT[:, q4, :], four(ident), ALU.add))
                        else:
                            dst, m = ((MTak, "upper"), (MTrb, "upper_eq"), (MTrk, "upper_eq"))[kind - 2]
                            vec.tell(v.tensor_tensor(dst[:, q4, :], src, four(f(m)), ALU.mult), S("pair_read"), n + 1)
                        n += 1

                for lev in range(1, LEVELS + 1):
                    if lev > 1:
                        dve.wait_ge(S("level_z"), lev - 1)
                    vec.tell(v.tensor_tensor(NT, MT, eight(lv[:, lev, :]), ALU.mult), S("level_nt"), lev)
                    if lev > 1:
                        grow(dve, v, lev - 1)
                grow(dve, v, LEVELS)
                dve.wait_ge(S("mv_done"), 1)
                vec.tell(v.tensor_copy(AM[:, :, 64:P], b3(2, 64)), S("mv_read"))
                dve.wait_ge(S("chunk_ops"), 1)
                vec.link(v.tensor_tensor(rp, b3(5), r_t, ALU.add))
                vec.link(v.tensor_tensor(phi, b3(7, 64), eight(f("eye2")), ALU.add))
                vec.link(v.tensor_copy(n0, b3(2, 64)))
                vec.link(v.tensor_copy(y0, b3(6)))
                for c in range(4):
                    last_decay = decay[:, :, 64 * c + 63:64 * c + 64].broadcast_to([P, 2, 64])
                    if c == 0:
                        vec.tell(v.tensor_tensor(st2[:, 1], n0[:, 0:2, :], last_decay, ALU.mult), S("rw_state"), 1)
                    elif c < 3:
                        dve.wait_ge(S("state_step"), c)
                        vec.link(v.tensor_tensor(stp, bank[4][:, 0:P].rearrange("p (c v) -> p c v", c=2),
                                                 n0[:, 2 * c:2 * c + 2, :], ALU.add))
                        vec.tell(v.tensor_tensor(st2[:, (c + 1) % 2], stp, last_decay, ALU.mult), S("rw_state"), c + 1)
                dve.wait_ge(S("state_step"), 3)
                vec.tell(v.tensor_tensor(y0[:, :, 64:T], y0[:, :, 64:T], b3(3)[:, :, 64:T], ALU.add), S("rw_y"))

                dve.wait_ge(S("gn_mean"), 1)
                vec.link(v.scalar_tensor_tensor(y0, b3(5), -1.0 / 64, y0, ALU.mult, ALU.add))
                vec.tell(v.tensor_tensor(yd2, y0, y0, ALU.mult), S("gn_squares"))
                dve.wait_ge(S("gn_var"), 1)
                vec.link(v.tensor_scalar(yd2, b3(6), 1.0 / 64, GN_EPS, ALU.mult, ALU.add))
                vec.tell(v.reciprocal(yd2, yd2), S("gn_inverse"))
                dve.wait_ge(S("gn_root"), 1)
                vec.link(v.tensor_tensor(y0, y0, yd2, ALU.mult))
                for c in range(2):
                    vec.link(v.tensor_scalar(y0[:, c, :], y0[:, c, :], col("rw_gn_g", c), col("rw_gn_b", c),
                                             ALU.mult, ALU.add))
                vec.link(v.tensor_tensor(y0, y0, bonus, ALU.add))
                vec.link(v.tensor_tensor(y[:, 4:6, :], y0, g_rw, ALU.mult))

            @block.scalar
            def _(act):
                a = nc.scalar
                sca.tell(a.activation(v_sg, v_sg, ACT.Gelu_apprx_tanh), S("sg_v"))
                a.activation(u_z, u_z, ACT.Gelu_apprx_tanh)
                act.wait_ge(S("sb_scores"), 1)
                for b, o in ((3, 0), (4, 512), (5, 1024)):
                    ins = a.activation(sb_l[:, o:o + 512], bank[b][:, :], ACT.Abs, scale=0.125)
                sca.link(ins)
                sca.link(a.activation(sb_l, sb_l, ACT.Exp, scale=-1.0))
                sca.tell(a.activation(sb_l, sb_l, ACT.Ln, bias=ones[:, 0:1]), S("sb_logs"))
                act.wait_ge(S("rw_mixed"), 1)
                a.activation(z[0:64, 6, :], z[0:64, 6, :], ACT.Tanh)
                sca.tell(a.activation(lora_h, g_z, ACT.Sigmoid), S("lora_in"))
                gate_reads(act, 2)
                act.wait_ge(S("rw_lora"), 1)
                for c in range(2):
                    a.activation(w_sig[:, c, :], b3(6)[:, c, :], ACT.Sigmoid, bias=col("rw_w0", c))
                    a.activation(a_sig[:, c, :], b3(7)[:, c, :], ACT.Sigmoid, bias=col("rw_a0", c))
                sca.tell(a.activation(g_rw, b3(2), ACT.Copy), S("rw_sigmoids"))
                act.wait_ge(S("kk_sum"), 1)
                sca.tell(a.activation(kk2, b3(3), ACT.Sqrt), S("kk_root"))
                act.wait_ge(S("sg_var"), 1)
                sca.tell(a.activation(sg_st[:, 2:4], sg_st[:, 2:4], ACT.Sqrt), S("sg_root"))
                act.wait_ge(S("rw_cum"), 1)
                a.activation(decay, cum, ACT.Exp, scale=-DECAY_SCALE)
                a.activation(d_inv, cum, ACT.Exp, scale=DECAY_SCALE)
                sca.tell(a.activation(d_prev, d_prev, ACT.Exp, scale=-DECAY_SCALE), S("rw_decays"))
                gate_reads(act, 3)
                act.wait_ge(S("sb_arg"), 1)
                sca.tell(a.activation(sb_k, sb_b, ACT.Exp), S("sb_exp"))
                gate_reads(act, 3)
                act.wait_ge(S("tm_done"), 1)
                for n in range(4):
                    ins = a.activation(tm[:, n], b3(4 + n), ACT.Copy)
                sca.tell(ins, S("tm_read"))
                gate_reads(act, 3)
                for lev in range(1, LEVELS + 1):
                    act.wait_ge(S("level_z"), lev)
                    a.activation(Z[:, 0:4, :], b3(2, P), ACT.Copy)
                    sca.tell(a.activation(Z[:, 4:8, :], b3(3, P), ACT.Copy), S("level_zc"), lev)
                    gate_reads(act, 2)
                for odd in range(2):
                    ins = a.activation(AM[:, 4 * odd:4 * odd + 4, 0:64].rearrange("p (a c) k -> p a c k", a=2),
                                       tm[:, 0].rearrange("p a (c r k) -> p r a c k", c=2, r=2)[:, odd], ACT.Copy)
                ins.then_inc(S("am_a"), 1)
                act.wait_ge(S("gh_done"), 1)
                a.activation(GH[:, 0:4, :], b3(3, P), ACT.Copy)
                sca.tell(a.activation(GH[:, 4:8, :], b3(4, P), ACT.Copy), S("gh_read"))
                gate_reads(act, 5)
                act.wait_ge(S("gn_inverse"), 1)
                sca.tell(a.activation(yd2, yd2, ACT.Sqrt), S("gn_root"))
                gate_reads(act, 6)
                for b in range(2):
                    act.wait_ge(drained[b], ev_at.banks[b] + 1)

            @block.tensor
            def _(pe):
                mm = nc.tensor.matmul

                def pair(m):
                    odd, tt, c = m // 4, m % 4 // 2, m % 2
                    return 2 * c + odd, c, 64 * odd, tt

                def head(hh):
                    return hh // 2, 64 * (hh % 2)

                for hh in (0, 2, 1, 3):
                    c, p = head(hh)
                    if hh == 1:
                        turn(pe, ins)
                    mm(bank[3 + hh // 2][:, hh % 2 * T:(hh % 2 + 1) * T], kk_z[p:p + 64, c, 0:P], q_z[p:p + 64, c, :],
                       start=True, stop=True)
                    ins = mm(bank[5][:, hh * P:(hh + 1) * P], kk_z[p:p + 64, c, P:T], q_z[p:p + 64, c, P:T],
                             start=True, stop=True)
                ins.then_inc(S("sb_scores"), 1)
                gate_products(pe, 2)
                pe.wait_ge(S("lora_in"), 1)
                lw = f("lora")
                for c in range(2):
                    o = slice(c * T, (c + 1) * T)
                    mm(bank[6][:, o], lw[0:64, c * P:(c + 1) * P], z[0:64, 6, :], start=True, stop=True)
                    mm(bank[7][:, o], lw[64:P, c * P:(c + 1) * P], z[64:P, 6, :], start=True, stop=True)
                    ins = mm(bank[2][:, o], lw[:, T + c * P:T + (c + 1) * P], lora_h, start=True, stop=True)
                ins.then_inc(S("rw_lora"), 1)
                pe.wait_ge(S("kk_squares"), 1)
                pe.wait_ge(S("sb_keep"), 1)
                mm(bank[3][:, :], f("same"), kk2.rearrange("p c t -> p (c t)"), start=True, stop=True)\
                    .then_inc(S("kk_sum"), 1)
                pe.wait_ge(S("rw_sigmoids"), 1)
                k0, k1 = sb_k[:, 0:1024], sb_k[:, 1024:1536]
                mm(bank[7][:, :], f("after"), k1, start=True, stop=True)
                for half in range(2):
                    b = bank[5 + half]
                    mm(b[:, :], f("after"), k0[:, half * 512:(half + 1) * 512], start=True, stop=False)
                    for q in range(2):
                        hh = 2 * half + q
                        ins = mm(b[:, q * T + P:(q + 1) * T], ones, k1[:, hh * P:(hh + 1) * P],
                                 start=False, stop=q == 1)
                ins.then_inc(S("sb_suffix"), 1)
                gate_products(pe, 3)
                pe.wait_ge(S("rw_rk"), 1)
                mm(bank[4][:, :], f("same"), kk2.rearrange("p c t -> p (c t)"), start=True, stop=True)\
                    .then_inc(S("rw_bonus"), 1)
                pe.wait_ge(S("sg_normed"), 1)
                for g in range(4):
                    c, p = head(g)
                    for tt in range(2):
                        ins = mm(bank[2][p:p + 64, c * T + tt * P:c * T + (tt + 1) * P],
                                 sg_q[:, tt, g * 64:(g + 1) * 64], sg_wt[:, g, :], start=True, stop=True)
                ins.then_inc(S("sg_mixed"), 1)
                pe.wait_ge(S("sb_weights"), 1)
                for hh in range(4):
                    c, p = head(hh)
                    mm(bank[3][p:p + 64, c * T:(c + 1) * T], v_sb[:, 0, hh * 64:(hh + 1) * 64],
                       k0[:, hh * T:(hh + 1) * T], start=True, stop=False)
                    ins = mm(bank[3][p:p + 64, c * T + P:(c + 1) * T], v_sb[:, 1, hh * 64:(hh + 1) * 64],
                             k1[:, hh * P:(hh + 1) * P], start=False, stop=True)
                ins.then_inc(S("sb_out"), 1)
                gate_products(pe, 3)
                pe.wait_ge(S("rw_scaled"), 1)
                pe.wait_ge(S("sb_arg"), 1)
                pe.wait_ge(S("rw_bonus_read"), 1)
                for n, m in enumerate((a_t, b_t, k_t, v_z)):
                    for tt in range(2):
                        for c in range(2):
                            o = tt * T + c * P
                            ins = nc.tensor.transpose(bank[4 + n][:, o:o + P], m[:, c, tt * P:(tt + 1) * P], ident)
                ins.then_inc(S("tm_done"), 1)
                gate_products(pe, 3)
                pe.wait_ge(S("early_read"), 1)
                pe.wait_ge(S("tm_read"), 1)
                n = 0
                for odd in range(2):
                    for lhs, rhs in ((a_t, b_t), (b_t, a_t), (k_t, a_t), (b_t, r_t), (k_t, r_t)):
                        if n >= 6:
                            pe.wait_ge(S("pair_read"), n - 5)
                        for m in range(4):
                            _, c, p, tt = pair(4 * odd + m)
                            o = slice(tt * P, (tt + 1) * P)
                            ins = mm(bank[2 + n % 6][:, m * P:(m + 1) * P], lhs[p:p + 64, c, o], rhs[p:p + 64, c, o],
                                     start=True, stop=True)
                        ins.then_inc(S("pair_done"), 1)
                        n += 1
                for lev in range(1, LEVELS + 1):
                    pe.wait_ge(S("level_nt"), lev)
                    if lev == 1:
                        pe.wait_ge(S("pair_read"), 10)
                    else:
                        pe.wait_ge(S("level_grown"), lev - 1)
                    for m in range(8):
                        ins = mm(bank[2 + m // 4][:, m % 4 * P:(m % 4 + 1) * P], NT[:, m, :], X[:, m, :],
                                 start=True, stop=True)
                    ins.then_inc(S("level_z"), 1)
                    gate_products(pe, 1)
                    pe.wait_ge(S("level_zc"), lev)
                    for m in range(8):
                        o = slice(m % 4 * P, (m % 4 + 1) * P)
                        if lev < LEVELS:
                            mm(bank[4 + m // 4][:, o], XT[:, m, :], Z[:, m, :], start=True, stop=True)
                        ins = mm(bank[6 + m // 4][:, o], Z[:, m, :], XT[:, m, :], start=True, stop=True)
                    ins.then_inc(S("level_x"), 1)
                    gate_products(pe, 1)
                for m in range(8):
                    hh, _, _, tt = pair(m)
                    ins = mm(bank[2][:, m * 64:(m + 1) * 64], MTak[:, m, :],
                             tm[:, 3, tt, hh * 64:(hh + 1) * 64], start=True, stop=True)
                ins.then_inc(S("mv_done"), 1)
                pe.wait_ge(S("level_grown"), LEVELS)
                pe.wait_ge(S("mv_read"), 1)
                pe.wait_ge(S("am_a"), 1)
                for m in range(8):
                    ins = mm(bank[3 + m // 4][:, m % 4 * P:(m % 4 + 1) * P], XT[:, m, :], AM[:, m, :],
                             start=True, stop=True)
                ins.then_inc(S("gh_done"), 1)
                gate_products(pe, 2)
                pe.wait_ge(S("gh_read"), 1)
                for m in range(8):
                    hh, c, p, tt = pair(m)
                    o = slice(c * T + tt * P, c * T + (tt + 1) * P)
                    mm(bank[5][p:p + 64, o], GH[:, m, 0:64], MTrb[:, m, :], start=True, stop=True)
                    mm(bank[6][p:p + 64, o], GH[:, m, 64:P], MTrb[:, m, :], start=True, stop=False)
                    mm(bank[6][p:p + 64, o], tm[:, 3, tt, hh * 64:(hh + 1) * 64], MTrk[:, m, :], start=False, stop=True)
                for ch in (0, 2, 1, 3):
                    if ch == 1:
                        turn(pe, ins)
                    tt, r = ch // 2, slice(64 * (ch % 2), 64 * (ch % 2) + 64)
                    for hh in range(4):
                        c, p = head(hh)
                        m, o, hs = 4 * (hh % 2) + 2 * tt + c, slice((2 * ch + c) * 64, (2 * ch + c + 1) * 64), slice(hh * 64, (hh + 1) * 64)
                        mm(bank[7][p:p + 64, o], GH[r, m, 0:64], tm[r, 1, tt, hs], start=True, stop=True)
                        mm(bank[2][p:p + 64, o], tm[r, 1, tt, hs], GH[r, m, 64:P], start=True, stop=False)
                        ins = mm(bank[2][p:p + 64, o], tm[r, 2, tt, hs], tm[r, 3, tt, hs], start=False, stop=True)
                ins.then_inc(S("chunk_ops"), 1)
                gate_products(pe, 3)
                for ch in range(1, 4):
                    pe.wait_ge(S("rw_state"), ch)
                    for hh in range(4):
                        c, p = head(hh)
                        ins = mm(bank[3][p:p + 64, c * T + 64 * ch:c * T + 64 * (ch + 1)], st2[p:p + 64, ch % 2, c, :],
                                 rp[p:p + 64, c, 64 * ch:64 * (ch + 1)], start=True, stop=True)
                    if ch < 3:
                        for hh in range(4):
                            c, p = head(hh)
                            ins = mm(bank[4][p:p + 64, c * 64:(c + 1) * 64], phi[p:p + 64, 2 * ch + c, :],
                                     st2[p:p + 64, ch % 2, c, :], start=True, stop=True)
                    ins.then_inc(S("state_step"), 1)
                pe.wait_ge(S("rw_y"), 1)
                mm(bank[5][:, :], f("same"), y0.rearrange("p c t -> p (c t)"), start=True, stop=True)\
                    .then_inc(S("gn_mean"), 1)
                pe.wait_ge(S("gn_squares"), 1)
                mm(bank[6][:, :], f("same"), yd2.rearrange("p c t -> p (c t)"), start=True, stop=True)\
                    .then_inc(S("gn_var"), 1)
                gate_products(pe, 6)

        a5 = Area(arena, scratch_at)
        merged, prod = a5.take(8, T), a5.take(4, T)
        W_O = (4, 5, 6, 7, 0, 1, 2, 3)
        o_filled = [pe_at.rounds[s] + 2 for s in W_O]
        o_base = split["blocks"]
        o_high = Area(arena_parts[25344]).take(SLOTS, D)
        in_z = Area(arena_parts[0])
        merged_high, merged_low = in_z.take(8, T), in_z.take(8, T)
        FF_FIRST, FF_SLOTS, FF_LAST = (0, 1, 3, 4), (0, 1, 2, 3, 4, 5), (6, 7)
        by_branch = gates.rearrange("p (b n) t -> p b n t", b=4)
        with nc.Block() as block:
            @block.sync
            def _(sp):
                load(sp, range(4))
                load(sp, range(4, 8))
                load(sp, range(4))
                load(sp, FF_FIRST)

            @block.tensor
            def _(pe):
                def branches(q, w, b, i):
                    for br in range(4):
                        dst = (b if br < 2 else bank[4 + q])[:, br % 2 * T:(br % 2 + 1) * T]
                        for k in range(2):
                            mm = nc.tensor.matmul(dst, w[:, 2 * br + k, :], y[:, 2 * br + k, :],
                                                  start=k == 0, stop=k == 1)
                    return mm

                def onto(first_m):
                    def mats(q, w, b, i):
                        s = W_O[first_m + q]
                        pe.wait_ge(S("low"), o_base + first_m + q + 1)
                        for k in range(KT):
                            if first_m + q == 0:
                                pe.wait_ge(S("merged"), k + 1)
                            c = slice(k * P, (k + 1) * P)
                            mm = three(b[:, 0:T], (o_high[:, s, c], low[:, s, c]), (merged_high[:, k, :], merged_low[:, k, :]),
                                       k == 0, k == KT - 1)
                        return mm
                    return mats

                project(pe, range(4, 8), range(4), 1, branches)
                project(pe, range(4), range(4), 1, branches)
                project(pe, range(4, 8), range(4), 1, onto(0))
                project(pe, range(4), range(4), 1, onto(4))

            @block.scalar
            def _(act):
                for n in range(KT):
                    nc.scalar.activation(by_branch[:, :, n, :], by_branch[:, :, n, :], ACT.Sigmoid)\
                        .then_inc(S("gate_open"), 1)
                for s, filled in zip(W_O, o_filled):
                    part_high(act, o_high, s, filled)

            @block.gpsimd
            def _(pool):
                for m, s in enumerate(W_O):
                    part_low(pool, nc.gpsimd, o_high, s, o_base + m + 1)

            @block.vector
            def _(dve):
                v = nc.vector
                def merge_one(n, q, b):
                    dve.wait_ge(S("gate_open"), n + 1)
                    vec.link(v.tensor_tensor(prod[:, 0:2, :], b[:, :].rearrange("p (c t) -> p c t", c=2),
                                             by_branch[:, 0:2, n, :], ALU.mult))
                    return v.tensor_tensor(prod[:, 2:4, :], b3(4 + q), by_branch[:, 2:4, n, :], ALU.mult)

                for half, slots in enumerate((range(4, 8), range(4))):
                    for q, s in enumerate(slots):
                        evacuate(dve, [s], [q], 1, lambda _, b, i: merge_one(4 * half + q, q, b))
                        dve.wait_ge(drained[q], ev_at.banks[q] + 1)
                        vec.link(v.tensor_tensor(prod[:, 0:2, :], prod[:, 0:2, :], prod[:, 2:4, :], ALU.add))
                        k = 4 * half + q
                        vec.link(v.tensor_tensor(merged[:, k, :], prod[:, 0, :], prod[:, 1, :], ALU.add))
                        vec.link(v.tensor_copy(merged_high[:, k, :], merged[:, k, :]))
                        vec.tell(v.tensor_tensor(merged_low[:, k, :], merged[:, k, :], merged_high[:, k, :].bitcast(F32),
                                                 ALU.subtract), S("merged"), k + 1)
                for half, slots in enumerate((range(4, 8), range(4))):
                    evacuate(dve, slots, range(4), 1, lambda q, b, i: v.tensor_tensor(
                        x[:, 4 * half + q, :], x[:, 4 * half + q, :], b[:, 0:T], ALU.add))
                dve.wait_ge(drained[3], ev_at.banks[3] + 1)
        split["blocks"] += 8

        a6 = Area(arena)
        conv = a6.take(2, 2, T)
        hidden = a6.take(2, T)
        xin = a6.take(KT, TT)
        sq2 = a6.take(KT, TT)
        a6p = Area(arena_parts[a6.at])
        high, h_high = a6p.take(SLOTS, D), a6p.take(KT, T)
        hid_high, hid_low = a6p.take(2, T), a6p.take(2, T)
        h_low = h_parts[:, :, 0:T]
        assert a6.at + a6p.at <= scratch_at
        pairs = FT // 2 - 1
        block_base, h_base = split["blocks"], split["h"]
        before = {s: pe_at.rounds[s] for s in range(SLOTS)}

        def ff_block(n, i=0):
            if n < 0:
                return FF_FIRST[n + 4], before[FF_FIRST[n + 4]] + 1, block_base + n + 5
            if isinstance(i, int) and i == pairs:
                s = FF_LAST[n]
                return s, before[s] + 1, block_base + 4 + 6 * pairs + n + 1
            s = FF_SLOTS[n]
            return s, i + (before[s] + (s in FF_FIRST) + 1), i * 6 + (block_base + 4 + n + 1)

        def ff_high(act, n, i=0):
            s, filled, number = ff_block(n, i)
            act.wait_ge(full[s], filled * 16)
            nc.scalar.activation(high[:, s, :], ring[:, s, :], ACT.Copy).then_inc(S("high"), 1)

        def ff_low(dve, n, i=0):
            s, filled, number = ff_block(n, i)
            dve.wait_ge(S("high"), number)
            nc.vector.tensor_tensor(low[:, s, :], ring[:, s, :], high[:, s, :].bitcast(F32), ALU.subtract)\
                .then_inc(S("low"), 1)

        rms_norm(lambda k: x[:, k, :], lambda k: h[:, k, 0:T], "ffn_norm_g", RMS_EPS, squares,
                 beside=(lambda act: [ff_high(act, n) for n in (-4, -3)], lambda dve: [ff_low(dve, n) for n in (-4, -3)]))
        with nc.Block() as block:
            @block.sync
            def _(sp):
                sp.dma_start(xin[:, :, 0:M], meta_t).then_inc(S("meta_in"), 16)
                load(sp, FF_SLOTS, pairs)
                load(sp, FF_LAST)
                load(sp, range(4))
                sp.wait_ge(S("meta_in"), 16)

            @block.tensor
            def _(pe):
                mm = nc.tensor.matmul
                for b in range(4):
                    pe.wait_ge(drained[b], pe_at.banks[b] + 1)
                    mm(bank[b][:, :], ident, x[:, 2 * b:2 * b + 2, :].rearrange("p c t -> p (c t)"), start=True, stop=False)

                def up(n, i=0):
                    j = n // 3 % 2 if n >= 0 else n // 2 % 2
                    if n >= 0:
                        pe.wait_ge(S("up_read"), i * 2 + (j + 1))
                    for part in range(2):
                        s, _, number = ff_block(n + part, i)
                        b = bank[4 + 2 * j + part][:, 0:T]
                        pe.wait_ge(S("low"), number)
                        for k in range(KT):
                            w = slice(k * P, (k + 1) * P)
                            if n == -4 and part == 0 and k % 4 == 0:
                                pe.wait_ge(S("h_parts"), h_base + k // 4 + 1)
                            mm(b, high[:, s, w], h_high[:, k, :], start=k == 0, stop=False)
                            mm(b, high[:, s, w], h_low[:, k, :], start=False, stop=False)
                            ins = mm(b, low[:, s, w], h_high[:, k, :], start=False, stop=k == KT - 1)
                        ins.then_inc(used[s], 1)

                def down(n, i, j, last_one=False):
                    s, _, number = ff_block(n, i)
                    pe.wait_ge(S("low"), number)
                    pe.wait_ge(S("ff_hidden"), i * 2 + (j + 3))
                    for c in range(KT):
                        b, w = bank[c // 2][:, c % 2 * T:(c % 2 + 1) * T], slice(c * P, (c + 1) * P)
                        mm(b, high[:, s, w], hid_high[:, j, :], start=False, stop=False)
                        mm(b, high[:, s, w], hid_low[:, j, :], start=False, stop=False)
                        ins = mm(b, low[:, s, w], hid_high[:, j, :], start=False, stop=last_one and c % 2 == 1)
                    ins.then_inc(used[s], 1)

                up(-4)
                up(-2)
                with pe.Fori(0, pairs) as i:
                    for j in range(2):
                        up(3 * j, i)
                        down(3 * j + 2, i, j)
                for j in range(2):
                    down(j, pairs, j, j == 1)

            @block.vector
            def _(dve):
                v = nc.vector

                def tap(k, c):
                    return par[:, bass.ds(c + (at["ffn_conv_w"] + 2 * FT * k), 1)]

                def convolve(i, j):
                    dve.wait_ge(S("ff_hidden"), i * 2 + (j + 1))
                    for part in range(2):
                        s = FF_SLOTS[3 * j + part]
                        dve.wait_ge(used[s], i + (before[s] + 1))
                    for back in range(3):
                        for part in range(2):
                            src, dst, c = bank[4 + 2 * j + part], conv[:, j, part, :], i * 2 + (j + FT * part)
                            if back == 0:
                                ins = v.tensor_scalar(dst, src[:, 0:T], tap(2, c), None, ALU.mult)
                            else:
                                dve.wait_ge(S("ff_step"), i * 12 + (6 * j + 2 * back + part - 1))
                                ins = v.scalar_tensor_tensor(dst[:, back:T], src[:, 0:T - back], tap(2 - back, c),
                                                             dst[:, back:T], ALU.mult, ALU.add)
                            ins.then_inc(S("ff_step"), 1)
                    dve.wait_ge(S("ff_step"), i * 12 + (6 * j + 6))
                    dve.sem_inc(S("up_read"), 1)

                for half in range(2):
                    dve.wait_ge(S("h_rounded"), h_base + half + 1)
                    k = slice(4 * half, 4 * half + 4)
                    v.tensor_tensor(h_low[:, k, :], h[:, k, 0:T], h_high[:, k, :].bitcast(F32), ALU.subtract)\
                        .then_inc(S("h_parts"), 1)
                for n in (-2, -1):
                    ff_low(dve, n)
                with dve.Fori(0, pairs) as i:
                    for j in range(2):
                        ff_low(dve, 3 * j, i)
                        ff_low(dve, 3 * j + 1, i)
                        convolve(i, j)
                        ff_low(dve, 3 * j + 2, i)
                for j in range(2):
                    ff_low(dve, j, pairs)
                for j in range(2):
                    convolve(pairs, j)
                dve.wait_ge(used[FF_LAST[1]], before[FF_LAST[1]] + 1)
                for b in range(4):
                    ins = v.tensor_copy(x[:, 2 * b:2 * b + 2, :], b3(b))
                    ins.then_inc(drained[b], 1)
                for b in range(4):
                    dve.wait_ge(drained[b], pe_at.banks[b] + 2)

            @block.scalar
            def _(act):
                def silu(i, j):
                    act.wait_ge(S("up_read"), i * 2 + (j + 1))
                    nc.scalar.activation(conv[:, j, 0, :], conv[:, j, 0, :], ACT.Silu).then_inc(S("ff_silu"), 1)

                for half in range(2):
                    k = slice(4 * half, 4 * half + 4)
                    nc.scalar.activation(h_high[:, k, :], h[:, k, 0:T], ACT.Copy).then_inc(S("h_rounded"), 1)
                for n in (-2, -1):
                    ff_high(act, n)
                with act.Fori(0, pairs) as i:
                    for j in range(2):
                        ff_high(act, 3 * j, i)
                        ff_high(act, 3 * j + 1, i)
                        ff_high(act, 3 * j + 2, i)
                        silu(i, j)
                for j in range(2):
                    ff_high(act, j, pairs)
                for j in range(2):
                    silu(pairs, j)

            @block.gpsimd
            def _(pool):
                p = nc.gpsimd
                pool.sem_inc(S("ff_hidden"), 2)

                def hide(i, j):
                    pool.wait_ge(S("ff_silu"), i * 2 + (j + 1))
                    s = FF_SLOTS[3 * j + 2]
                    pool.wait_ge(used[s], i + before[s])
                    hid = hidden[:, j, :]
                    p.tensor_tensor(hid, conv[:, j, 0, :], conv[:, j, 1, :], ALU.mult).then_inc(S("hid_step"), 1)
                    pool.wait_ge(S("hid_step"), i * 4 + (2 * j + 1))
                    p.tensor_tensor(hid_high[:, j, :].rearrange("p (a t) -> p a t", a=2),
                                    hid.rearrange("p (a t) -> p a t", a=2),
                                    ones.unsqueeze(1).broadcast_to([P, 2, P]), ALU.mult).then_inc(S("hid_step"), 1)
                    pool.wait_ge(S("hid_step"), i * 4 + (2 * j + 2))
                    p.tensor_tensor(hid_low[:, j, :], hid, hid_high[:, j, :].bitcast(F32), ALU.subtract)\
                        .then_inc(S("ff_hidden"), 1)

                with pool.Fori(0, pairs) as i:
                    hide(i, 0)
                    hide(i, 1)
                hide(pairs, 0)
                hide(pairs, 1)
            split["blocks"] += 3 * FT
            split["h"] += 2
            for tiles in (pe_at, ev_at):
                tiles.advance(FF_FIRST, 1, None)
                tiles.advance(FF_SLOTS, pairs, None)
                tiles.advance(FF_LAST, 1, None)
                for b in range(4):
                    tiles.banks[b] += 1
        rms_norm(lambda k: x[:, k, :], lambda k: xin[:, k, M:TT], "final_norm_g", RMS_EPS, squares_b := sq2)

        xp = Area(arena_parts[25344])
        xn_block, xn_high, xn_low = xp.take(4, D), xp.take(KT, TT), xp.take(KT, TT)
        xn_filled = [pe_at.rounds[s] + 1 for s in range(4)]

        def xn_part_high(act, n, i=0):
            if not (isinstance(i, int) and i * 4 + n >= 12):
                part_high(act, xn_block, n % 4, i + (n // 4 + xn_filled[n % 4]))

        rms_norm(lambda k: xin[:, k, :], lambda k: h[:, k, :], "norm1_g_2", RMS_EPS, squares_b, TT,
                 beside=(lambda act: [xn_part_high(act, n) for n in range(AHEAD)], lambda dve: None))
        a7 = Area(arena, a6.at)
        us, xm = a7.take(4, TT), a7.take(8, TT)
        zg = a7.take(24, T)
        s_at, s_size = offsets(SECOND)
        snd = a7.take(s_size)

        def g2(name, lo=0, n=None):
            return snd[:, s_at[name] + lo:s_at[name] + lo + (n or SECOND[name])]

        with nc.Block() as block:
            @block.sync
            def _(sp):
                sp.dma_start(snd, second).then_inc(S("second_in"), 16)
                load(sp, range(4), 2)
                load(sp, (4, 5, 6))
                load(sp, range(4))
                sp.wait_ge(S("second_in"), 16)

            @block.gpsimd
            def _(pool):
                poo.link(nc.gpsimd.tensor_copy(x[:], xin[:, :, M:TT]))

            @block.tensor
            def _(pe):
                def product(q, w, b, i):
                    pe.wait_ge(S("low"), i * 4 + (split["blocks"] + q + 1))
                    for k in range(KT):
                        c = slice(k * P, (k + 1) * P)
                        ins = three(b[:, 0:TT], (xn_block[:, q, c], low[:, q, c]), (xn_high[:, k, :], xn_low[:, k, :]),
                                    k == 0, k == KT - 1)
                    return ins

                pe.wait_ge(S("h_parts"), split["h"] + 2)
                project(pe, range(4), range(4), 3, product)

            @block.vector
            def _(dve):
                for half in range(2):
                    k = slice(4 * half, 4 * half + 4)
                    dve.wait_ge(S("h_rounded"), split["h"] + half + 1)
                    nc.vector.tensor_tensor(xn_low[:, k, :], h[:, k, :], xn_high[:, k, :].bitcast(F32), ALU.subtract)\
                        .then_inc(S("h_parts"), 1)
                with dve.Fori(0, 3) as i:
                    for n in range(4):
                        part_low(dve, nc.vector, xn_block, n, i * 4 + (split["blocks"] + n + 1))

            @block.scalar
            def _(act):
                for half in range(2):
                    k = slice(4 * half, 4 * half + 4)
                    nc.scalar.activation(xn_high[:, k, :], h[:, k, :], ACT.Copy).then_inc(S("h_rounded"), 1)
                both = arena[:, a6.at:a6.at + 12 * TT].rearrange("p (c t) -> p c t", t=TT)
                before_reads = list(ev_at.rounds)

                def read(n, i):
                    act.wait_ge(used[n], i + (before_reads[n] + 1))
                    dst = both[:, bass.ds(i * 4 + n, 1), :].rearrange("p a t -> p (a t)")
                    nc.scalar.activation(dst, bank[n][:, 0:TT], ACT.Copy).then_inc(drained[n], 1)

                with act.Fori(0, 2) as i:
                    for n in range(4):
                        xn_part_high(act, n + AHEAD, i)
                        read(n, i)
                for n in range(4):
                    xn_part_high(act, n + AHEAD, 2)
                    read(n, 2)
                ev_at.advance(range(4), 3, range(4))
        split["blocks"] += 12
        split["h"] += 2

        r1 = Area(arena)
        e_t = r1.take(2, 1024)
        rows = r1.take(6, TT)
        small = r1.take(20, 16)
        colb = r1.take(3, 4)
        rs4 = r1.take(4, T)
        dmat = [r1.take(640)]
        assert r1.at <= a6.at
        a8 = Area(arena, a7.at)
        er, ei = a8.take(16, TT), a8.take(16, TT)
        xc = a8.take(8, TT)
        dmat.append(a8.take(640))
        s5_at = a8.at
        kc, vc, vt = a8.take(8, TT), a8.take(8, TT), a8.take(3, D)
        qc, h_ml = xm, xm[:, :, M:TT]
        a9 = Area(arena, s5_at)
        bu = a9.take(2, 4, TT)
        zt = a9.take(2, 4, TT)
        rot, rt = a9.take(2, 2 * TT), a9.take(2, 2 * TT)
        s_out, s_tmp = ([e_t[:, k, :].rearrange("p (c s t) -> p c s t", c=2, s=2), a9.take(2, 2, T)] for k in range(2))
        proj_n = {"pe": 0, "act": 0}
        zsig, gs_g, gm_g = zg[:, 0:8, :], zg[:, 8:16, :], zg[:, 16:24, :]
        PAIRS, SHARED = 8, 2

        def z_products(pe, n):
            for _ in range(n):
                s = proj_n["pe"] % 4
                project(pe, [s], [s % 2], 1, channels(T, M))
                proj_n["pe"] += 1

        def z_reads(act, n):
            for _ in range(n):
                g = proj_n["act"]
                evacuate(act, [g % 4], [g % 2], 1, lambda q, b, i: nc.scalar.activation(zg[:, g, :], b[:, 0:T], ACT.Copy))
                proj_n["act"] += 1

        def sm(n):
            return small[:, n, :]

        (S_DT, S_X, S_TH, S_K, S_R, S_SIN, S_HALF, S_COS, S_TANH, S_EM, S_NR, S_NI, S_DEN, S_CR, S_CI, S_T, S_ER, S_EI,
         S_E2R, S_E2I) = range(20)

        with nc.Block() as block:
            bd = [pe_at.rounds[s] for s in (4, 5, 6)]

            @block.sync
            def _(sp):
                load(sp, range(4), 5)
                load(sp, (7,))
                load(sp, (4, 5, 6))
                load(sp, (3,))
                load(sp, (0, 1, 2))

            @block.vector
            def _(dve):
                v = nc.vector
                are, aim = par[:, at["ssm_a_re_2"]:at["ssm_a_re_2"] + 16], par[:, at["ssm_a_im_2"]:at["ssm_a_im_2"] + 16]
                dve.wait_ge(S("s5_dt"), 1)
                vec.link(v.tensor_tensor(sm(S_X), are, sm(S_DT), ALU.mult))
                vec.link(v.tensor_tensor(sm(S_TH), aim, sm(S_DT), ALU.mult))
                vec.link(v.tensor_scalar(sm(S_K), sm(S_TH), 1.0 / TWO_PI, None, ALU.mult))
                vec.link(v.tensor_scalar(sm(S_K), sm(S_K), 12582912.0, None, ALU.add))
                vec.link(v.tensor_scalar(sm(S_K), sm(S_K), 12582912.0, None, ALU.subtract))
                vec.link(v.scalar_tensor_tensor(sm(S_TH), sm(S_K), -6.28125, sm(S_TH), ALU.mult, ALU.add))
                vec.link(v.scalar_tensor_tensor(sm(S_TH), sm(S_K), -0.0019353071795864769, sm(S_TH), ALU.mult, ALU.add))
                vec.tell(v.tensor_scalar(sm(S_TH), sm(S_TH), 3.1415925, -3.1415925, ALU.min, ALU.max), S("s5_angle"))
                w0 = at["ml_conv_w_2"]
                for c in range(8):
                    vec.link(v.tensor_scalar(xc[:, c, :], xm[:, c, :], par[:, w0 + 24 + c:w0 + 25 + c],
                                             col("ml_conv_b_2", c), ALU.mult, ALU.add))
                    for back in (1, 2, 3):
                        j = w0 + 8 * (3 - back) + c
                        ins = v.scalar_tensor_tensor(xc[:, c, back:TT], xm[:, c, 0:TT - back], par[:, j:j + 1],
                                                     xc[:, c, back:TT], ALU.mult, ALU.add)
                        vec.link(ins) if back < 3 else vec.tell(ins, S("ml_conv"), c + 1)
                dve.wait_ge(S("s5_sines"), 1)
                vec.link(v.tensor_tensor(sm(S_T), sm(S_HALF), sm(S_HALF), ALU.mult))
                vec.link(v.tensor_scalar(sm(S_COS), sm(S_T), -2.0, 1.0, ALU.mult, ALU.add))
                vec.link(v.tensor_copy(sm(S_ER), sm(S_COS)))
                vec.tell(v.tensor_copy(sm(S_EI), sm(S_SIN)), S("s5_unit"))
                vec.link(v.tensor_scalar(sm(S_DEN), sm(S_TANH), -1.0, 1.0, ALU.mult, ALU.add))
                vec.link(v.reciprocal(sm(S_DEN), sm(S_DEN)))
                vec.link(v.scalar_tensor_tensor(sm(S_EM), sm(S_TANH), 2.0, sm(S_DEN), ALU.mult, ALU.mult))
                vec.link(v.tensor_tensor(sm(S_NR), sm(S_EM), sm(S_COS), ALU.mult))
                vec.link(v.scalar_tensor_tensor(sm(S_NR), sm(S_T), -2.0, sm(S_NR), ALU.mult, ALU.add))
                vec.link(v.tensor_tensor(sm(S_NI), sm(S_R), sm(S_SIN), ALU.mult))
                vec.link(v.tensor_tensor(sm(S_DEN), are, are, ALU.mult))
                vec.link(v.tensor_tensor(sm(S_T), aim, aim, ALU.mult))
                vec.link(v.tensor_tensor(sm(S_DEN), sm(S_DEN), sm(S_T), ALU.add))
                vec.link(v.reciprocal(sm(S_DEN), sm(S_DEN)))
                vec.link(v.tensor_tensor(sm(S_CR), sm(S_NR), are, ALU.mult))
                vec.link(v.tensor_tensor(sm(S_T), sm(S_NI), aim, ALU.mult))
                vec.link(v.tensor_tensor(sm(S_CR), sm(S_CR), sm(S_T), ALU.add))
                vec.link(v.tensor_tensor(sm(S_CR), sm(S_CR), sm(S_DEN), ALU.mult))
                vec.link(v.tensor_tensor(sm(S_CI), sm(S_NI), are, ALU.mult))
                vec.link(v.tensor_tensor(sm(S_T), sm(S_NR), aim, ALU.mult))
                vec.link(v.tensor_tensor(sm(S_CI), sm(S_CI), sm(S_T), ALU.subtract))
                vec.link(v.tensor_tensor(sm(S_CI), sm(S_CI), sm(S_DEN), ALU.mult))
                c_re, c_im = (g2(n).rearrange("p (s c) -> p s c", s=16) for n in ("c_re", "c_im"))
                t0, t1, t2 = (rs4.rearrange("p a b -> p (a b)")[:, 0:512].rearrange("p (s c) -> p s c", s=16),
                              dmat[0][:, 0:512].rearrange("p (s c) -> p s c", s=16),
                              dmat[1][:, 0:512].rearrange("p (s c) -> p s c", s=16))
                cr, ci = (sm(n).unsqueeze(2).broadcast_to([P, 16, 32]) for n in (S_CR, S_CI))
                vec.link(v.tensor_tensor(t0, c_re, cr, ALU.mult))
                vec.link(v.tensor_tensor(t1, c_im, ci, ALU.mult))
                vec.link(v.tensor_tensor(t0, t0, t1, ALU.subtract))
                vec.link(v.tensor_tensor(t1, c_re, ci, ALU.mult))
                vec.link(v.tensor_tensor(t2, c_im, cr, ALU.mult))
                vec.link(v.tensor_copy(c_re, t0))
                vec.link(v.scalar_tensor_tensor(c_im, t1, -1.0, t2, ALU.mult, ALU.subtract))

                dve.wait_ge(S("if_sum"), 1)
                vec.tell(v.tensor_copy(rows[0:8, 5, :], bank[6][0:8, 0:TT]), S("if_rows"))
                dve.wait_ge(S("if_split"), 1)
                ig, lf, cf, mx, ab, tr = (rows[0:4, n, :] for n in range(6))
                vec.link(v.tensor_scalar(ig, bank[7][0:4, 0:TT], col("ml_b_if_2", 0)[0:4], None, ALU.add))
                vec.link(v.tensor_scalar(lf, bank[6][0:4, 0:TT], col("ml_b_if_2", 1)[0:4], None, ALU.add))
                vec.tell(v.scalar_tensor_tensor(ab, lf, -1.0, lf, ALU.mult, ALU.max), S("ml_abs"))
                dve.wait_ge(S("ml_log"), 1)
                vec.link(v.tensor_scalar(lf, lf, 0.0, None, ALU.min))
                vec.link(v.tensor_tensor(lf, lf, ab, ALU.subtract))
                one_row = ones[0:4, 0:1].broadcast_to([4, TT])
                vec.link(v.tensor_tensor_scan(cf, one_row, lf, 0.0, ALU.mult, ALU.add))
                vec.link(v.tensor_tensor_scan(mx, lf, ig, 0.0, ALU.add, ALU.max))
                vec.link(v.tensor_tensor(ig, ig, cf, ALU.subtract))
                vec.tell(v.tensor_tensor(cf, cf, mx, ALU.subtract), S("ml_rows"))
                dve.wait_ge(S("ml_cols"), 1)
                vec.tell(v.tensor_copy(colb, bank[5][:, 0:12].rearrange("p (s h) -> p s h", s=3)), S("ml_cols_read"))
                for hh in range(4):
                    d = dmat[hh % 2]
                    d1, d2, dm = d[:, 0:T], d[:, T:T + P], d[0:M, 384:640]
                    dve.wait_ge(S("head_scores"), hh + 1)
                    vec.link(v.scalar_tensor_tensor(d1, bank[2][:, 0:T], colb[:, 1, hh:hh + 1], g2("neg0"),
                                                    ALU.add, ALU.add))
                    vec.link(v.scalar_tensor_tensor(d2, bank[2][:, P:T], colb[:, 2, hh:hh + 1], g2("neg1", P, P),
                                                    ALU.add, ALU.add))
                    vec.tell(v.tensor_scalar(dm, bank[2][0:M, 0:T], colb[0:M, 0, hh:hh + 1], None, ALU.add),
                             S("head_logs"), hh + 1)
                    dve.wait_ge(S("head_exp"), hh + 1)
                    vec.link(v.scalar_tensor_tensor(d[:, 0:384], bank[3][:, 0:384], 0.0625, d[:, 0:384], ALU.mult, ALU.mult))
                    vec.tell(v.scalar_tensor_tensor(dm, bank[4][0:M, 0:T], 0.0625, dm, ALU.mult, ALU.mult),
                             S("head_weights"), hh + 1)
                    dve.wait_ge(S("head_sums"), hh + 1)
                    rd = rs4[:, 0, :]
                    vec.link(v.tensor_scalar(rd, bank[6][:, 0:T], -1.0, None, ALU.mult))
                    vec.link(v.tensor_tensor(rd, rd, bank[6][:, 0:T], ALU.max))
                    vec.link(v.tensor_tensor(rd, rd, bank[2][:, T:2 * T], ALU.max))
                    vec.link(v.reciprocal(rd, rd))
                    vec.tell(v.tensor_tensor(h_ml[:, 2 * hh:2 * hh + 2, :], b3(5), rd.unsqueeze(1).broadcast_to([P, 2, T]),
                                             ALU.mult), S("head_read"), hh + 1)
                dve.wait_ge(S("z_sigmoid"), 1)
                vec.link(v.tensor_tensor(h_ml, h_ml, zsig, ALU.mult))
                hsq = vc[:, :, 0:T]
                vec.tell(v.tensor_tensor(hsq, h_ml, h_ml, ALU.mult), S("ml_squares"))
                dve.wait_ge(S("ml_sums"), 1)
                for half in range(2):
                    vec.link(v.tensor_scalar(rs4[:, 2 * half:2 * half + 2, :], b3(2 + half), 1.0 / T, RMS_EPS,
                                             ALU.mult, ALU.add))
                vec.tell(v.reciprocal(rs4, rs4), S("ml_inverse"))
                dve.wait_ge(S("ml_root"), 1)
                for c in range(8):
                    vec.link(v.scalar_tensor_tensor(h_ml[:, c, :], h_ml[:, c, :], col("ml_norm_g_2", c), rs4[:, c // 2, :],
                                                    ALU.mult, ALU.mult))
                    vec.link(v.scalar_tensor_tensor(h_ml[:, c, :], xc[:, c, M:TT], col("ml_skip_2", c), h_ml[:, c, :],
                                                    ALU.mult, ALU.add))
                dve.sem_inc(S("ml_out"), 1)

                dve.wait_ge(S("tables"), 1)
                for p in range(PAIRS):
                    dve.wait_ge(S("bu_ready"), 4 * p + 4)
                    cs, sn = er[:, 2 * p:2 * p + 2, :], ei[:, 2 * p:2 * p + 2, :]
                    src = bu[:, p % 2].rearrange("p (s c) t -> p c s t", s=2)
                    re, im = src[:, 0], src[:, 1]
                    xr, xi = (rot[:, n, :].rearrange("p (s t) -> p s t", s=2) for n in range(2))
                    q0, q1 = (rt[:, n, :].rearrange("p (s t) -> p s t", s=2) for n in range(2))
                    vec.link(v.tensor_tensor(q0, im, sn, ALU.mult))
                    vec.link(v.tensor_tensor(xr, re, cs, ALU.mult))
                    vec.link(v.tensor_tensor(xr, xr, q0, ALU.add))
                    vec.link(v.tensor_tensor(q1, re, sn, ALU.mult))
                    vec.link(v.tensor_tensor(xi, im, cs, ALU.mult))
                    vec.tell(v.tensor_tensor(xi, xi, q1, ALU.subtract), S("bu_turned"), p + 1)
                    if p >= 2:
                        dve.wait_ge(S("s_ready"), p - 1)
                    if p >= PAIRS - SHARED:
                        dve.wait_ge(S("c_done"), p - 1)
                    for s in range(2):
                        r = sm(S_R)[:, 2 * p + s:2 * p + s + 1].broadcast_to([P, TT])
                        for c, xx in ((0, xr), (1, xi)):
                            ins = v.tensor_tensor_scan(zt[:, p % 2, 2 * c + s, :], r, xx[:, s, :], 0.0, ALU.mult, ALU.add)
                    vec.link(ins)
                    vec.tell(v.tensor_tensor(s_tmp[p % 2][:, 1], zt[:, p % 2, 2:4, M:TT], cs[:, :, M:TT], ALU.mult),
                             S("z_ready"), p + 1)
                    if p >= PAIRS - SHARED:
                        so, st = s_out[p % 2], s_tmp[p % 2]
                        vec.link(v.tensor_tensor(so[:, 1], zt[:, p % 2, 0:2, M:TT], sn[:, :, M:TT], ALU.mult))
                        vec.tell(v.tensor_tensor(so[:, 1], so[:, 1], st[:, 1], ALU.add), S("s_imag"), p - PAIRS + SHARED + 1)
                dve.wait_ge(S("c_done"), PAIRS)
                for c in range(4):
                    ins = v.scalar_tensor_tensor(us[:, c, M:TT], us[:, c, M:TT], col("ssm_d_2", c),
                                                 bank[6 + c // 2][:, c % 2 * T:(c % 2 + 1) * T], ALU.mult, ALU.add)
                vec.tell(ins, S("s5_y"))

            @block.gpsimd
            def _(pool):
                g = nc.gpsimd
                pool.wait_ge(S("s5_unit"), 1)
                poo.link(g.memset(er[:, :, 0:1], 1.0))
                poo.link(g.memset(ei[:, :, 0:1], 0.0))
                n = 1
                while n < TT:
                    w = min(n, TT - n)
                    for half in range(2):
                        o = slice(8 * half, 8 * half + 8)
                        br = sm(S_ER)[:, o].unsqueeze(2).broadcast_to([P, 8, w])
                        bi = sm(S_EI)[:, o].unsqueeze(2).broadcast_to([P, 8, w])
                        ta, tb = (e_t[:, k, 0:8 * min(w, P)].rearrange("p (s t) -> p s t", s=8) for k in range(2))
                        lo_r, lo_i, hi_r, hi_i = er[:, o, 0:w], ei[:, o, 0:w], er[:, o, n:n + w], ei[:, o, n:n + w]
                        poo.link(g.tensor_tensor(hi_r, lo_r, br, ALU.mult))
                        poo.link(g.tensor_tensor(ta, lo_i, bi, ALU.mult))
                        poo.link(g.tensor_tensor(hi_r, hi_r, ta, ALU.subtract))
                        poo.link(g.tensor_tensor(hi_i, lo_i, br, ALU.mult))
                        poo.link(g.tensor_tensor(tb, lo_r, bi, ALU.mult))
                        poo.link(g.tensor_tensor(hi_i, hi_i, tb, ALU.add))
                    poo.link(g.tensor_tensor(sm(S_E2R), sm(S_ER), sm(S_ER), ALU.mult))
                    poo.link(g.tensor_tensor(sm(S_E2I), sm(S_EI), sm(S_EI), ALU.mult))
                    poo.link(g.tensor_tensor(sm(S_EI), sm(S_ER), sm(S_EI), ALU.mult))
                    poo.link(g.tensor_tensor(sm(S_EI), sm(S_EI), sm(S_EI), ALU.add))
                    poo.link(g.tensor_tensor(sm(S_ER), sm(S_E2R), sm(S_E2I), ALU.subtract))
                    n *= 2
                pool.sem_inc(S("tables"), 1)
                for p in range(PAIRS):
                    cs, sn = er[:, 2 * p:2 * p + 2, M:TT], ei[:, 2 * p:2 * p + 2, M:TT]
                    zr, zi = zt[:, p % 2, 0:2, M:TT], zt[:, p % 2, 2:4, M:TT]
                    pool.wait_ge(S("z_ready"), p + 1)
                    if p >= 2:
                        pool.wait_ge(S("c_done"), p - 1)
                    so, st = s_out[p % 2], s_tmp[p % 2]
                    poo.link(g.tensor_tensor(so[:, 0], zr, cs, ALU.mult))
                    poo.link(g.tensor_tensor(st[:, 0], zi, sn, ALU.mult))
                    real = g.tensor_tensor(so[:, 0], so[:, 0], st[:, 0], ALU.subtract)
                    if p >= PAIRS - SHARED:
                        poo.tell(real, S("s_ready"), p + 1)
                        continue
                    poo.link(real)
                    poo.link(g.tensor_tensor(so[:, 1], zr, sn, ALU.mult))
                    poo.tell(g.tensor_tensor(so[:, 1], so[:, 1], st[:, 1], ALU.add), S("s_ready"), p + 1)

            @block.scalar
            def _(act):
                a = nc.scalar
                qn = {"n": 0}

                def read_unit(dst, src):
                    act.wait_ge(S("qkv_done"), qn["n"] + 1)
                    a.activation(dst, src, ACT.Copy).then_inc(S("qkv_read"), 1)
                    qn["n"] += 1

                ldt = par[:, at["ssm_log_dt_2"]:at["ssm_log_dt_2"] + 16]
                sca.tell(a.activation(sm(S_DT), ldt, ACT.Exp), S("s5_dt"))
                z_reads(act, 2)
                act.wait_ge(S("s5_angle"), 1)
                a.activation(sm(S_R), sm(S_X), ACT.Exp)
                a.activation(sm(S_TANH), sm(S_X), ACT.Tanh, scale=0.5)
                a.activation(sm(S_SIN), sm(S_TH), ACT.Sin)
                sca.tell(a.activation(sm(S_HALF), sm(S_TH), ACT.Sin, scale=0.5), S("s5_sines"))
                for k in range(8):
                    read_unit(vc[:, k, :], bank[2 + qn["n"] % 4][:, 0:TT])
                for st in range(3):
                    for half in range(2):
                        n = M if st == 0 else P
                        read_unit(vt[0:n, st, half * 512:(half + 1) * 512], bank[2 + qn["n"] % 4][0:n, :])
                z_reads(act, 2)
                for c in range(8):
                    act.wait_ge(S("ml_conv"), c + 1)
                    a.activation(xc[:, c, :], xc[:, c, :], ACT.Silu).then_inc(S("xc_ready"), 1)
                for dst in (qc, kc):
                    for k in range(8):
                        read_unit(dst[:, k, :], bank[2 + qn["n"] % 4][:, 0:TT])
                z_reads(act, 4)
                for b in range(2):
                    act.wait_ge(drained[b], ev_at.banks[b] + 1)
                sca.tell(a.activation(zsig.rearrange("p c t -> p (c t)"), zsig.rearrange("p c t -> p (c t)"), ACT.Sigmoid),
                         S("z_sigmoid"))
                act.wait_ge(S("ml_abs"), 1)
                ab, mx = rows[0:4, 4, :], rows[0:4, 3, :]
                sca.link(a.activation(ab, ab, ACT.Exp, scale=-1.0))
                sca.tell(a.activation(ab, ab, ACT.Ln, bias=ones[0:4, 0:1]), S("ml_log"))
                act.wait_ge(S("ml_rows"), 1)
                sca.tell(a.activation(mx, mx, ACT.Exp, scale=-1.0), S("ml_expm"))
                z_reads(act, 2)
                for hh in range(4):
                    d = dmat[hh % 2]
                    act.wait_ge(S("head_logs"), hh + 1)
                    a.activation(d[:, 0:384], d[:, 0:384], ACT.Exp)
                    sca.tell(a.activation(d[0:M, 384:640], d[0:M, 384:640], ACT.Exp), S("head_exp"), hh + 1)
                    z_reads(act, 1)
                z_reads(act, 2)
                act.wait_ge(S("ml_inverse"), 1)
                sca.tell(a.activation(rs4, rs4, ACT.Sqrt), S("ml_root"))
                act.wait_ge(S("ml_out"), 1)
                for p in range(PAIRS):
                    act.wait_ge(S("bu_done"), p + 1)
                    if p >= 2:
                        act.wait_ge(S("bu_turned"), p - 1)
                    for n in range(4):
                        a.activation(bu[:, p % 2, n, :], bank[2 + n][:, 0:TT], ACT.Copy).then_inc(S("bu_ready"), 1)
                    z_reads(act, 1)
                for b in range(2):
                    act.wait_ge(drained[b], ev_at.banks[b] + 1)
                sca.link(a.activation(zg[:, 8:24, :].rearrange("p c t -> p (c t)"),
                                      zg[:, 8:24, :].rearrange("p c t -> p (c t)"), ACT.Sigmoid))
                nc.scalar.activation(spare[:], ones[:, 0:1], ACT.Gelu_apprx_tanh)
                act.wait_ge(S("s5_y"), 1)
                sca.link(a.activation(us[:, :, M:TT], us[:, :, M:TT], ACT.Gelu_apprx_tanh))

            @block.tensor
            def _(pe):
                mm = nc.tensor.matmul
                blockdiag = [ring[:, s, :].rearrange("p (k n) -> p k n", n=P) for s in (4, 5, 6)]
                un = {"n": 0}

                def unit_bank():
                    n = un["n"]
                    if n >= 4:
                        pe.wait_ge(S("qkv_read"), n - 3)
                    un["n"] += 1
                    return bank[2 + n % 4]

                spans = ((0, M), (M, P), (M + P, P))
                z_products(pe, 2)
                pe.wait_ge(full[6], 16 * (bd[2] + 1))
                for k in range(8):
                    ins = mm(unit_bank()[:, 0:TT], blockdiag[2][:, k, :], xm[:, k, :], start=True, stop=True)
                    ins.then_inc(S("qkv_done"), 1)
                for st, (lo, n) in enumerate(spans):
                    for half in range(2):
                        b = unit_bank()
                        for k in range(4):
                            ins = mm(b[0:n, k * P:(k + 1) * P], xm[:, 4 * half + k, lo:lo + n],
                                     blockdiag[2][:, 4 * half + k, :], start=True, stop=True)
                        ins.then_inc(S("qkv_done"), 1)
                z_products(pe, 2)
                pe.wait_ge(S("xc_ready"), 8)
                for w in range(2):
                    pe.wait_ge(full[4 + w], 16 * (bd[w] + 1))
                    for k in range(8):
                        ins = mm(unit_bank()[:, 0:TT], blockdiag[w][:, k, :], xc[:, k, :], start=True, stop=True)
                        ins.then_inc(S("qkv_done"), 1)
                z_products(pe, 4)
                pe.wait_ge(S("qkv_read"), 30)
                w_if = g2("w_if").rearrange("p (k n) -> p k n", n=8)
                for n in range(24):
                    src = (qc, kc, vc)[n // 8][:, n % 8, :]
                    ins = mm(bank[6][0:8, 0:TT], w_if[:, n, :], src, start=n == 0, stop=n == 23)
                ins.then_inc(S("if_sum"), 1)
                for w in range(3):
                    pe.sem_inc(used[4 + w], 1)
                pe.wait_ge(S("if_rows"), 1)
                mm(bank[7][0:4, 0:TT], ident[0:8, 0:4], rows[0:8, 5, :], start=True, stop=True)
                mm(bank[6][0:4, 0:TT], ident[0:8, 4:8], rows[0:8, 5, :], start=True, stop=True).then_inc(S("if_split"), 1)
                z_products(pe, 2)
                pe.wait_ge(S("ml_rows"), 1)
                for st, (lo, n) in enumerate(spans):
                    ins = mm(bank[5][0:n, 4 * st:4 * st + 4], rows[0:4, 0, lo:lo + n], ident[0:4, 0:4], start=True, stop=True)
                ins.then_inc(S("ml_cols"), 1)
                pe.wait_ge(S("ml_expm"), 1)
                pe.wait_ge(S("ml_cols_read"), 1)
                sel = g2("sel").rearrange("p (h n) -> p h n", h=4)
                for hh in range(4):
                    if hh:
                        pe.wait_ge(S("head_read"), hh)
                    mm(bank[2][:, 0:T], sel[0:4, hh, :], rows[0:4, 2, M:TT], start=True, stop=True)
                    mm(bank[2][:, T:2 * T], sel[0:4, hh, :], rows[0:4, 3, M:TT], start=True, stop=True)
                    for st, (b, off, tlo) in enumerate(((4, 0, 0), (3, 0, 0), (3, T, P))):
                        lo, n = spans[st]
                        for c in (2 * hh, 2 * hh + 1):
                            ins = mm(bank[b][0:n, off:off + T - tlo], kc[:, c, lo:lo + n], qc[:, c, M + tlo:TT],
                                     start=c % 2 == 0, stop=c % 2 == 1)
                    ins.then_inc(S("head_scores"), 1)
                    z_products(pe, 1)
                    pe.wait_ge(S("head_weights"), hh + 1)
                    d = dmat[hh % 2]
                    wts = ((d[:, 0:T], 1, P, 0), (d[:, T:T + P], 2, P, P), (d[0:M, 384:640], 0, M, 0))
                    for e in range(3):
                        for j, (w, st, n, tlo) in enumerate(wts):
                            lhs = ones[0:n, :] if e == 2 else vt[0:n, st, hh * T + e * P:hh * T + (e + 1) * P]
                            dst = bank[6][:, tlo:T] if e == 2 else bank[5][:, e * T + tlo:(e + 1) * T]
                            ins = mm(dst, lhs, w, start=j == 0, stop=j == 2)
                    ins.then_inc(S("head_sums"), 1)
                z_products(pe, 2)
                pe.wait_ge(S("ml_squares"), 1)
                for c in range(8):
                    hh = c // 2
                    ins = mm(bank[2 + hh // 2][:, hh % 2 * T:(hh % 2 + 1) * T], ones, vc[:, c, 0:T],
                             start=c % 2 == 0, stop=c % 2 == 1)
                ins.then_inc(S("ml_sums"), 1)
                pe.wait_ge(S("ml_inverse"), 1)
                b_re, b_im = (g2(n).rearrange("p (c n) -> p c n", c=4) for n in ("b_re", "b_im"))
                c_re, c_im = (g2(n).rearrange("p (s c) -> p s c", s=16) for n in ("c_re", "c_im"))

                def states(p):
                    pe.wait_ge(S("s_ready"), p + 1)
                    if p >= PAIRS - SHARED:
                        pe.wait_ge(S("s_imag"), p - PAIRS + SHARED + 1)
                    for s in range(2):
                        j = 2 * p + s
                        c, r = j // 4, 32 * (j % 4)
                        dst = bank[6 + c // 2][r:r + 32, c % 2 * T:(c % 2 + 1) * T]
                        mm(dst, c_re[:, j, :], s_out[p % 2][:, 0, s, :], start=True, stop=False)
                        ins = mm(dst, c_im[:, j, :], s_out[p % 2][:, 1, s, :], start=False, stop=True)
                    ins.then_inc(S("c_done"), 1)

                for p in range(PAIRS):
                    if p:
                        pe.wait_ge(S("bu_ready"), 4 * p)
                    for s in range(2):
                        j = 2 * p + s
                        c, r = j // 4, 32 * (j % 4)
                        for k, w in enumerate((b_re, b_im)):
                            ins = mm(bank[2 + 2 * s + k][:, 0:TT], w[r:r + 32, c, :], us[r:r + 32, c, :], start=True, stop=True)
                        if s == 0:
                            turn(pe, ins)
                    ins.then_inc(S("bu_done"), 1)
                    z_products(pe, 1)
                    if p >= 2:
                        states(p - 2)
                states(PAIRS - 2)
                states(PAIRS - 1)
            pe_at.advance((4, 5, 6), 1, None)
            ev_at.advance((4, 5, 6), 1, None)

        a10 = Area(arena)
        glu, mixed, part = a10.take(4, T), a10.take(8, T), a10.take(4, T)
        assert a10.at <= a6.at
        y5 = us[:, :, M:TT]
        combos = ((5, 6, 3), (0, 1, 2), (7, 4, 5), (6, 3, 0))
        cycle = (1, 2, 7, 4, 5, 6, 3, 0)
        QS = (7, 4, 5, 6, 3, 0) * 2 + (7, 4, 5, 6)
        sequence = [7, 4] + [s for slots in combos for s in slots] + list(cycle)
        to_split = [(s, pe_at.rounds[s] + sequence[:m].count(s) + 1) for m, s in enumerate(sequence)
                    if m >= 14 or (m >= 2 and (m - 2) % 3)]
        mix_high = Area(arena_parts[17152]).take(SLOTS, D)
        mp = Area(arena_parts[25344])
        ml_high, ml_low, mixed_high, mixed_low = (mp.take(8, T) for _ in range(4))
        mix_base = split["blocks"]
        with nc.Block() as block:
            @block.sync
            def _(sp):
                for slots in combos[2:]:
                    load(sp, slots)
                load(sp, cycle)
                load(sp, (1, 2))
                load(sp, QS[0:6])

            @block.tensor
            def _(pe):
                def gate(q, w, b, i):
                    for n in range(2):
                        for k in range(4):
                            mm = nc.tensor.matmul(b[:, n * T:(n + 1) * T], w[:, 4 * n + k, :], y5[:, k, :],
                                                  start=k == 0, stop=k == 3)
                    return mm

                def branches(q, w, b, i):
                    if q == 0:
                        return gate(q, w, b, i)
                    return parted(2 * combo["n"] + q - 1, b, ml_high, ml_low)

                def onto(q, w, b, i):
                    return parted(8 + q, b, mixed_high, mixed_low)

                combo = {"n": 0}

                def parted(m, b, moving_high, moving_low):
                    s = to_split[m][0]
                    pe.wait_ge(S("low"), mix_base + m + 1)
                    for k in range(KT):
                        c = slice(k * P, (k + 1) * P)
                        ins = three(b[:, 0:T], (mix_high[:, s, c], low[:, s, c]), (moving_high[:, k, :], moving_low[:, k, :]),
                                    k == 0, k == KT - 1)
                    return ins

                project(pe, (7, 4), (0, 1), 1, gate)
                pe.wait_ge(S("s5_gated"), 1)
                pe.wait_ge(S("h_parts"), split["h"] + 1)
                for n, slots in enumerate(combos):
                    combo["n"] = n
                    project(pe, slots, ((2, 3, 4), (5, 6, 7))[n % 2], 1, branches)
                pe.wait_ge(S("mixed"), 4)
                project(pe, cycle, range(4), 1, onto)

            @block.scalar
            def _(act):
                def sigmoids(q, b, i):
                    for n in range(2):
                        ins = nc.scalar.activation(glu[:, 2 * q + n, :], b[:, n * T:(n + 1) * T], ACT.Sigmoid,
                                                   bias=col("ssm_b_glu_2", 2 * q + n))
                    return ins
                nc.scalar.activation(ml_high, h_ml, ACT.Copy).then_inc(S("h_rounded"), 1)
                for m in range(2):
                    part_high(act, mix_high, *to_split[m])
                evacuate(act, (7, 4), (0, 1), 1, sigmoids)
                for m in range(2, 16):
                    part_high(act, mix_high, *to_split[m])

            @block.gpsimd
            def _(pool):
                for m in range(16):
                    part_low(pool, nc.gpsimd, mix_high, to_split[m][0], mix_base + m + 1)

            @block.vector
            def _(dve):
                v = nc.vector
                dve.wait_ge(S("h_rounded"), split["h"] + 1)
                v.tensor_tensor(ml_low, h_ml, ml_high.bitcast(F32), ALU.subtract).then_inc(S("h_parts"), 1)
                for b in range(2):
                    dve.wait_ge(drained[b], ev_at.banks[b] + 1)
                vec.tell(v.tensor_tensor(y5, y5, glu, ALU.mult), S("s5_gated"))
                for n, slots in enumerate(combos):
                    def mix(q, b, i):
                        if q == 0:
                            return v.tensor_tensor(part[:, 0:2, :], b[:, :].rearrange("p (c t) -> p c t", c=2),
                                                   gs_g[:, 2 * n:2 * n + 2, :], ALU.mult)
                        return v.tensor_tensor(part[:, 1 + q, :], b[:, 0:T], gm_g[:, 2 * n + q - 1, :], ALU.mult)
                    banks = ((2, 3, 4), (5, 6, 7))[n % 2]
                    evacuate(dve, slots, banks, 1, mix)
                    for b in banks:
                        dve.wait_ge(drained[b], ev_at.banks[b] + 1)
                    two = slice(2 * n, 2 * n + 2)
                    vec.link(v.tensor_tensor(mixed[:, two, :], part[:, 0:2, :], part[:, 2:4, :], ALU.add))
                    vec.link(v.tensor_copy(mixed_high[:, two, :], mixed[:, two, :]))
                    vec.tell(v.tensor_tensor(mixed_low[:, two, :], mixed[:, two, :], mixed_high[:, two, :].bitcast(F32),
                                             ALU.subtract), S("mixed"), n + 1)
                evacuate(dve, cycle, range(4), 1, lambda q, b, i: v.tensor_tensor(
                    x[:, q, :], x[:, q, :], b[:, 0:T], ALU.add))
                dve.wait_ge(drained[3], ev_at.banks[3] + 1)
        split["blocks"] += 16
        split["h"] += 1

        ge = Area(arena)
        G = ge.take(P, T)
        early = ge.take(EARLY, T)
        parts = Area(arena_parts[ge.at])
        h_high = parts.take(KT, T)
        h_low = h_parts[:, :, 0:T]
        ge.at += parts.at
        expert_high = parts.take(2, D)
        chosen = ge.take(3, T)
        ap_ = Area(arena)
        qp = ap_.take(16, T)
        sc = ap_.take(2, 16, P)
        work = ap_.take(4, T)
        sv = ap_.take(2, 16, 16)
        CANDIDATES = ((0, 0, 2, 16), (32, 2, 2, 8), (48, 4, 4, 4), (64, 8, 8, 2))
        N_CAND = 80
        lines = [(float(nb), float(start // nb - a0)) for start, a0, na, nb in CANDIDATES]
        cand = ap_.take(8, N_CAND)
        cs, ci = ap_.take(8, 16), ap_.take(8, 16)
        flat_f, which_f, hot = ap_.take(P), ap_.take(2, P), ap_.take(P, 16)
        shift_u, shift_f = ap_.take(4, P).bitcast(U32), ap_.take(4, P)
        spread = Area(arena, 25344)
        hot = [hot] + [spread.take(P, 16) for _ in range(3)]
        si, tops = ([spread.take(a, 16), spread.take(a, 16)] for a in (16, 8))
        assert spread.at <= P * T
        picked = ap_.take(2, 3, P)
        sums = ap_.take(2, 8)
        si_u = ap_.take(2, 16, 16).bitcast(U32)
        ci_u = ci.bitcast(U32)
        assert ap_.at <= 17152

        ER = (3, 0, 1, 2, 7, 4, 5, 6)
        PEER_BANKS = (4, 5, 6, 7)

        SQ = QS + ER
        fillings = []
        for m, s in enumerate(SQ):
            fillings.append(pe_at.rounds[s] + SQ[:m].count(s) + (s in (1, 2)) + 1)
        q_high = Area(arena_parts[17152]).take(SLOTS, D)
        q_base = split["blocks"]

        def hot_times_keys(engine, tt, s):
            h4 = hot[2 * tt + s].rearrange("p (h k) a -> p h k a", h=8)
            ki = si[tt].rearrange("p (h s) k -> p h s k", s=2)[:, :, s, :]
            return engine.tensor_tensor(h4, h4, ki.unsqueeze(2).broadcast_to([P, 8, 16, 16]), ALU.mult)

        def sq_high(act, m):
            part_high(act, q_high, SQ[m], fillings[m])

        rms_norm(lambda k: x[:, k, :], lambda k: h[:, k, 0:T], "norm2_g_2", RMS_EPS, Area(arena).take(KT, T),
                 beside=(lambda act: [sq_high(act, m) for m in range(AHEAD)], lambda dve: None))
        with nc.Block() as block:
            @block.sync
            def _(sp):
                load(sp, QS[6:12])
                load(sp, QS[12:16])
                load(sp, ER)
                load(sp, ER)

            @block.tensor
            def _(pe):
                def scores(n):
                    if n >= 2:
                        pe.wait_ge(S("scores_read"), n - 1)
                    w = ring[:, 1 + n // 8, n % 8 * P:(n % 8 + 1) * P]
                    for tt in range(2):
                        mm = nc.tensor.matmul(bank[2 + n % 2][:, tt * P:(tt + 1) * P], qp[:, n, tt * P:(tt + 1) * P], w,
                                              start=True, stop=True)
                    mm.then_inc(S("scores_done"), 1)

                keys_in = [16 * (pe_at.rounds[s] + 1) for s in (1, 2)]
                for b in (2, 3):
                    pe.wait_ge(drained[b], pe_at.banks[b] + 1)
                def product(m):
                    def mats(q, w, b, i):
                        pe.wait_ge(S("low"), q_base + m + q + 1)
                        for k in range(KT):
                            c = slice(k * P, (k + 1) * P)
                            ins = three(b[:, 0:T], (q_high[:, SQ[m + q], c], low[:, SQ[m + q], c]),
                                        (h_high[:, k, :], h_low[:, k, :]), k == 0, k == KT - 1)
                        return ins
                    return mats

                pe.wait_ge(S("h_parts"), split["h"] + 2)
                for n in range(16):
                    project(pe, QS[n:n + 1], (n % 2,), 1, product(n))
                    if n % 8 == 1:
                        pe.wait_ge(full[1 + n // 8], keys_in[n // 8])
                    if n:
                        b = (n - 1) % 2
                        pe.wait_ge(drained[b], pe_at.banks[b] + 1)
                        scores(n - 1)
                pe.wait_ge(drained[1], pe_at.banks[1] + 1)
                scores(15)
                pe.wait_ge(S("scores_read"), 16)
                for s in (1, 2):
                    pe.sem_inc(used[s], 1)
                pe_at.advance((1, 2), 1, None)
                for b in range(4):
                    pe.wait_ge(drained[b], pe_at.banks[b] + 1)
                    for c in range(4):
                        k = 4 * (b % 2) + c
                        mm = nc.tensor.matmul(bank[b][:, c * P:(c + 1) * P], x[:, k, b // 2 * P:(b // 2 + 1) * P], ident,
                                              start=c == 0, stop=False)
                project(pe, ER, PEER_BANKS, 1, product(16))
                for b in PEER_BANKS[0:2]:
                    pe.wait_ge(drained[b], pe_at.banks[b] + 1)
                pe.wait_ge(S("picked"), 2)
                for tt in range(2):
                    for n in range(3):
                        mm = nc.tensor.transpose(bank[4 + tt][:, n * P:(n + 1) * P], picked[:, tt, n, :], ident)
                mm.then_inc(S("chosen_t"), 1)

            @block.scalar
            def _(act):
                def read_scores(n):
                    act.wait_ge(S("scores_done"), n + 1)
                    nc.scalar.activation(sc[:, :, n, :], bank[2 + n % 2][:, 0:T].rearrange("p (a n) -> p a n", a=2),
                                         ACT.Copy).then_inc(S("scores_read"), 1)

                for half in range(2):
                    k = slice(4 * half, 4 * half + 4)
                    nc.scalar.activation(h_high[:, k, :], h[:, k, 0:T], ACT.Copy).then_inc(S("h_rounded"), 1)
                for n in range(16):
                    if n + AHEAD < 18:
                        sq_high(act, n + AHEAD)
                    evacuate(act, QS[n:n + 1], (n % 2,), 1, lambda q, b, i: nc.scalar.activation(
                        qp[:, n, :], b[:, 0:T], ACT.Copy))
                    if n:
                        read_scores(n - 1)
                read_scores(15)
                ev_at.advance((1, 2), 1, None)
                for n in range(7):
                    if n < 6:
                        sq_high(act, 18 + n)
                    evacuate(act, ER[n:n + 1], PEER_BANKS[n % 4:n % 4 + 1], 1, lambda q, b, i: nc.scalar.activation(
                        early[:, n, :], b[:, 0:T], ACT.Gelu_apprx_tanh))
                for tt in range(2):
                    act.wait_ge(S("soft_arg"), tt + 1)
                    nc.scalar.activation(tops[tt], tops[tt], ACT.Exp).then_inc(S("soft_exp"), 1)

            @block.gpsimd
            def _(pool):
                for m, s in enumerate(SQ):
                    part_low(pool, nc.gpsimd, q_high, s, q_base + m + 1)
                for n in range(3):
                    pool.wait_ge(S("hot_made"), n + 1)
                    poo.link(hot_times_keys(nc.gpsimd, n // 2, n % 2))
                    nc.gpsimd.tensor_tensor(hot[n][:, :, 0:8], hot[n][:, :, 0:8], hot[n][:, :, 8:16], ALU.add)\
                        .then_inc(S("hot_keys"), 1)

            @block.vector
            def _(dve):
                v = nc.vector

                def step(ins):
                    vec.n += 1
                    ins.then_inc(vec.steps, 1)
                    return vec.n

                def top16(rows, width):
                    found = [step(v.max(val[:, 0:8], src)) for val, ind, src in rows]
                    for r, (val, ind, src) in enumerate(rows):
                        dve.wait_ge(vec.steps, found[r])
                        step(v.max_index(ind[:, 0:8], val[:, 0:8], src))
                        found[r] = step(v.match_replace(work[:, r, 0:width], val[:, 0:8], src, -3e38))
                    for r, (val, ind, src) in enumerate(rows):
                        dve.wait_ge(vec.steps, found[r])
                        found[r] = step(v.max(val[:, 8:16], work[:, r, 0:width]))
                    for r, (val, ind, src) in enumerate(rows):
                        dve.wait_ge(vec.steps, found[r])
                        last_one = step(v.max_index(ind[:, 8:16], val[:, 8:16], work[:, r, 0:width]))
                    dve.wait_ge(vec.steps, last_one)

                for half in range(2):
                    k = slice(4 * half, 4 * half + 4)
                    dve.wait_ge(S("h_rounded"), split["h"] + half + 1)
                    v.tensor_tensor(h_low[:, k, :], h[:, k, 0:T], h_high[:, k, :].bitcast(F32), ALU.subtract)\
                        .then_inc(S("h_parts"), 1)
                for n in range(0, 16, 2):
                    dve.wait_ge(S("scores_read"), n + 2)
                    top16([(sv[:, tt, m], si_u[:, tt, m], sc[:, tt, m]) for tt in range(2) for m in (n, n + 1)], P)
                def candidates(tt):
                    vec.link(v.tensor_copy(si[tt], si_u[:, tt]))
                    by_half = sv[:, tt].rearrange("p (h s) k -> p h s k", s=2)
                    for start, a0, na, nb in CANDIDATES:
                        first_s = by_half[:, :, 0, a0:a0 + na].unsqueeze(3).broadcast_to([P, 8, na, nb])
                        second_s = by_half[:, :, 1, 0:nb].unsqueeze(2).broadcast_to([P, 8, na, nb])
                        ins = v.tensor_tensor(cand[:, :, start:start + na * nb].rearrange("p h (a b) -> p h a b", a=na),
                                              first_s, second_s, ALU.add)
                    vec.link(ins)
                    for n in (0, 4):
                        top16([(cs[:, m], ci_u[:, m], cand[:, m]) for m in range(n, n + 4)], N_CAND)
                    vec.tell(v.tensor_tensor(tops[tt], cs, cs[:, :, 0:1].broadcast_to([P, 8, 16]), ALU.subtract),
                             S("soft_arg"), tt + 1)
                    flat = ci_u.rearrange("p h k -> p (h k)")
                    for j in range(4):
                        ins = v.tensor_scalar(shift_u[:, j, :], flat, 4 - j, None, ALU.logical_shift_right)
                    v.tensor_copy(flat_f, flat)
                    vec.link(ins)
                    vec.link(v.tensor_copy(shift_f, shift_u))
                    a_f, b_f = which_f[:, 0, :], which_f[:, 1, :]
                    (_, less) = lines[1]
                    vec.link(v.scalar_tensor_tensor(a_f, shift_f[:, 1, :], -less, shift_f[:, 0, :], ALU.add, ALU.max))
                    for j in (2, 3):
                        vec.link(v.scalar_tensor_tensor(a_f, shift_f[:, j, :], -lines[j][1], a_f, ALU.add, ALU.max))
                    for j, (scale_a, less) in enumerate(lines):
                        dst = b_f if j == 0 else shift_f[:, j, :]
                        ins = v.scalar_tensor_tensor(dst, a_f, -scale_a, flat_f, ALU.mult, ALU.add)
                    vec.link(ins)
                    for j in (1, 2, 3):
                        vec.link(v.scalar_tensor_tensor(b_f, shift_f[:, j, :], -lines[j][0] * lines[j][1], b_f,
                                                        ALU.add, ALU.max))
                    for s in range(2):
                        vec.tell(v.tensor_tensor(hot[2 * tt + s], which_f[:, s, :].unsqueeze(2).broadcast_to([P, P, 16]),
                                                 iota[:, 0:16].unsqueeze(1).broadcast_to([P, P, 16]), ALU.is_equal),
                                 S("hot_made"), 2 * tt + s + 1)

                def pick(tt):
                    for s in range(2):
                        if (tt, s) != (1, 1):
                            dve.wait_ge(S("hot_keys"), 2 * tt + s + 1)
                        row = hot[2 * tt + s] if (tt, s) == (1, 1) else hot[2 * tt + s][:, :, 0:8]
                        vec.link(v.tensor_reduce(picked[:, tt, s, :], row, AX, ALU.add))
                    dve.wait_ge(S("soft_exp"), tt + 1)
                    vec.link(v.tensor_reduce(sums[:, 0, :], tops[tt], AX, ALU.add))
                    vec.link(v.reciprocal(sums[:, 1, :], sums[:, 0, :]))
                    vec.tell(v.tensor_tensor(picked[:, tt, 2, :].rearrange("p (h k) -> p h k", h=8), tops[tt],
                                             sums[:, 1, :].unsqueeze(2).broadcast_to([P, 8, 16]), ALU.mult),
                             S("picked"), tt + 1)

                candidates(0)
                candidates(1)
                vec.link(hot_times_keys(v, 1, 1))
                pick(0)
                pick(1)
                dve.wait_ge(S("chosen_t"), 1)
                for tt in range(2):
                    ins = v.tensor_copy(chosen[:, :, tt * P:(tt + 1) * P],
                                        bank[4 + tt][:, 0:3 * P].rearrange("p (n t) -> p n t", n=3))
                vec.link(ins)
        split["blocks"] += len(SQ)
        split["h"] += 2

        quads = T // 4
        hots = [x[:, 4 * n:4 * n + 4, :].rearrange("p a t -> p (a t)").rearrange("p (c q n) -> p c q n", c=2, q=4)
                for n in range(2)] + [ge.take(2, 4, P)]
        with nc.Block() as block:
            def all_quads(eng, one):
                with eng.Fori(0, quads // 3) as i:
                    for b in range(3):
                        one(b, i)
                for b in range(quads % 3):
                    one(b, quads // 3)

            def of_tokens(n, i, b):
                return chosen[:, n, bass.ds(i * 12 + 4 * b, 4)].unsqueeze(2).broadcast_to([P, 4, P])

            @block.vector
            def _(dve):
                keys = iota.unsqueeze(1).broadcast_to([P, 4, P])

                def one(b, i):
                    dve.wait_ge(S("rows_free"), i * 3 + (b + 1))
                    nc.vector.tensor_tensor(hots[b][:, 1], keys, of_tokens(1, i, b), ALU.is_equal)
                    nc.vector.tensor_tensor(hots[b][:, 0], keys, of_tokens(0, i, b), ALU.is_equal)\
                        .then_inc(S("rows_made"), 1)
                all_quads(dve, one)

            @block.gpsimd
            def _(pool):
                def one(b, i):
                    pool.wait_ge(S("rows_made"), i * 3 + (b + 1))
                    nc.gpsimd.tensor_tensor(hots[b][:, 0], hots[b][:, 0], of_tokens(2, i, b), ALU.mult)\
                        .then_inc(S("rows_ready"), 1)
                all_quads(pool, one)

            @block.tensor
            def _(pe):
                def one(b, i):
                    pe.wait_ge(S("rows_ready"), i * 3 + (b + 1))
                    pe.wait_ge(S("gates_read"), i * 3 + (b + 1))
                    for q in range(4):
                        mm = nc.tensor.matmul(bank[4 + b][:, q * P:(q + 1) * P], hots[b][:, 0, q, :], hots[b][:, 1, q, :],
                                              start=True, stop=True)
                    mm.then_inc(S("rows_free"), 1)
                pe.sem_inc(S("rows_free"), 3)
                all_quads(pe, one)

            @block.scalar
            def _(act):
                def one(b, i):
                    act.wait_ge(S("rows_free"), i * 3 + (b + 4))
                    nc.scalar.activation(G[:, :, bass.ds(i * 12 + 4 * b, 4)],
                                         bank[4 + b][:, :].rearrange("p (q n) -> p n q", q=4), ACT.Copy)\
                        .then_inc(S("gates_read"), 1)
                act.sem_inc(S("gates_read"), 3)
                all_quads(act, one)

        high = expert_high
        gate_high, gate_low = x_parts[:, 0:4, :], x_parts[:, 4:8, :]
        rounds = (P - EARLY) // 8
        slot_base = {s: pe_at.rounds[s] for s in ER}
        bank_base = {b: pe_at.banks[b] - 2 for b in PEER_BANKS}
        HALF, halves = D // 2, split["blocks"]

        def uses(m, i, ahead=0):
            return i * 2 + (slot_base[ER[m % 8]] + m // 8 + ahead)

        with nc.Block() as block:
            @block.sync
            def _(sp):
                load(sp, ER, 2 * rounds)

            @block.tensor
            def _(pe):
                mm = nc.tensor.matmul

                def experts(m, i, s):
                    slot, b = ER[m % 8], PEER_BANKS[s % 4]
                    pe.wait_ge(drained[b], i * 2 + (bank_base[b] + s // 4 + 3))
                    for k in range(KT):
                        if k % 4 == 0:
                            pe.wait_ge(S("low"), i * 32 + (halves + 2 * m + k // 4 + 1))
                        w = slice(k * P, (k + 1) * P)
                        mm(bank[b][:, 0:T], high[:, m % 2, w], h_high[:, k, :], start=k == 0, stop=False)
                        mm(bank[b][:, 0:T], high[:, m % 2, w], h_low[:, k, :], start=False, stop=False)
                        ins = mm(bank[b][:, 0:T], low[:, slot, w], h_high[:, k, :], start=False, stop=k == KT - 1)
                        if k == 3:
                            ins.then_inc(S("half_used"), 1)
                    ins.then_inc(used[slot], 1)

                def values(m, i, s, last_one=False):
                    slot = ER[m % 8]
                    pe.wait_ge(S("gated"), i * 8 + (s + 2))
                    for half in range(2):
                        pe.wait_ge(S("low"), i * 32 + (halves + 2 * m + half + 1))
                        w = slice(half * HALF, (half + 1) * HALF)
                        for tt in range(2):
                            b, t = bank[2 * tt + half][:, :], slice(tt * P, (tt + 1) * P)
                            mm(b, gate_high[:, s % 4, t], high[:, m % 2, w], start=False, stop=False)
                            mm(b, gate_high[:, s % 4, t], low[:, slot, w], start=False, stop=False)
                            ins = mm(b, gate_low[:, s % 4, t], high[:, m % 2, w], start=False, stop=last_one)
                        if half == 0:
                            ins.then_inc(S("half_used"), 1)
                    ins.then_inc(used[slot], 1)

                pe.sem_inc(S("half_used"), 2)
                with pe.Fori(0, rounds) as i:
                    for s in range(8):
                        experts(2 * s, i, s)
                        values(2 * s + 1, i, s)
                for s in range(8):
                    values(s, rounds, s, s == 7)

            @block.scalar
            def _(act):
                def split_high(m, i):
                    slot = ER[m % 8]
                    act.wait_ge(full[slot], i * 32 + 16 * (slot_base[slot] + m // 8 + 1))
                    act.wait_ge(S("half_used"), i * 16 + (m + 1))
                    nc.scalar.activation(high[:, m % 2, 0:HALF], ring[:, slot, 0:HALF], ACT.Copy).then_inc(S("high"), 1)
                    act.wait_ge(used[ER[(m - 2) % 8]], uses(m - 2, i, 1))
                    nc.scalar.activation(high[:, m % 2, HALF:D], ring[:, slot, HALF:D], ACT.Copy).then_inc(S("high"), 1)

                def gelu(s, i):
                    act.wait_ge(used[ER[(2 * s - 2) % 8]], uses(2 * s - 2, i, 1))
                    act.wait_ge(S("gated"), i * 8 + (s + 1))
                    b = PEER_BANKS[(s - 1) % 4]
                    nc.scalar.activation(early[:, (s - 1) % 8, :], bank[b][:, 0:T], ACT.Gelu_apprx_tanh)\
                        .then_inc(drained[b], 1)

                with act.Fori(0, rounds) as i:
                    for s in range(8):
                        split_high(2 * s, i)
                        gelu(s, i)
                        split_high(2 * s + 1, i)
                gelu(0, rounds)
                for m in range(8):
                    split_high(m, rounds)

            @block.vector
            def _(dve):
                def split_low(m, i):
                    for half in range(2):
                        dve.wait_ge(S("high"), i * 32 + (halves + 2 * m + half + 1))
                        w = slice(half * HALF, (half + 1) * HALF)
                        nc.vector.tensor_tensor(low[:, ER[m % 8], w], ring[:, ER[m % 8], w],
                                                high[:, m % 2, w].bitcast(F32), ALU.subtract).then_inc(S("low"), 1)

                with dve.Fori(0, rounds) as i:
                    for m in range(16):
                        split_low(m, i)
                for m in range(8):
                    split_low(m, rounds)

            @block.gpsimd
            def _(pool):
                p = nc.gpsimd
                pool.sem_inc(S("gated"), 1)

                def gate(s, i, m):
                    b = PEER_BANKS[s % 4]
                    pool.wait_ge(drained[b], i * 2 + (bank_base[b] + s // 4 + 2))
                    pool.wait_ge(used[ER[m % 8]], uses(m, i, 1))
                    e = early[:, s, :]
                    j = i * 8 + s
                    g = G[:, j, :] if isinstance(j, int) else G[:, bass.ds(j, 1), :].rearrange("p a t -> p (a t)")
                    p.tensor_tensor(e, e, g, ALU.mult).then_inc(S("gate_step"), 1)
                    pool.wait_ge(S("gate_step"), i * 16 + (2 * s + 1))
                    p.tensor_tensor(gate_high[:, s % 4, :].rearrange("p (a t) -> p a t", a=2),
                                    e.rearrange("p (a t) -> p a t", a=2),
                                    ones.unsqueeze(1).broadcast_to([P, 2, P]), ALU.mult).then_inc(S("gate_step"), 1)
                    pool.wait_ge(S("gate_step"), i * 16 + (2 * s + 2))
                    p.tensor_tensor(gate_low[:, s % 4, :], e, gate_high[:, s % 4, :].bitcast(F32), ALU.subtract)\
                        .then_inc(S("gated"), 1)

                with pool.Fori(0, rounds) as i:
                    for s in range(8):
                        gate(s, i, 2 * s + 1 - 8)
                for s in range(8):
                    gate(s, rounds, s - 4 if s >= 4 else 2 * s - 7)

        a_end = Area(arena)
        square, result, stat = a_end.take(4, 512), a_end.take(4, 512), a_end.take(2, 4)
        last_g = a_end.take(D)
        with nc.Block() as block:
            @block.scalar
            def _(act):
                act.dma_start(last_g, last).then_inc(S("last_in"), 16)
                for b in range(4):
                    nc.scalar.activation(square[:, b, :], bank[b][:, :], ACT.Square).then_inc(S("norm_squares"), 1)
                nc.scalar.activation(spare[:], ones[:, 0:1], ACT.Sqrt)
                act.wait_ge(S("last_mean"), 1)
                nc.scalar.activation(stat[:, :, 1:2], stat[:, :, 1:2], ACT.Sqrt).then_inc(S("last_root"), 1)

            @block.vector
            def _(dve):
                v = nc.vector
                for b in range(4):
                    dve.wait_ge(S("norm_squares"), normed["n"] * 4 + b + 1)
                    ins = v.tensor_reduce(stat[:, b // 2, 2 * (b % 2):2 * (b % 2) + 1], square[:, b, :], AX, ALU.add)
                vec.link(ins)
                vec.link(v.tensor_tensor(stat[:, :, 1:2], stat[:, :, 0:1], stat[:, :, 2:3], ALU.add))
                vec.link(v.tensor_scalar(stat[:, :, 1:2], stat[:, :, 1:2], 1.0 / D, RMS_EPS, ALU.mult, ALU.add))
                vec.tell(v.reciprocal(stat[:, :, 1:2], stat[:, :, 1:2]), S("last_mean"))
                dve.wait_ge(S("last_root"), 1)
                dve.wait_ge(S("last_in"), 16)
                for b in range(4):
                    c = b % 2 * 512
                    v.scalar_tensor_tensor(result[:, b, :], bank[b][:, :], stat[:, b // 2, 1:2], last_g[:, c:c + 512],
                                           ALU.mult, ALU.mult).then_inc(S("result"), 1)

            @block.sync
            def _(sp):
                for b in range(4):
                    c = b % 2 * 512
                    sp.wait_ge(S("result"), b + 1)
                    sp.dma_start(out[b // 2 * P:(b // 2 + 1) * P, c:c + 512], result[:, b, :]).then_inc(S("written"), 16)
                sp.wait_ge(S("written"), 64)


def _blocks(w):
    k, n = w.shape
    return w.reshape(k // P, P, n // P, P).transpose(2, 1, 0, 3).reshape(n // P, P, k)


def _columns(v):
    return v.reshape(-1, P).T


def lay_out(a):
    import numpy as np

    f32 = np.float32
    a = {k: np.asarray(v) for k, v in a.items()}
    w_in, w_in2 = a["w_in"][0], a["w_in_2"][0]
    sc, sb, rw, sg, gate = 0, 768, 1536, 2560, 3072
    order = [w_in[:, rw:rw + 1024], w_in[:, sc:sc + 768], w_in[:, sb:sb + 512], w_in[:, sg:sg + 256],
             w_in[:, sb + 512:sb + 768], w_in[:, sg + 256:sg + 512], w_in[:, gate:]]
    parts = [_blocks(w) for w in order]
    outs = np.stack([a[n][0] for n in ("sc_out", "sb_out", "rw_out", "sg_out")])
    parts.append(outs.reshape(4, 2, P, KT, P).transpose(3, 2, 0, 1, 4).reshape(KT, P, D))
    parts.append(_blocks(a["w_o"][0]))
    up = _blocks(a["w_up"][0])
    gv, down = np.stack([up[:FT], up[FT:]], 1), a["w_down"][0].reshape(FT, 1, P, D)
    parts += [gv[:2].reshape(4, P, D), np.concatenate([gv[2:], down[:-2]], 1).reshape(-1, P, D), down[-2:, 0]]
    parts.append(_blocks(w_in2[:, :1536]))
    for n in ("ml_wq_2", "ml_wk_2", "ml_wv_2"):
        w = a[n][0]
        m = np.zeros((D // 4, 4, D // 4, 4), f32)
        r = np.arange(D // 4)
        m[r, :, r, :] = w
        m = m.reshape(KT, P, KT, P)
        parts.append(np.stack([m[k, :, k, :] for k in range(KT)], 1).reshape(1, P, D))
    parts.append(_blocks(w_in2[:, 1536:]))
    glu = a["ssm_w_glu_2"][0].reshape(4, P, 2, 2, P).transpose(2, 1, 3, 0, 4).reshape(2, P, D)
    parts.append(glu)
    ssm = a["w_ssm_out_2"][0].reshape(4, P, 4, 2, P).transpose(2, 1, 3, 0, 4).reshape(4, P, D)
    ml, wo = _blocks(a["w_ml_out_2"][0]), _blocks(a["w_out_2"][0])
    for n in range(4):
        parts += [ssm[n:n + 1], ml[2 * n:2 * n + 2]]
    parts.append(wo)
    keys = a["peer_sub_keys_2"][0].reshape(16, P, P).transpose(2, 0, 1).reshape(P, 2, D)
    parts.append(keys.transpose(1, 0, 2))
    parts.append(_blocks(a["peer_w_q_2"][0]))
    u = a["peer_u_2"][0].reshape(P, P, KT, P).transpose(1, 3, 2, 0).reshape(P, P, D)
    v = a["peer_v_2"][0].reshape(P, P, D).transpose(1, 0, 2)
    parts += [u[:EARLY], np.stack([u[EARLY:], v[:-EARLY]], 1).reshape(-1, P, D), v[-EARLY:]]
    stream = np.concatenate(parts)

    cols = {}
    for n in ("mix_norm_g", "gate_b", "rw_mu", "rw_w0", "rw_a0", "rw_k_k", "rw_k_a", "rw_gn_g", "rw_gn_b",
              "ffn_norm_g", "norm1_g_2", "ssm_d_2", "ssm_b_glu_2", "ml_conv_b_2", "ml_norm_g_2", "ml_skip_2",
              "norm2_g_2"):
        cols[n] = _columns(a[n][0])
    cols["final_norm_g"] = _columns(a["final_norm_g"])
    cols["rw_r_k"] = _columns(a["rw_r_k"][0].reshape(-1))
    for n in ("sc_conv_w", "ffn_conv_w", "ml_conv_w_2"):
        cols[n] = np.concatenate([_columns(w) for w in a[n][0]], 1)
    cols["ssm_a_re_2"] = _columns(a["ssm_a_re_2"][0].reshape(-1))
    cols["ssm_a_im_2"] = _columns(a["ssm_a_im_2"][0].reshape(-1))
    cols["ssm_log_dt_2"] = _columns(np.repeat(a["ssm_log_dt_2"][0], 64))
    b_if = np.zeros((P, 2), f32)
    b_if[:4, 0], b_if[:4, 1] = a["ml_b_if_2"][0][:4], a["ml_b_if_2"][0][4:]
    cols["ml_b_if_2"] = b_if
    assert {k: v.shape[1] for k, v in cols.items()} == COLS
    cols = np.concatenate([cols[k] for k in COLS], 1)

    lora = np.concatenate([np.concatenate([a["rw_w2"][0], a["rw_a2"][0]], 0), a["rw_g2"][0]], 1)
    ln_rows = np.broadcast_to(np.concatenate([a["sg_ln_g"][0], a["sg_ln_b"][0]])[None], (P, 512))
    sgw = a["sg_w"][0].transpose(2, 0, 1).reshape(P, 512)
    sgb = np.tile(np.repeat(a["sg_b"][0], 64, axis=0).reshape(2, P, 1, P), (1, 1, 2, 1)).transpose(1, 0, 2, 3)
    i = np.arange(P)
    s_, t_ = i[:, None], i[None, :]
    t2 = np.arange(T)[None, :]
    same = (s_ // 64) == (t_ // 64)
    masks = [same, same & (s_ < t_), same & (s_ <= t_)]
    levels = []
    for w in (1, 2, 4, 8, 16, 32):
        m = (s_ // (2 * w) == t_ // (2 * w)) & (s_ // w % 2 == 1) & (t_ // w % 2 == 0)
        levels.append(m)
    masks += levels[:1] + [m.T for m in levels]
    masks += [s_ > t_, s_ <= t_, s_ < t2, s_ < t2[:, P:] - P, (t2 % 64 != 0) & (s_ >= 0)]
    eye2 = np.concatenate([np.eye(64), np.eye(64)], 0)
    first = [lora, ln_rows, sgw, sgb.reshape(P, 512)] + [m.astype(f32) for m in masks] + [eye2]
    first = np.concatenate([x.astype(f32, copy=False) for x in first], 1)
    assert first.shape[1] == sum(FIRST.values())

    bmats, cmats = [], []
    for n in ("ssm_b_re_2", "ssm_b_im_2"):
        b = a[n][0].reshape(4, 4, 2, 64, 16)
        m = np.zeros((4, 2, 16, 4, 2, 64), f32)
        for g in range(2):
            m[:, g, :, :, g, :] = b[:, :, g].transpose(1, 3, 0, 2)
        bmats.append(m.reshape(P, 512))
    for n in ("ssm_c_re_2", "ssm_c_im_2"):
        c = a[n][0].reshape(16, 2, 16, 64)
        m = np.zeros((2, 64, 16, 2, 16), f32)
        for g in range(2):
            m[g, :, :, g, :] = c[:, g].transpose(2, 0, 1)
        cmats.append(m.reshape(P, 512))
    wif = a["ml_w_if_2"][0].reshape(24, P, 8).transpose(1, 0, 2).reshape(P, 192)
    neg = [np.where(s_ <= t2, 0.0, -1e30), np.where(s_ + P <= t2, 0.0, -1e30)]
    sel = np.zeros((P, 4, P))
    sel[i[:4], i[:4]] = 1
    second = np.concatenate([x.astype(f32, copy=False) for x in bmats + cmats + [wif] + neg + [sel.reshape(P, 512)]], 1)
    assert second.shape[1] == sum(SECOND.values())
    last = np.broadcast_to(a["final_norm_g_2"][None], (P, D))
    keep = np.concatenate([np.eye(P), np.ones((P, P)), np.broadcast_to(i[None], (P, P))], 1).astype(f32)
    return {
        "stream": stream, "x_t": a["x"][0].T.reshape(KT, P, T).transpose(1, 0, 2),
        "meta_t": a["meta_tokens_2"].T.reshape(KT, P, M).transpose(1, 0, 2),
        "cols": cols, "first": first, "second": second, "last": last, "keep": keep,
    }


def kernel(**inputs):
    import numpy as np
    import concourse.bacc as bacc
    from concourse.bass_utils import run_bass_kernel_spmd

    arrays = {k: np.ascontiguousarray(v) for k, v in lay_out(inputs).items()}
    nc = bacc.Bacc("TRN2", target_bir_lowering=False, num_devices=1)
    args = {n: nc.dram_tensor(n, a.shape, mybir.dt.from_np(a.dtype), kind="ExternalInput").ap()
            for n, a in arrays.items()}
    out = nc.dram_tensor("out", (T, D), F32, kind="ExternalOutput").ap()
    build(nc, out, **args)
    r = run_bass_kernel_spmd(nc, [arrays], core_ids=[0])
    return r.results[0]["out"].reshape(1, T, D)
```
